# Optimizing a Trainium2 kernel written in Bass

```python
import jax, jax.numpy as jnp
from jax import lax
import numpy as np

D_MODEL = 1024
BATCH = 1
SEQ = 512
DEPTH = 1

N_MEM = 256
D_MIX = D_MODEL
POOL_WIDTH = D_MIX // 2
POOL_WINDOWS = (2, 4, 8, 16)
POOL_GROUPS = len(POOL_WINDOWS)
POOL_GROUP_DIM = POOL_WIDTH // POOL_GROUPS
SGU_WIDTH = D_MIX - POOL_WIDTH
SGU_HEADS = 4
SGU_HEAD_DIM = SGU_WIDTH // SGU_HEADS
CHUNK = 128
D_IN_PROJ = POOL_WIDTH + 2 * SGU_WIDTH
XATTN_HEADS = 4
XATTN_HEAD_DIM = D_MODEL // XATTN_HEADS
D_FF = 2816
CONV_WIDTH = 3
EPS = 1e-6


def rmsnorm(x, g):
    xf = x.astype(jnp.float32)
    y = xf * lax.rsqrt(jnp.mean(xf * xf, axis=-1, keepdims=True) + EPS)
    return (y * g.astype(jnp.float32)).astype(x.dtype)

def layernorm_nobias(x, g):
    xf = x.astype(jnp.float32)
    mu = jnp.mean(xf, axis=-1, keepdims=True)
    xc = xf - mu
    y = xc * lax.rsqrt(jnp.mean(xc * xc, axis=-1, keepdims=True) + EPS)
    return (y * g.astype(jnp.float32)).astype(x.dtype)

def pool_mixer(p, pool_w, pool_scale):
    B, S, _ = p.shape
    pf = p.astype(jnp.float32)
    c = jnp.pad(jnp.cumsum(pf, axis=1), ((0, 0), (1, 0), (0, 0)))
    t = jnp.arange(S)
    diffs = []
    for gi, win in enumerate(POOL_WINDOWS):
        sl = slice(gi * POOL_GROUP_DIM, (gi + 1) * POOL_GROUP_DIM)
        cg = c[..., sl]
        prev = jnp.pad(cg, ((0, 0), (win - 1, 0), (0, 0)))[:, :S]
        count = jnp.minimum(t + 1, win).astype(jnp.float32)[None, :, None]
        diffs.append((cg[:, 1:] - prev) / count - pf[..., sl])
    d = jnp.stack(diffs, axis=2).astype(p.dtype)
    y = jnp.einsum('bsgc,gcd->bsgd', d, pool_w).reshape(B, S, POOL_WIDTH)
    return y * pool_scale

def sgu_mixer(u, v, sgu_g, sgu_w, sgu_b):
    B, S, _ = u.shape
    vn = layernorm_nobias(v, sgu_g)
    vc = vn.reshape(B, S // CHUNK, CHUNK, SGU_HEADS, SGU_HEAD_DIM)
    mask = jnp.tril(jnp.ones((CHUNK, CHUNK), dtype=bool))
    w_masked = jnp.where(mask[None], sgu_w, jnp.zeros_like(sgu_w))
    z = jnp.einsum('hts,bnshd->bnthd', w_masked, vc) + sgu_b.T[:, :, None]
    return u * z.reshape(B, S, SGU_WIDTH)

def mem_cross_attention(xn, mem, mem_g, wq, wk, wv, wo):
    B, S, _ = xn.shape
    memn = rmsnorm(mem, mem_g)
    q = (xn @ wq).reshape(B, S, XATTN_HEADS, XATTN_HEAD_DIM)
    k = (memn @ wk).reshape(B, N_MEM, XATTN_HEADS, XATTN_HEAD_DIM)
    v = (memn @ wv).reshape(B, N_MEM, XATTN_HEADS, XATTN_HEAD_DIM)
    s = jnp.einsum('bshd,bmhd->bhsm', q, k).astype(jnp.float32) * (XATTN_HEAD_DIM ** -0.5)
    pr = jax.nn.softmax(s, axis=-1).astype(v.dtype)
    o = jnp.einsum('bhsm,bmhd->bshd', pr, v).reshape(B, S, D_MODEL)
    return o @ wo

def conv_ffn(xn, w_up, conv_w, conv_b, w_down):
    S = xn.shape[1]
    h = xn @ w_up
    hp = jnp.pad(h, ((0, 0), (CONV_WIDTH - 1, 0), (0, 0)))
    hc = conv_b + sum(conv_w[k] * hp[:, k:k + S] for k in range(CONV_WIDTH))
    gate, val = jnp.split(hc, 2, axis=-1)
    return (jax.nn.silu(gate) * val) @ w_down

def first_inputs(seed: int = 0) -> dict:
    key = jax.random.key(seed)
    ks = jax.random.split(key, 24)
    f32 = jnp.float32
    n = lambda k, shape, s: (jax.random.normal(k, shape, f32) * s)
    gain = lambda k, shape: 1.0 + 0.05 * jax.random.normal(k, shape, f32)
    L = DEPTH
    return {
        "x": jax.random.normal(ks[0], (BATCH, SEQ, D_MODEL), f32),
        "mem": jax.random.normal(ks[1], (BATCH, N_MEM, D_MODEL), f32),
        "norm_mix_g": gain(ks[2], (L, D_MODEL)),
        "w_in": n(ks[3], (L, D_MODEL, D_IN_PROJ), D_MODEL ** -0.5),
        "pool_w": n(ks[4], (L, POOL_GROUPS, POOL_GROUP_DIM, POOL_GROUP_DIM), POOL_GROUP_DIM ** -0.5),
        "pool_scale": 1.0 + 0.1 * jax.random.normal(ks[5], (L, POOL_WIDTH), f32),
        "sgu_g": gain(ks[6], (L, SGU_WIDTH)),
        "sgu_w": n(ks[7], (L, SGU_HEADS, CHUNK, CHUNK), CHUNK ** -0.5),
        "sgu_b": 1.0 + 0.05 * jax.random.normal(ks[8], (L, SGU_HEADS, CHUNK), f32),
        "w_out": n(ks[9], (L, D_MIX, D_MODEL), D_MIX ** -0.5),
        "norm_xattn_g": gain(ks[10], (L, D_MODEL)),
        "mem_norm_g": gain(ks[11], (L, D_MODEL)),
        "wq": n(ks[12], (L, D_MODEL, D_MODEL), D_MODEL ** -0.5),
        "wk": n(ks[13], (L, D_MODEL, D_MODEL), D_MODEL ** -0.5),
        "wv": n(ks[14], (L, D_MODEL, D_MODEL), D_MODEL ** -0.5),
        "wo": n(ks[15], (L, D_MODEL, D_MODEL), D_MODEL ** -0.5),
        "norm_ffn_g": gain(ks[16], (L, D_MODEL)),
        "w_up": n(ks[17], (L, D_MODEL, 2 * D_FF), D_MODEL ** -0.5),
        "conv_w": n(ks[18], (L, CONV_WIDTH, 2 * D_FF), CONV_WIDTH ** -0.5),
        "conv_b": n(ks[19], (L, 2 * D_FF), 0.02),
        "w_down": n(ks[20], (L, D_FF, D_MODEL), D_FF ** -0.5),
        "final_norm_g": gain(ks[21], (D_MODEL,)),
    }

def first_block(x, mem, norm_mix_g, w_in, pool_w, pool_scale, sgu_g, sgu_w, sgu_b, w_out,
              norm_xattn_g, mem_norm_g, wq, wk, wv, wo,
              norm_ffn_g, w_up, conv_w, conv_b, w_down, final_norm_g):
    h = x
    for l in range(DEPTH):
        xn = rmsnorm(h, norm_mix_g[l])
        proj = xn @ w_in[l]
        p = proj[..., :POOL_WIDTH]
        uv = jax.nn.gelu(proj[..., POOL_WIDTH:], approximate=False)
        u, v = uv[..., :SGU_WIDTH], uv[..., SGU_WIDTH:]
        y_pool = pool_mixer(p, pool_w[l], pool_scale[l])
        y_sgu = sgu_mixer(u, v, sgu_g[l], sgu_w[l], sgu_b[l])
        h = h + jnp.concatenate([y_pool, y_sgu], axis=-1) @ w_out[l]
        xn = rmsnorm(h, norm_xattn_g[l])
        h = h + mem_cross_attention(xn, mem, mem_norm_g[l], wq[l], wk[l], wv[l], wo[l])
        xn = rmsnorm(h, norm_ffn_g[l])
        h = h + conv_ffn(xn, w_up[l], conv_w[l], conv_b[l], w_down[l])
    return rmsnorm(h, final_norm_g)


ATTN_HEADS = 8
HEAD_DIM = 64
ATTN_WIDTH = ATTN_HEADS * HEAD_DIM
CONV_WIDTH_2 = D_MODEL - ATTN_WIDTH
CONV_KERNEL = 31
FFN_KERNEL = 3
BLOCK_Q = 128
IN_WIDTH = 3 * ATTN_WIDTH + 2 * CONV_WIDTH_2


def rms_norm(x, g):
    xf = x.astype(jnp.float32)
    y = xf * lax.rsqrt(jnp.mean(xf * xf, axis=-1, keepdims=True) + EPS)
    return (y * g.astype(jnp.float32)).astype(x.dtype)

def layer_norm(x, g, b):
    xf = x.astype(jnp.float32)
    mu = jnp.mean(xf, axis=-1, keepdims=True)
    xc = xf - mu
    var = jnp.mean(xc * xc, axis=-1, keepdims=True)
    y = xc * lax.rsqrt(var + EPS) * g.astype(jnp.float32) + b.astype(jnp.float32)
    return y.astype(x.dtype)

def causal_depthwise_conv(x, w, b):
    k_width, channels = w.shape
    y = lax.conv_general_dilated(
        x, w[:, None, :].astype(x.dtype),
        window_strides=(1,), padding=[(k_width - 1, 0)],
        dimension_numbers=("NWC", "WIO", "NWC"),
        feature_group_count=channels)
    return y + b.astype(x.dtype)

def stick_breaking_attention(q, k, v):
    seq = q.shape[1]
    scale = q.shape[-1] ** -0.5
    outs = []
    for start in range(0, seq, BLOCK_Q):
        end = min(start + BLOCK_Q, seq)
        qb = q[:, start:end].astype(jnp.float32)
        kb = k[:, :end].astype(jnp.float32)
        vb = v[:, :end].astype(jnp.float32)
        z = jnp.einsum("bqhd,bkhd->bhqk", qb, kb) * scale
        t_idx = start + jnp.arange(end - start)[:, None]
        s_idx = jnp.arange(end)[None, :]
        mask = s_idx < t_idx
        log_beta = jax.nn.log_sigmoid(z)
        log_one_minus = jnp.where(mask, jax.nn.log_sigmoid(-z), 0.0)
        tail = lax.cumsum(log_one_minus, axis=3, reverse=True) - log_one_minus
        weights = jnp.where(mask, jnp.exp(log_beta + tail), 0.0)
        outs.append(jnp.einsum("bhqk,bkhd->bqhd", weights, vb))
    return jnp.concatenate(outs, axis=1).astype(v.dtype)

def second_inputs(seed: int = 0) -> dict:
    key = jax.random.key(seed)
    ks = jax.random.split(key, 16)
    f32 = jnp.float32
    out_scale = (2.0 * DEPTH) ** -0.5

    def nrm(k, shape, s):
        return jax.random.normal(k, shape, f32) * s

    return {
        "x": jax.random.normal(ks[0], (BATCH, SEQ, D_MODEL), f32),
        "norm1_g": 1.0 + nrm(ks[1], (DEPTH, D_MODEL), 0.02),
        "w_in": nrm(ks[2], (DEPTH, D_MODEL, IN_WIDTH), D_MODEL ** -0.5),
        "q_norm_g": 1.0 + nrm(ks[3], (DEPTH, HEAD_DIM), 0.02),
        "k_norm_g": 1.0 + nrm(ks[4], (DEPTH, HEAD_DIM), 0.02),
        "conv_dw_w": nrm(ks[5], (DEPTH, CONV_KERNEL, CONV_WIDTH_2), CONV_KERNEL ** -0.5),
        "conv_dw_b": nrm(ks[6], (DEPTH, CONV_WIDTH_2), 0.01),
        "conv_ln_g": 1.0 + nrm(ks[7], (DEPTH, CONV_WIDTH_2), 0.02),
        "conv_ln_b": nrm(ks[8], (DEPTH, CONV_WIDTH_2), 0.01),
        "w_out": nrm(ks[9], (DEPTH, D_MODEL, D_MODEL), D_MODEL ** -0.5 * out_scale),
        "norm2_g": 1.0 + nrm(ks[10], (DEPTH, D_MODEL), 0.02),
        "w_up": nrm(ks[11], (DEPTH, D_MODEL, 2 * D_FF), D_MODEL ** -0.5),
        "ffn_dw_w": nrm(ks[12], (DEPTH, FFN_KERNEL, D_FF), FFN_KERNEL ** -0.5),
        "ffn_dw_b": nrm(ks[13], (DEPTH, D_FF), 0.01),
        "w_down": nrm(ks[14], (DEPTH, D_FF, D_MODEL), D_FF ** -0.5 * out_scale),
    }

def second_block(x, norm1_g, w_in, q_norm_g, k_norm_g, conv_dw_w, conv_dw_b,
              conv_ln_g, conv_ln_b, w_out, norm2_g, w_up, ffn_dw_w, ffn_dw_b,
              w_down):
    bsz, seq, _ = x.shape
    splits = [ATTN_WIDTH, 2 * ATTN_WIDTH, 3 * ATTN_WIDTH, 3 * ATTN_WIDTH + CONV_WIDTH_2]
    for layer in range(DEPTH):
        h = rms_norm(x, norm1_g[layer])
        proj = h @ w_in[layer]
        q, k, v, glu_a, glu_b = jnp.split(proj, splits, axis=-1)
        q = rms_norm(q.reshape(bsz, seq, ATTN_HEADS, HEAD_DIM), q_norm_g[layer])
        k = rms_norm(k.reshape(bsz, seq, ATTN_HEADS, HEAD_DIM), k_norm_g[layer])
        v = v.reshape(bsz, seq, ATTN_HEADS, HEAD_DIM)
        attn = stick_breaking_attention(q, k, v).reshape(bsz, seq, ATTN_WIDTH)

        c = glu_a * jax.nn.sigmoid(glu_b)
        c = causal_depthwise_conv(c, conv_dw_w[layer], conv_dw_b[layer])
        c = jax.nn.silu(layer_norm(c, conv_ln_g[layer], conv_ln_b[layer]))

        mixed = jnp.concatenate([attn, c], axis=-1) @ w_out[layer]
        x = x + mixed

        h = rms_norm(x, norm2_g[layer])
        gate, val = jnp.split(h @ w_up[layer], 2, axis=-1)
        gate = jax.nn.silu(causal_depthwise_conv(gate, ffn_dw_w[layer], ffn_dw_b[layer]))
        x = x + (gate * val) @ w_down[layer]
    return x


def setup_inputs(seed=0):
    out = dict(first_inputs(seed))
    for name, value in second_inputs(seed + 1).items():
        if name != "x":
            out[name + "_2"] = value
    return out


def reference(
    x, mem, norm_mix_g, w_in, pool_w, pool_scale, sgu_g, sgu_w, sgu_b, w_out, norm_xattn_g,
    mem_norm_g, wq, wk, wv, wo, norm_ffn_g, w_up, conv_w, conv_b, w_down, final_norm_g,
    norm1_g_2, w_in_2, q_norm_g_2, k_norm_g_2, conv_dw_w_2, conv_dw_b_2, conv_ln_g_2,
    conv_ln_b_2, w_out_2, norm2_g_2, w_up_2, ffn_dw_w_2, ffn_dw_b_2, w_down_2,
):
    x = first_block(
        x, mem, norm_mix_g, w_in, pool_w, pool_scale, sgu_g, sgu_w, sgu_b, w_out, norm_xattn_g,
        mem_norm_g, wq, wk, wv, wo, norm_ffn_g, w_up, conv_w, conv_b, w_down, final_norm_g,
    )
    return second_block(
        x, norm1_g_2, w_in_2, q_norm_g_2, k_norm_g_2, conv_dw_w_2, conv_dw_b_2, conv_ln_g_2,
        conv_ln_b_2, w_out_2, norm2_g_2, w_up_2, ffn_dw_w_2, ffn_dw_b_2, w_down_2,
    )


_drawn_inputs = setup_inputs


def setup_inputs(seed=0):
    import zlib

    import numpy as np

    out = dict(_drawn_inputs(seed))
    spreads = {}
    factors = {'sgu_g': 3.735,
     'sgu_b': 2.856,
     'norm_xattn_g': 8.0,
     'mem_norm_g': 7.955,
     'conv_b': 4.377,
     'norm1_g_2': 5.606,
     'q_norm_g_2': 8.0,
     'k_norm_g_2': 8.0,
     'conv_dw_b_2': 8.0,
     'conv_ln_g_2': 24.484,
     'conv_ln_b_2': 47.431,
     'norm2_g_2': 5.4,
     'ffn_dw_b_2': 31.167,
     'norm_ffn_g': 3.893}
    for name, (base, spread) in spreads.items():
        noise = np.random.default_rng([zlib.crc32(name.encode()), seed]).standard_normal(out[name].shape)
        drawn = base * np.exp(spread * noise) if base else spread * noise
        out[name] = __import__('jax').numpy.asarray(drawn.astype(out[name].dtype))
    for name, factor in factors.items():
        out[name] = (out[name] * factor).astype(out[name].dtype)
    return out
```

```python
from contextlib import ExitStack

import concourse.bass as bass
import numpy as np
from concourse import mybir

F32 = mybir.dt.float32
F32R = mybir.dt.float32r
ACT = mybir.ActivationFunctionType
ALU = mybir.AluOpType
AX = mybir.AxisListType

P = 128
D = 1024
DT = D // P
SEQ = 512
ST = SEQ // P
MEM = 256
MT = MEM // P
FF = 2816
FT = FF // P
EPS = 1e-6
POOL_WINDOWS = (2, 4, 8, 16)
PAD = 16
XH = 4
HEADS = 8
HD = 64
TAPS = 31
FFN_CHUNKS = (8, 8, 6)
BLK = 8 * P
RING = 4
AUX = 4
Z_MAX = 40.0

MEMK = 0
MEMV = MEMK + 8
INV = MEMV + 8
INP = INV + 4
INU = INP + 4
WOUT = INU + 4
WQ = WOUT + 8
WO = WQ + 8
FFN1 = WO + 8
FFN_BLOCKS = 2 * FT + DT * len(FFN_CHUNKS)
GLU = FFN1 + FFN_BLOCKS
V2 = GLU + 8
QK = V2 + 4
WOUT2 = QK + 8
FFN2 = WOUT2 + 8
BLOCKS = FFN2 + FFN_BLOCKS
USE_LAG = 4

COLS = {}
_n = 0
for _name, _k in (("norm_mix_g", DT), ("norm_xattn_g", DT), ("mem_norm_g", DT), ("norm_ffn_g", DT),
                  ("final_norm_g", DT), ("norm1_g_2", DT), ("norm2_g_2", DT), ("pool_scale", 4),
                  ("conv_w", 6 * FT), ("conv_b", 2 * FT), ("ffn_dw_w_2", 3 * FT), ("ffn_dw_b_2", FT),
                  ("conv_dw_w_2", TAPS * 4), ("conv_dw_b_2", 4), ("conv_ln_g_2", 4), ("conv_ln_b_2", 4),
                  ("q_norm_g_2", 1), ("k_norm_g_2", 1)):
    COLS[_name] = _n
    _n += _k
N_COLS = _n

NORM_MEM, NORM_MIX, NORM_XATTN, NORM_FFN, NORM_FINAL, NORM_ONE, NORM_TWO = range(7)
TILE0 = {NORM_MEM: 0, NORM_MIX: 8, NORM_XATTN: 16, NORM_FFN: 24, NORM_ONE: 32, NORM_TWO: 40}
SQ0 = {NORM_MEM: 0, NORM_MIX: 8, NORM_XATTN: 16, NORM_FFN: 24, NORM_FINAL: 32, NORM_TWO: 48}


class Count:

    def __init__(self):
        self.base, self.k = 0, 0

    def tick(self):
        self.k += 1
        return self.now()

    def now(self):
        return self.base + self.k

    def enter(self, i, per):
        self.start, self.per = self.base + self.k, per
        self.base, self.k = self.start + i * per, 0

    def leave(self, times):
        assert self.k == self.per, (self.k, self.per)
        self.base, self.k = self.start + times * self.per, 0


def ffn_plan(first):
    out, b, p = [], first, 0
    for n in FFN_CHUNKS:
        out.append((b, n, p, b + 2 * n))
        b += 2 * n + DT
        p += n
    return out


def build(nc, a_mem, a_x, a_cols, a_mats, a_corr, a_w, a_out):
    ctx = ExitStack()
    with ctx:
        def sb(name, shape, dt=F32):
            return ctx.enter_context(nc.sbuf_tensor(name, shape, dt))

        def sem(name):
            return ctx.enter_context(nc.semaphore(name))

        w_raw = sb("w_raw", [P, RING, BLK])
        w_hi = sb("w_hi", [P, RING, BLK], F32R)
        w_lo = sb("w_lo", [P, RING, BLK], F32R)
        h = sb("h", [P, DT, SEQ])
        xg_hi = sb("xg_hi", [P, DT, SEQ], F32R)
        xg_lo = sb("xg_lo", [P, DT, SEQ], F32R)
        y_hi = sb("y_hi", [P, DT, SEQ], F32R)
        y_lo = sb("y_lo", [P, DT, SEQ], F32R)
        slab = sb("slab", [P, 28 * SEQ])
        memg_hi = y_hi[:, 0:4, :].rearrange("p a (b t) -> p (a b) t", b=2)
        memg_lo = y_lo[:, 0:4, :].rearrange("p a (b t) -> p (a b) t", b=2)

        def units(first, n):
            return slab[:, first * SEQ:(first + n) * SEQ]

        k1 = units(0, 4).rearrange("p (m t) -> p m t", t=MEM)
        v1 = units(4, 4).rearrange("p (m d) -> p m d", d=D)
        mem = units(8, 4).rearrange("p (m t) -> p m t", t=MEM)
        u = units(8, 4).rearrange("p (m t) -> p m t", t=SEQ)
        vtok = units(12, 4).rearrange("p (m d) -> p m d", d=SEQ)
        WP = PAD + SEQ
        pp = slab[:, 16 * SEQ:16 * SEQ + 4 * WP].rearrange("p (m t) -> p m t", t=WP)
        win = slab[:, 16 * SEQ + 4 * WP:16 * SEQ + 6 * WP].rearrange("p (m t) -> p m t", t=WP)
        mats = units(24, 4)
        pool_w = mats[:, 0:512].rearrange("p (g d) -> p g d", g=4)
        sgu_w = mats[:, 512:1024].rearrange("p (g d) -> p g d", g=4)
        sgu_g = mats[:, 1024:1536]
        sgu_b = mats[:, 1536:2048].rearrange("p (g t) -> p g t", g=4)
        q1 = units(8, 8).rearrange("p (m t) -> p m t", t=SEQ)
        probs = units(16, 4).rearrange("p (b a m) -> p b a m", b=2, m=MEM)
        probs_t = units(20, 2).rearrange("p (m t) -> p m t", t=SEQ)
        acc = units(0, 4).rearrange("p (m t) -> p m t", t=SEQ)
        prod = units(4, 2).rearrange("p (m t) -> p m t", t=SEQ)
        q2 = units(0, 4).rearrange("p (m t) -> p m t", t=SEQ)
        k2 = units(4, 4).rearrange("p (m t) -> p m t", t=SEQ)
        v2 = units(8, 4).rearrange("p (m d) -> p m d", d=SEQ)
        conv_in = units(12, 4).rearrange("p (m t) -> p m t", t=SEQ)
        conv = units(16, 4).rearrange("p (m t) -> p m t", t=SEQ)
        STICK = SEQ * ST - P * (ST * (ST - 1) // 2)
        stick = slab[:, 20 * SEQ:20 * SEQ + 3 * STICK].rearrange("p (b t) -> p b t", t=STICK)

        cols = sb("cols", [P, N_COLS])
        corr = sb("corr", [P, 4, PAD])
        gain_12 = sb("gain_12", [P, DT])
        ident = sb("ident", [P, P])
        ones = sb("ones", [P, 1])
        half = sb("half", [P, 2])
        minus_half = sb("minus_half", [P, 8])
        mask_incl = sb("mask_incl", [P, P])
        mask_strict = sb("mask_strict", [P, P])
        mask_min = sb("mask_min", [P, P])
        neg_tri = sb("neg_tri", [P, P])
        neg_ones = sb("neg_ones", [P, P])
        sq = sb("sq", [P, 2, SEQ])
        ssq = sb("ssq", [P, 2, SEQ])
        later_sums = sb("later_sums", [P, 2, 3 * P])
        rstd_bc = sb("rstd_bc", [P, SEQ])
        var = sb("var", [P, 8])
        rcol = sb("rcol", [P, 8, ST])
        wide = sb("wide", [P, ST, P])
        bn = sb("bn", [P, ST, 6])
        bna = sb("bna", [P, ST, 2])
        tiny = sb("tiny", [P, 4, 8])
        top = sb("top", [P, XH, ST])
        rsum = sb("rsum", [P, XH, ST])
        ps = ctx.enter_context(nc.psum_tensor("ps", [P, 8, SEQ], F32))

        def col(name, k):
            return cols[:, bass.ds(COLS[name] + k, 1)]

        loaded_mem, loaded_x0, loaded_x1 = sem("loaded_mem"), sem("loaded_x0"), sem("loaded_x1")
        loaded_cols, loaded_mats = sem("loaded_cols"), sem("loaded_mats")
        w_loaded = [sem(f"w_loaded{s}") for s in range(RING)]
        w_hi_ready, w_lo_ready = sem("w_hi_ready"), sem("w_lo_ready")
        blocks_done, banks_freed = sem("blocks_done"), sem("banks_freed")
        consts0, consts, gain_ready = sem("consts0"), sem("consts"), sem("gain_ready")
        vstep, astep = sem("vstep"), sem("astep")
        tile_hi, tile_lo = sem("tile_hi"), sem("tile_lo")
        sq_ready, sq_added = sem("sq_ready"), sem("sq_added")
        sums_ready, var_ready, rcol_ready = sem("sums_ready"), sem("var_ready"), sem("rcol_ready")
        wide_ready, spread_ready = sem("wide_ready"), sem("spread_ready")
        y_hi_ready, y_lo_ready = sem("y_hi_ready"), sem("y_lo_ready")
        v_scaled, v_gelu, v_var, v_rstd, vn_ready = (sem(n) for n in ("v_scaled", "v_gelu", "v_var", "v_rstd", "vn_ready"))
        u_gelu, pooled, pool_done, z_done, sgu_masked = (sem(n) for n in ("u_gelu", "pooled", "pool_done", "z_done", "sgu_masked"))
        sgu_prod = sem("sgu_prod")
        x_scores, x_top, x_exp, x_probs, x_turned, x_copied, x_out = (
            sem(n) for n in ("x_scores", "x_top", "x_exp", "x_probs", "x_turned", "x_copied", "x_out"))
        f_scaled, f_base, f_silu, f_prod = (sem(n) for n in ("f_scaled", "f_base", "f_silu", "f_prod"))
        glu_sig, glu_done, conv_init = sem("glu_sig"), sem("glu_done"), sem("conv_init")
        qk_sums, qk_var, qk_rstd, qk_wide, qk_spread, qk_ready = (
            sem(n) for n in ("qk_sums", "qk_var", "qk_rstd", "qk_wide", "qk_spread", "qk_ready"))
        s_z, s_min, s_exp, s_log, s_sp, s_cum, s_cut, s_att, s_out = (
            sem(n) for n in ("s_z", "s_min", "s_exp", "s_log", "s_sp", "s_cum", "s_cut", "s_att", "s_out"))
        ln_sum, ln_sums, ln_col, ln_wide, ln_spread, ln_xc, ln_sq, ln_var, ln_rstd, ln_norm, ln_silu = (
            sem(n) for n in ("ln_sum", "ln_sums", "ln_col", "ln_wide", "ln_spread", "ln_xc", "ln_sq", "ln_var",
                             "ln_rstd", "ln_norm", "ln_silu"))
        qk_square, ln_square = sem("qk_square"), sem("ln_square")
        stored = sem("stored")

        Y_MIX, Y_X, Y_F1, Y_MIX2, Y_F2 = 0, 8, 16, 16 + FT, 24 + FT

        block = ctx.enter_context(nc.Block())

        @block.sync
        def _(sp):
            sp.dma_start(mem, a_mem).then_inc(loaded_mem, 16)
            for b in range(RING):
                sp.dma_start(w_raw[:, b, :], a_w[b]).then_inc(w_loaded[b], 16)
            region = [(RING, FFN1 + FFN_BLOCKS - DT, BLK), (FFN1 + FFN_BLOCKS - DT, GLU, FFN_CHUNKS[-1] * P),
                      (GLU, BLOCKS - DT, BLK), (BLOCKS - DT, BLOCKS, FFN_CHUNKS[-1] * P)]
            for first, end, width in region:
                with sp.Fori(0, (end - first) // RING) as i:
                    for s in range(RING):
                        sp.wait_ge(w_lo_ready, i * RING + (first + s + 1 - RING))
                        sp.dma_start(w_raw[:, s, 0:width], a_w[i * RING + (first + s)][:, 0:width]).then_inc(w_loaded[s], 16)
            last_down = ffn_plan(FFN2)[-1][3]
            for m in range(DT):
                sp.wait_ge(banks_freed, last_down + m + 1 - USE_LAG)
                sp.dma_start(a_out[:, m, :], h[:, m, :]).then_inc(stored, 16)
            sp.wait_ge(stored, 16 * DT)

        @block.gpsimd
        def _(pool):
            def weights_lo(b, s):
                pool.wait_ge(w_hi_ready, b + 1)
                nc.gpsimd.tensor_tensor(w_lo[:, s, :], w_raw[:, s, :], w_hi[:, s, :].bitcast(F32),
                                        ALU.subtract).then_inc(w_lo_ready, 1)

            def weights_lo_for(first, n):
                n = min(n, BLOCKS - RING - first)
                if n > 0:
                    with pool.Fori(0, n // RING) as i:
                        for s in range(RING):
                            pool.wait_ge(blocks_done, i * RING + (first + s + 1))
                            weights_lo(i * RING + (first + s + RING), s)

            def rstd(n, sizes=ST):
                pool.wait_ge(var_ready, n + 1)
                nc.gpsimd.tensor_tensor(rcol[:, n, 0:sizes], var[:, 0:sizes], minus_half[:, 0:sizes],
                                        ALU.pow).then_inc(rcol_ready, 1)

            for t, value in ((ident, 0.0), (ones, 1.0), (half, 1.0), (minus_half, -0.5), (mask_incl, 1.0),
                             (mask_strict, 1.0), (mask_min, 0.0), (neg_tri, -1.0), (neg_ones, -1.0)):
                nc.gpsimd.memset(t[:], value).then_inc(consts0, 1)
            pool.wait_ge(consts0, 9)

            def select(t, op, fill, base, step, per_partition):
                nc.gpsimd.affine_select(out=t, in_=t, compare_op=op, fill=fill, base=base, pattern=[[step, t.shape[1]]],
                                        channel_multiplier=per_partition).then_inc(consts, 1)

            select(ident[:], ALU.not_equal, 1.0, 0, -1, 1)
            select(half[:, 0:1], ALU.is_ge, 0.0, HD - 1, 0, -1)
            select(half[:, 1:2], ALU.is_ge, 0.0, -HD, 0, 1)
            select(mask_incl[:], ALU.is_ge, 0.0, 0, 1, -1)
            select(mask_strict[:], ALU.is_ge, 0.0, -1, 1, -1)
            select(mask_min[:], ALU.is_ge, -1000.0, -1, 1, -1)
            select(neg_tri[:], ALU.is_ge, 0.0, 0, -1, 1)

            for b in range(RING):
                weights_lo(b, b)
            rstd(NORM_MEM, MT)
            weights_lo_for(MEMK, INV - MEMK)
            rstd(NORM_MIX)
            weights_lo_for(INV, INP - INV)
            pool.wait_ge(v_var, ST)
            nc.gpsimd.tensor_tensor(tiny[:, 0, 0:ST], tiny[:, 1, 0:ST], minus_half[:, 0:ST], ALU.pow).then_inc(v_rstd, 1)
            weights_lo_for(INP, WQ - INP)
            rstd(NORM_XATTN)
            weights_lo_for(WQ, FFN1 - WQ)
            rstd(NORM_FFN)
            weights_lo_for(FFN1, FFN_BLOCKS)
            rstd(NORM_FINAL)
            rstd(NORM_ONE)
            weights_lo_for(GLU, QK - GLU)
            for t in range(8):
                pool.wait_ge(blocks_done, QK + t + 1)
                weights_lo(QK + t + RING, t % RING)
                pool.wait_ge(qk_var, t + 1)
                nc.gpsimd.tensor_tensor(tiny[:, 2 + t % 2, :], tiny[:, t % 2, :], minus_half[:], ALU.pow).then_inc(qk_rstd, 1)
            pool.wait_ge(ln_var, 1)
            nc.gpsimd.tensor_tensor(rcol[:, 7, :], var[:, 4:8], minus_half[:, 0:ST], ALU.pow).then_inc(ln_rstd, 1)
            weights_lo_for(WOUT2, FFN2 - WOUT2)
            rstd(NORM_TWO)
            weights_lo_for(FFN2, FFN_BLOCKS)

        @block.scalar
        def _(act):
            own = Count()
            act.dma_start(cols[:], a_cols).then_inc(loaded_cols, 16)
            act.dma_start(h[:, 0:4, :], a_x[:, 0:4, :]).then_inc(loaded_x0, 16)
            act.dma_start(h[:, 4:8, :], a_x[:, 4:8, :]).then_inc(loaded_x1, 16)
            act.dma_start(mats, a_mats).then_inc(loaded_mats, 16)
            act.dma_start(corr[:], a_corr).then_inc(loaded_mats, 16)

            def weights_hi(b, s, use):
                if b >= RING:
                    act.wait_ge(blocks_done, b + 1 - RING)
                act.wait_ge(w_loaded[s], 16 * (use + 1))
                nc.scalar.activation(w_hi[:, s, :], w_raw[:, s, :], ACT.Copy).then_inc(w_hi_ready, 1)

            def weights_hi_for(b):
                b += RING
                if b < BLOCKS:
                    weights_hi(b, b % RING, b // RING)

            def weights_hi_loop(i, first, s):
                act.wait_ge(blocks_done, i * RING + (first + s + 1))
                act.wait_ge(w_loaded[s], i * 16 + 16 * (first // RING + 2))
                nc.scalar.activation(w_hi[:, s, :], w_raw[:, s, :], ACT.Copy).then_inc(w_hi_ready, 1)

            def weights_hi_run(first, n):
                n = min(n, BLOCKS - RING - first)
                if n > 0:
                    with act.Fori(0, n // RING) as i:
                        for s in range(RING):
                            weights_hi_loop(i, first, s)

            def square(src, gain, n):
                if n >= 2:
                    act.wait_ge(sq_added, n - 1)
                nc.scalar.activation(sq[:, n % 2, 0:src.shape[1]], src, ACT.Square, scale=gain).then_inc(sq_ready, 1)

            def split_gain(dst, src, gain):
                nc.scalar.activation(dst, src, ACT.Copy, scale=gain).then_inc(tile_hi, 1)

            def residual(first, norm, gain):
                for m in range(DT):
                    act.wait_ge(banks_freed, first + m + 1 - USE_LAG)
                    split_gain(xg_hi[:, m, :], h[:, m, :], gain(m))
                    if norm == NORM_FINAL:
                        square(h[:, m, :], 1.0, SQ0[norm] + 2 * m)
                        square(h[:, m, :], col("final_norm_g", m), SQ0[norm] + 2 * m + 1)
                    else:
                        square(h[:, m, :], 1.0, SQ0[norm] + m)
                    weights_hi_for(first + m)

            def ffn(first, both):
                nc.scalar.preload_act_table_set("silu_and_others")
                w, b, n_w = ("conv_w", "conv_b", 2 * FT) if both else ("ffn_dw_w_2", "ffn_dw_b_2", FT)
                f0, y0, s0 = (0, Y_F1, 0) if both else (FT, Y_F2, 2 * FT)
                p0 = 0 if both else 2 * FT
                for first_b, n, pair0, down in ffn_plan(first):
                    with act.Fori(0, n // 2) as i:
                        for j in range(2):
                            s, pair = 2 * j, i * 2 + (pair0 + j)
                            for v in range(2 if both else 1):
                                act.wait_ge(f_scaled, pair * 2 + (s0 + v + 1))
                                nc.scalar.activation(acc[:, s + v, :], ps[:, s + v, :], ACT.Identity,
                                                     scale=col(w, pair + (2 * n_w + v * FT)),
                                                     bias=col(b, pair + v * FT)).then_inc(f_base, 1)
                            weights_hi_loop(i, first_b, s)
                            act.wait_ge(banks_freed, i * RING + (first_b + s + 1 - USE_LAG))
                            nc.scalar.activation(acc[:, s, :], acc[:, s, :], ACT.Silu).then_inc(f_silu, 1)
                            act.wait_ge(f_prod, pair + (f0 + 1))
                            nc.scalar.activation(y_hi[:, bass.ds(i * 2 + j, 1), :].rearrange("p a t -> p (a t)"),
                                                 prod[:, j, :], ACT.Copy).then_inc(y_hi_ready, 1)
                            weights_hi_loop(i, first_b, s + 1)
                    if down != ffn_plan(first)[-1][3] or not both:
                        weights_hi_run(down, DT)

            weights_hi(0, 0, 0)
            act.wait_ge(loaded_cols, 16)
            act.wait_ge(loaded_mem, 16)
            for m in range(DT):
                split_gain(memg_hi[:, m, :], mem[:, m, :], col("mem_norm_g", m))
                square(mem[:, m, :], 1.0, SQ0[NORM_MEM] + m)
            for b in range(1, RING):
                weights_hi(b, b, 0)
            for m in range(DT):
                if m in (0, 4):
                    act.wait_ge((loaded_x0, loaded_x1)[m // 4], 16)
                split_gain(xg_hi[:, m, :], h[:, m, :], col("norm_mix_g", m))
                square(h[:, m, :], 1.0, SQ0[NORM_MIX] + m)
                weights_hi_for(MEMK + m)
            weights_hi_run(MEMV, INP - MEMV)

            nc.scalar.preload_act_table_set("gelu_and_others")
            for t in range(ST):
                act.wait_ge(v_scaled, t + 1)
                nc.scalar.activation(vtok[:, t, :], vtok[:, t, :], ACT.Gelu).then_inc(v_gelu, 1)
            for b in range(INP, INU):
                weights_hi_for(b)
            for t in range(4):
                act.wait_ge(banks_freed, INU + t + 1 - USE_LAG)
                nc.scalar.activation(u[:, t, :], u[:, t, :], ACT.Gelu).then_inc(u_gelu, 1)
                weights_hi_for(INU + t)
                if t == 0:
                    for g in range(4):
                        act.wait_ge(pool_done, g + 1)
                        nc.scalar.activation(y_hi[:, g, :], ps[:, AUX + g, :], ACT.Copy,
                                             scale=col("pool_scale", g)).then_inc(y_hi_ready, 1)
            for g in range(4):
                act.wait_ge(sgu_prod, 2 * g + 2)
                nc.scalar.activation(y_hi[:, 4 + g, :], u[:, g, :], ACT.Copy).then_inc(y_hi_ready, 1)
            residual(WOUT, NORM_XATTN, lambda m: col("norm_xattn_g", m))

            def x_softmax(hd):
                act.wait_ge(x_top, hd + 1)
                for t in range(ST):
                    nc.scalar.activation(probs[:, hd % 2, t, :], ps[:, AUX + t // 2, (t % 2) * MEM:(t % 2 + 1) * MEM],
                                         ACT.Exp, bias=top[:, hd, t:t + 1], scale=MEM ** -0.5,
                                         accum_out=rsum[:, hd, t:t + 1]).then_inc(x_exp, 1)

            def x_result(hd):
                for d in range(2):
                    act.wait_ge(x_out, 2 * hd + d + 1)
                    nc.scalar.activation(y_hi[:, 2 * hd + d, :], ps[:, AUX + 2 + d, :], ACT.Copy).then_inc(y_hi_ready, 1)

            nc.scalar.preload_act_table_set("natural_log_exp_and_others")
            for b in range(4):
                weights_hi_for(WQ + b)
            x_softmax(0)
            weights_hi_for(WQ + 4)
            weights_hi_for(WQ + 5)
            x_result(0)
            x_softmax(1)
            weights_hi_for(WQ + 6)
            weights_hi_for(WQ + 7)
            x_result(1)
            x_softmax(2)
            x_result(2)
            x_softmax(3)
            x_result(3)
            residual(WO, NORM_FFN, lambda m: col("norm_ffn_g", m))
            ffn(FFN1, True)
            act.wait_ge(gain_ready, 1)
            residual(ffn_plan(FFN1)[-1][3], NORM_FINAL, lambda m: gain_12[:, m:m + 1])

            nc.scalar.preload_act_table_set("sigmoid_and_others")
            for i in range(4):
                act.wait_ge(banks_freed, GLU + 2 * i + 2 - USE_LAG)
                nc.scalar.activation(k2[:, i, :], k2[:, i, :], ACT.Sigmoid).then_inc(glu_sig, 1)
                weights_hi_for(GLU + 2 * i)
                weights_hi_for(GLU + 2 * i + 1)
                act.wait_ge(glu_done, i + 1)
                nc.scalar.activation(conv[:, i, :], conv_in[:, i, :], ACT.Identity,
                                     scale=col("conv_dw_w_2", (TAPS - 1) * 4 + i),
                                     bias=col("conv_dw_b_2", i)).then_inc(conv_init, 1)
            for b in range(V2, QK):
                weights_hi_for(b)
            nc.scalar.preload_act_table_set("natural_log_exp_and_others")
            for t in range(8):
                act.wait_ge(banks_freed, QK + t + 1 - USE_LAG)
                if t >= 2:
                    act.wait_ge(qk_sums, t - 1)
                nc.scalar.activation(sq[:, t % 2, :], (q2, k2)[t % 2][:, t // 2, :], ACT.Square).then_inc(qk_square, 1)
                weights_hi_for(QK + t)

            def s_logs(hd):
                t = stick[:, hd % 3, :]
                act.wait_ge(s_min, hd + 1)
                nc.scalar.activation(t, t, ACT.Exp).then_inc(s_exp, 1)
                act.wait_ge(s_exp, hd + 1)
                nc.scalar.activation(t, t, ACT.Ln, bias=1.0).then_inc(s_log, 1)

            s_logs(0)
            for hd in range(HEADS):
                if hd + 1 < HEADS:
                    s_logs(hd + 1)
                act.wait_ge(s_cut, hd + 1)
                for j, (at, n) in enumerate(((0, 512), (512, 512), (1024, 256))):
                    nc.scalar.activation(stick[:, hd % 3, at:at + n], ps[:, 3 * (hd % 2) + j, 0:n], ACT.Exp).then_inc(s_att, 1)
                if hd % 2 == 0 and hd >= 2:
                    act.wait_ge(s_out, hd)
                    nc.scalar.activation(y_hi[:, hd // 2 - 1, :], ps[:, 6, :], ACT.Copy).then_inc(y_hi_ready, 1)
                if hd == 6:
                    for i in range(4):
                        act.wait_ge(ln_xc, i + 1)
                        if i >= 2:
                            act.wait_ge(ln_sq, i - 1)
                        nc.scalar.activation(sq[:, i % 2, :], conv[:, i, :], ACT.Square).then_inc(ln_square, 1)
            act.wait_ge(s_out, HEADS)
            nc.scalar.activation(y_hi[:, 3, :], ps[:, 6, :], ACT.Copy).then_inc(y_hi_ready, 1)
            nc.scalar.preload_act_table_set("silu_and_others")
            for i in range(4):
                act.wait_ge(ln_norm, i + 1)
                nc.scalar.activation(conv[:, i, :], conv[:, i, :], ACT.Silu, scale=col("conv_ln_g_2", i),
                                     bias=col("conv_ln_b_2", i)).then_inc(ln_silu, 1)
                act.wait_ge(ln_silu, i + 1)
                nc.scalar.activation(y_hi[:, 4 + i, :], conv[:, i, :], ACT.Copy).then_inc(y_hi_ready, 1)
            residual(WOUT2, NORM_TWO, lambda m: col("norm2_g_2", m))
            ffn(FFN2, False)

        @block.vector
        def _(dve):
            own = Count()

            def multiply_by_rstd(out, b, bank, width=SEQ):
                dve.wait_ge(blocks_done, b + 1)
                return nc.vector.tensor_tensor(out, ps[:, bank, 0:width], rstd_bc[:, 0:width], ALU.mult)

            def add_squares(n, which, first, width=SEQ):
                dve.wait_ge(sq_ready, n + 1)
                dst = ssq[:, which, 0:width]
                if first:
                    nc.vector.tensor_copy(dst, sq[:, n % 2, 0:width]).then_inc(sq_added, 1)
                else:
                    dve.wait_ge(sq_added, n)
                    nc.vector.tensor_tensor(dst, dst, sq[:, n % 2, 0:width], ALU.add).then_inc(sq_added, 1)

            def split_gain_lo(n, dst, src, gain, hi):
                dve.wait_ge(tile_hi, n + 1)
                nc.vector.scalar_tensor_tensor(out=dst, in0=src, scalar=gain, in1=hi.bitcast(F32), op0=ALU.mult,
                                               op1=ALU.subtract).then_inc(tile_lo, 1)

            def split_lo(dst, src, hi, n):
                dve.wait_ge(y_hi_ready, n + 1)
                nc.vector.tensor_tensor(dst, src, hi.bitcast(F32), ALU.subtract).then_inc(y_lo_ready, 1)

            def variance(n, count, sizes=ST, sums=None):
                dve.wait_ge(sums_ready, n + 1 if n <= NORM_FINAL else n)
                nc.vector.tensor_scalar(var[:, 0:sizes], ps[:, AUX, 0:sizes], 1.0 / count, EPS, ALU.mult,
                                        ALU.add).then_inc(var_ready, 1)

            def spread(n, wides, sizes=ST, dst=None):
                dve.wait_ge(rcol_ready, n + 1)
                nc.vector.tensor_copy(wide[:, 0:sizes, :], rcol[:, n, 0:sizes].rearrange("p (a b) -> p a b", b=1)
                                      .broadcast_to([P, sizes, P])).then_inc(wide_ready, 1)
                dve.wait_ge(spread_ready, wides)
                nc.vector.tensor_copy(rstd_bc[:, 0:sizes * P], ps[:, AUX + 1, 0:sizes * P]).then_inc(vstep, 1)
                own.tick()
                dve.wait_ge(vstep, own.now())

            def residual(first, norm, gain):
                for m in range(DT):
                    dve.wait_ge(blocks_done, first + m + 1)
                    nc.vector.tensor_tensor(h[:, m, :], ps[:, m % RING, :], h[:, m, :], ALU.add).then_inc(banks_freed, 1)
                    n = TILE0[NORM_ONE if norm == NORM_FINAL else norm] + m
                    split_gain_lo(n, xg_lo[:, m, :], h[:, m, :], gain(m), xg_hi[:, m, :])
                    if norm == NORM_FINAL:
                        add_squares(SQ0[norm] + 2 * m, 0, m == 0)
                        add_squares(SQ0[norm] + 2 * m + 1, 1, m == 0)
                    else:
                        add_squares(SQ0[norm] + m, 0, m == 0)

            def ffn(first, both):
                w, n_w = ("conv_w", 2 * FT) if both else ("ffn_dw_w_2", FT)
                f0, y0, s0, c0 = (0, Y_F1, 0, 0) if both else (FT, Y_F2, 2 * FT, 2 * FT)
                for first_b, n, pair0, down in ffn_plan(first):
                    with dve.Fori(0, n // 2) as i:
                        own.enter(i, 4 if both else 2)
                        for j in range(2):
                            s, pair = 2 * j, i * 2 + (pair0 + j)
                            b = i * RING + (first_b + s)
                            for v in range(2):
                                multiply_by_rstd(ps[:, s + v, :], b + v, s + v).then_inc(f_scaled, 1)
                            convolved = range(2 if both else 1)
                            for v in convolved:
                                dve.wait_ge(f_base, (pair * 2 if both else pair) + (c0 + v + 1))
                                nc.vector.scalar_tensor_tensor(out=acc[:, s + v, 1:], in0=ps[:, s + v, 0:SEQ - 1],
                                                               scalar=col(w, pair + (n_w + v * FT)),
                                                               in1=acc[:, s + v, 1:], op0=ALU.mult, op1=ALU.add).then_inc(vstep, 1)
                                own.tick()
                            for v in convolved:
                                dve.wait_ge(vstep, own.now() - (convolved[-1] - v))
                                nc.vector.scalar_tensor_tensor(out=acc[:, s + v, 2:], in0=ps[:, s + v, 0:SEQ - 2],
                                                               scalar=col(w, pair + v * FT),
                                                               in1=acc[:, s + v, 2:], op0=ALU.mult, op1=ALU.add).then_inc(banks_freed, 1)
                            dve.wait_ge(f_silu, pair + (f0 + 1))
                            if both:
                                dve.wait_ge(banks_freed, b + (2 - USE_LAG))
                                nc.vector.tensor_tensor(prod[:, j, :], acc[:, s, :], acc[:, s + 1, :], ALU.mult).then_inc(f_prod, 1)
                            else:
                                dve.wait_ge(f_scaled, pair * 2 + (s0 + 2))
                                nc.vector.tensor_tensor(prod[:, j, :], ps[:, s + 1, :], acc[:, s, :], ALU.mult).then_inc(f_prod, 1)
                                dve.wait_ge(f_prod, pair + (f0 + 1))
                                nc.vector.memset(tiny[:, 3, 0:1], 0.0).then_inc(banks_freed, 1)
                            y = y_lo[:, bass.ds(i * 2 + j, 1), :].rearrange("p a t -> p (a t)")
                            yh = y_hi[:, bass.ds(i * 2 + j, 1), :].rearrange("p a t -> p (a t)")
                            dve.wait_ge(f_prod, pair + (f0 + 1))
                            split_lo(y, prod[:, j, :], yh, pair + y0)
                            if not both:
                                pass
                        if both:
                            own.leave(n // 2)
                        else:
                            own.leave(n // 2)
                    if down != ffn_plan(first)[-1][3]:
                        for m in range(DT):
                            dve.wait_ge(blocks_done, down + m + 1)
                            nc.vector.tensor_tensor(h[:, m, :], ps[:, m % RING, :], h[:, m, :], ALU.add).then_inc(banks_freed, 1)

            nc.vector.memset(slab[:, 16 * SEQ:16 * SEQ + 6 * WP], 0.0).then_inc(vstep, 1)
            own.tick()
            dve.wait_ge(loaded_cols, 16)
            nc.vector.tensor_tensor(gain_12[:], cols[:, COLS["final_norm_g"]:COLS["final_norm_g"] + DT],
                                    cols[:, COLS["norm1_g_2"]:COLS["norm1_g_2"] + DT], ALU.mult).then_inc(gain_ready, 1)
            dve.wait_ge(loaded_mem, 16)
            for m in range(DT):
                split_gain_lo(TILE0[NORM_MEM] + m, memg_lo[:, m, :], mem[:, m, :], col("mem_norm_g", m), memg_hi[:, m, :])
                add_squares(SQ0[NORM_MEM] + m, 0, m == 0, MEM)
            variance(NORM_MEM, D, MT)
            spread(NORM_MEM, 1, MT)
            for m in range(DT):
                if m in (0, 4):
                    dve.wait_ge((loaded_x0, loaded_x1)[m // 4], 16)
                split_gain_lo(TILE0[NORM_MIX] + m, xg_lo[:, m, :], h[:, m, :], col("norm_mix_g", m), xg_hi[:, m, :])
                add_squares(SQ0[NORM_MIX] + m, 1, m == 0)
                multiply_by_rstd(k1[:, m, :], MEMK + m, m % RING, MEM).then_inc(banks_freed, 1)
            for half_ in range(2):
                dve.wait_ge(blocks_done, MEMV + 4 * half_ + 4)
                for t in range(MT):
                    nc.vector.tensor_scalar(v1[:, t, half_ * SEQ:(half_ + 1) * SEQ], ps[:, 2 * half_ + t, :],
                                            rcol[:, NORM_MEM, t:t + 1], None, ALU.mult).then_inc(banks_freed, 1)
                if half_ == 0:
                    dve.wait_ge(loaded_mats, 32)
                    dve.wait_ge(consts, 7)
                    nc.vector.tensor_tensor(sgu_w, sgu_w, mask_incl[:].rearrange("p (a t) -> p a t", a=1)
                                            .broadcast_to([P, 4, P]), ALU.mult).then_inc(sgu_masked, 1)
            variance(NORM_MIX, D)
            spread(NORM_MIX, 2)

            dve.wait_ge(blocks_done, INV + 4)
            for t in range(ST):
                nc.vector.tensor_scalar(vtok[:, t, :], ps[:, t, :], rcol[:, NORM_MIX, t:t + 1], None,
                                        ALU.mult).then_inc(v_scaled, 1)
            dve.wait_ge(v_scaled, ST)
            for t in range(ST):
                nc.vector.memset(tiny[:, 3, t:t + 1], 0.0).then_inc(banks_freed, 1)
            for t in range(ST):
                dve.wait_ge(v_gelu, t + 1)
                nc.vector.bn_stats(bn[:, t, :], vtok[:, t, :]).then_inc(vstep, 1)
                own.tick()
            for t in range(ST):
                dve.wait_ge(vstep, own.now() - (ST - 1 - t) if t == 0 else own.now() - (ST - 1))
                nc.vector.bn_aggr(bna[:, t, :], bn[:, t, :]).then_inc(vstep, 1)
                own.tick()
            dve.wait_ge(vstep, own.now())
            for t in range(ST):
                nc.vector.tensor_scalar(tiny[:, 1, t:t + 1], bna[:, t, 1:2], EPS, None, ALU.add).then_inc(v_var, 1)

            def pool_windows(g):
                multiply_by_rstd(pp[:, g, PAD:], INP + g, g).then_inc(banks_freed, 1)
                dve.wait_ge(banks_freed, INP + g + 1 - USE_LAG)
                src, step, at = pp[:, g, :], 1, 0
                while step < POOL_WINDOWS[g]:
                    dst = win[:, at, :]
                    nc.vector.tensor_tensor(dst[:, step:], src[:, step:], src[:, 0:WP - step], ALU.add).then_inc(vstep, 1)
                    own.tick()
                    dve.wait_ge(vstep, own.now())
                    src, step, at = dst, 2 * step, 1 - at
                nc.vector.tensor_tensor(src[:, PAD:2 * PAD], src[:, PAD:2 * PAD], corr[:, g, :], ALU.mult).then_inc(vstep, 1)
                own.tick()
                dve.wait_ge(vstep, own.now())
                nc.vector.scalar_tensor_tensor(out=pp[:, g, PAD:], in0=src[:, PAD:], scalar=1.0 / POOL_WINDOWS[g],
                                               in1=pp[:, g, PAD:], op0=ALU.mult, op1=ALU.subtract).then_inc(pooled, 1)
                dve.wait_ge(pooled, g + 1)

            pool_windows(0)
            dve.wait_ge(v_rstd, 1)
            for t in range(ST):
                nc.vector.tensor_scalar(vtok[:, t, :], vtok[:, t, :], bna[:, t, 0:1], tiny[:, 0, t:t + 1], ALU.subtract,
                                        ALU.mult).then_inc(vstep, 1)
                own.tick()
            for t in range(ST):
                dve.wait_ge(vstep, own.now() - (ST - 1 - t))
                nc.vector.tensor_tensor(vtok[:, t, :], vtok[:, t, :], sgu_g, ALU.mult).then_inc(vn_ready, 1)
            for g in range(1, 4):
                pool_windows(g)
            for t in range(4):
                multiply_by_rstd(u[:, t, :], INU + t, t).then_inc(banks_freed, 1)
                if t == 0:
                    for g in range(4):
                        dve.wait_ge(y_hi_ready, Y_MIX + g + 1)
                        nc.vector.scalar_tensor_tensor(out=y_lo[:, g, :], in0=ps[:, AUX + g, :], scalar=col("pool_scale", g),
                                                       in1=y_hi[:, g, :].bitcast(F32), op0=ALU.mult,
                                                       op1=ALU.subtract).then_inc(y_lo_ready, 1)
            for g in range(4):
                dve.wait_ge(z_done, g + 1)
                z = ps[:, AUX + g, :].rearrange("p (c t) -> p c t", t=P)
                nc.vector.tensor_tensor(z, z, sgu_b[:, g:g + 1, :].broadcast_to([P, ST, P]), ALU.add).then_inc(sgu_prod, 1)
                dve.wait_ge(sgu_prod, 2 * g + 1)
                dve.wait_ge(u_gelu, g + 1)
                nc.vector.tensor_tensor(u[:, g, :], ps[:, AUX + g, :], u[:, g, :], ALU.mult).then_inc(sgu_prod, 1)
                dve.wait_ge(sgu_prod, 2 * g + 2)
                split_lo(y_lo[:, 4 + g, :], u[:, g, :], y_hi[:, 4 + g, :], Y_MIX + 4 + g)
            residual(WOUT, NORM_XATTN, lambda m: col("norm_xattn_g", m))

            def x_max(hd):
                for b in range(2):
                    dve.wait_ge(x_scores, 2 * hd + b + 1)
                    nc.vector.tensor_reduce(top[:, hd, 2 * b:2 * b + 2], ps[:, AUX + b, :].rearrange("p (a m) -> p a m", m=MEM),
                                            AX.X, ALU.max).then_inc(vstep, 1)
                    own.tick()
                dve.wait_ge(vstep, own.now())
                nc.vector.tensor_scalar(top[:, hd, :], top[:, hd, :], -(MEM ** -0.5), None, ALU.mult).then_inc(x_top, 1)

            def x_normalise(hd):
                dve.wait_ge(x_exp, ST * (hd + 1))
                nc.vector.reciprocal(rsum[:, hd, :], rsum[:, hd, :]).then_inc(vstep, 1)
                own.tick()
                dve.wait_ge(vstep, own.now())
                for t in range(ST):
                    nc.vector.tensor_scalar(probs[:, hd % 2, t, :], probs[:, hd % 2, t, :], rsum[:, hd, t:t + 1], None,
                                            ALU.mult).then_inc(x_probs, 1)

            def x_turn(hd):
                for m in range(MT):
                    dve.wait_ge(x_turned, 2 * hd + m + 1)
                    nc.vector.tensor_copy(probs_t[:, m, :], ps[:, AUX + 2 + m, :]).then_inc(x_copied, 1)

            def x_lo(hd):
                for d in range(2):
                    t = 2 * hd + d
                    split_lo(y_lo[:, t, :], ps[:, AUX + 2 + d, :], y_hi[:, t, :], Y_X + t)

            variance(NORM_XATTN, D)
            spread(NORM_XATTN, 3)

            def x_query(m):
                multiply_by_rstd(q1[:, m, :], WQ + m, m % RING).then_inc(banks_freed, 1)

            for m in range(4):
                x_query(m)
            x_max(0)
            x_query(4)
            x_query(5)
            for hd in range(XH):
                if hd == 1:
                    x_query(6)
                    x_query(7)
                x_normalise(hd)
                x_turn(hd)
                x_lo(hd)
                if hd + 1 < XH:
                    x_max(hd + 1)
            residual(WO, NORM_FFN, lambda m: col("norm_ffn_g", m))
            variance(NORM_FFN, D)
            spread(NORM_FFN, 4)
            ffn(FFN1, True)
            residual(ffn_plan(FFN1)[-1][3], NORM_FINAL, lambda m: gain_12[:, m:m + 1])

            variance(NORM_FINAL, D)
            dve.wait_ge(rcol_ready, NORM_FINAL + 1)
            nc.vector.tensor_tensor(tiny[:, 0, 0:ST], rcol[:, NORM_FINAL, :], rcol[:, NORM_FINAL, :], ALU.mult).then_inc(vstep, 1)
            own.tick()
            dve.wait_ge(vstep, own.now())
            nc.vector.tensor_tensor(tiny[:, 0, 0:ST], ps[:, AUX, ST:2 * ST], tiny[:, 0, 0:ST], ALU.mult).then_inc(vstep, 1)
            own.tick()
            dve.wait_ge(vstep, own.now())
            nc.vector.tensor_scalar(var[:, 0:ST], tiny[:, 0, 0:ST], 1.0 / D, EPS, ALU.mult, ALU.add).then_inc(var_ready, 1)
            spread(NORM_FINAL, 5)
            for m in range(DT):
                nc.vector.scalar_tensor_tensor(out=h[:, m, :], in0=h[:, m, :], scalar=col("final_norm_g", m), in1=rstd_bc[:],
                                               op0=ALU.mult, op1=ALU.mult).then_inc(vstep, 1)
                own.tick()
            dve.wait_ge(rcol_ready, NORM_ONE + 1)
            dve.wait_ge(vstep, own.now())
            nc.vector.tensor_tensor(rcol[:, NORM_ONE, :], rcol[:, NORM_ONE, :], rcol[:, NORM_FINAL, :], ALU.mult).then_inc(vstep, 1)
            own.tick()
            dve.wait_ge(vstep, own.now())
            spread(NORM_ONE, 6)

            tap_order = [(i0 + i, j) for i0 in (0, 2) for j in range(1, TAPS) for i in range(2)]
            taps_done = Count()

            def conv_taps(n):
                for _ in range(n):
                    if not tap_order:
                        return
                    i, j = tap_order.pop(0)
                    if j == 1:
                        dve.wait_ge(conv_init, i + 1)
                    else:
                        dve.wait_ge(ln_sum, taps_done.now() - 1)
                    nc.vector.scalar_tensor_tensor(out=conv[:, i, j:], in0=conv_in[:, i, 0:SEQ - j],
                                                   scalar=col("conv_dw_w_2", (TAPS - 1 - j) * 4 + i),
                                                   in1=conv[:, i, j:], op0=ALU.mult, op1=ALU.add).then_inc(ln_sum, 1)
                    taps_done.tick()

            for i in range(4):
                multiply_by_rstd(q2[:, i, :], GLU + 2 * i, (2 * i) % RING).then_inc(banks_freed, 1)
                multiply_by_rstd(k2[:, i, :], GLU + 2 * i + 1, (2 * i + 1) % RING).then_inc(banks_freed, 1)
                dve.wait_ge(banks_freed, GLU + 2 * i + 2 - USE_LAG)
                dve.wait_ge(glu_sig, i + 1)
                nc.vector.tensor_tensor(conv_in[:, i, :], q2[:, i, :], k2[:, i, :], ALU.mult).then_inc(glu_done, 1)
                if i >= 2:
                    conv_taps(8)
            conv_taps(16)
            dve.wait_ge(blocks_done, V2 + 4)
            for t in range(ST):
                nc.vector.tensor_scalar(v2[:, t, :], ps[:, t, :], rcol[:, NORM_ONE, t:t + 1], None, ALU.mult).then_inc(banks_freed, 1)

            def qk_square_sums(t):
                dve.wait_ge(qk_sums, t + 1)
                if t >= 2:
                    dve.wait_ge(qk_rstd, t - 1)
                nc.vector.tensor_scalar(tiny[:, t % 2, :], ps[:, AUX, 0:8], 1.0 / HD, EPS, ALU.mult, ALU.add).then_inc(qk_var, 1)

            def qk_scale(t):
                dve.wait_ge(qk_rstd, t + 1)
                nc.vector.tensor_scalar(wide[:].rearrange("p a (b c) -> p (a b) c", b=2),
                                        tiny[:, 2 + t % 2, :].rearrange("p (a b) -> p a b", b=1).broadcast_to([P, 8, HD]),
                                        HD ** -0.5 if t % 2 == 0 else 1.0, None, ALU.mult).then_inc(qk_wide, 1)

            def qk_apply(t):
                dst = (q2, k2)[t % 2][:, t // 2, :]
                dve.wait_ge(qk_spread, t + 1)
                nc.vector.scalar_tensor_tensor(out=dst, in0=dst, scalar=col(("q_norm_g_2", "k_norm_g_2")[t % 2], 0),
                                               in1=ps[:, AUX + 1, :], op0=ALU.mult, op1=ALU.mult).then_inc(qk_ready, 1)

            for t in range(8 + 2):
                if t < 8:
                    multiply_by_rstd((q2, k2)[t % 2][:, t // 2, :], QK + t, t % RING).then_inc(banks_freed, 1)
                if t >= 2:
                    qk_apply(t - 2)
                if 1 <= t <= 8:
                    qk_square_sums(t - 1)
                    conv_taps(6)
                    qk_scale(t - 1)

            BANKS = ((0, 0, 512), (1, 512, 512), (2, 1024, 256))
            TILES = ((0, 0, 512), (1, 512, 384), (2, 1024, 256), (1, 896, 128))

            def z_of(hd, tile):
                bank, at, n = TILES[tile]
                return ps[:, 3 * (hd % 2) + bank, at - 512 * bank:at - 512 * bank + n]

            def s_minimum(hd):
                if hd >= 3:
                    dve.wait_ge(s_out, hd - 2)
                for bank, at, n in BANKS:
                    dve.wait_ge(s_z, 3 * hd + bank + 1)
                    i = nc.vector.tensor_scalar(stick[:, hd % 3, at:at + n], ps[:, 3 * (hd % 2) + bank, 0:n], Z_MAX, None, ALU.min)
                    if bank < 2:
                        i.then_inc(vstep, 1)
                        own.tick()
                i.then_inc(s_min, 1)

            def s_softplus(hd):
                t = stick[:, hd % 3, :]
                dve.wait_ge(s_log, hd + 1)
                for bank, at, n in BANKS:
                    nc.vector.tensor_tensor(t[:, at:at + n], ps[:, 3 * (hd % 2) + bank, 0:n], t[:, at:at + n], ALU.max).then_inc(vstep, 1)
                    own.tick()
                dve.wait_ge(vstep, own.now())
                for _, at, _ in TILES:
                    nc.vector.tensor_tensor(t[:, at:at + P], t[:, at:at + P], mask_strict[:], ALU.mult).then_inc(vstep, 1)
                    own.tick()
                dve.wait_ge(vstep, own.now())
                later = later_sums[:, hd % 2, :]
                if hd >= 2:
                    dve.wait_ge(s_cum, hd - 1)
                o = [at for _, at, _ in TILES]
                for dst, a, b in ((later[:, 0:P], t[:, o[2] + P:o[2] + 2 * P], t[:, o[3]:o[3] + P]),
                                  (later[:, P:2 * P], t[:, o[1] + P:o[1] + 2 * P], t[:, o[2]:o[2] + P])):
                    nc.vector.tensor_tensor(dst, a, b, ALU.add).then_inc(vstep, 1)
                    own.tick()
                dve.wait_ge(vstep, own.now())
                nc.vector.tensor_tensor(later[:, 2 * P:3 * P], t[:, o[1] + 2 * P:o[1] + 3 * P], later[:, 0:P],
                                        ALU.add).then_inc(s_sp, 1)

            def s_cutoff(hd):
                dve.wait_ge(s_cum, hd + 1)
                for tile in range(ST):
                    d = z_of(hd, tile)[:, 0:P]
                    i = nc.vector.tensor_tensor(d, d, mask_min[:], ALU.min)
                    if tile < ST - 1:
                        i.then_inc(vstep, 1)
                        own.tick()
                i.then_inc(s_cut, 1)

            s_minimum(0)
            s_softplus(0)
            for hd in range(HEADS):
                if hd + 1 < HEADS:
                    s_minimum(hd + 1)
                s_cutoff(hd)
                if hd + 1 < HEADS:
                    s_softplus(hd + 1)
                if hd < 6:
                    conv_taps(8)
                if hd % 2 == 0 and hd >= 2:
                    split_lo(y_lo[:, hd // 2 - 1, :], ps[:, 6, :], y_hi[:, hd // 2 - 1, :], Y_MIX2 + hd // 2 - 1)
                if hd == 5:
                    assert not tap_order
                    n_taps = taps_done.now()
                    dve.wait_ge(ln_sum, n_taps)
                    nc.vector.tensor_tensor(ssq[:, 0, :], conv[:, 0, :], conv[:, 1, :], ALU.add).then_inc(vstep, 1)
                    nc.vector.tensor_tensor(ssq[:, 1, :], conv[:, 2, :], conv[:, 3, :], ALU.add).then_inc(vstep, 1)
                    own.tick()
                    own.tick()
                    dve.wait_ge(vstep, own.now())
                    nc.vector.tensor_tensor(ssq[:, 0, :], ssq[:, 0, :], ssq[:, 1, :], ALU.add).then_inc(ln_col, 1)
                    dve.wait_ge(ln_sums, 1)
                    nc.vector.tensor_scalar(wide[:], ps[:, 7, 0:ST].rearrange("p (a b) -> p a b", b=1).broadcast_to([P, ST, P]),
                                            1.0 / SEQ, None, ALU.mult).then_inc(ln_wide, 1)
                    dve.wait_ge(ln_spread, 1)
                    for i in range(4):
                        nc.vector.tensor_tensor(conv[:, i, :], conv[:, i, :], ps[:, 7, :], ALU.subtract).then_inc(ln_xc, 1)
                if hd == 6:
                    for i in range(4):
                        dve.wait_ge(ln_square, i + 1)
                        if i == 0:
                            nc.vector.tensor_copy(ssq[:, 0, :], sq[:, i % 2, :]).then_inc(ln_sq, 1)
                        else:
                            dve.wait_ge(ln_sq, i)
                            nc.vector.tensor_tensor(ssq[:, 0, :], ssq[:, 0, :], sq[:, i % 2, :], ALU.add).then_inc(ln_sq, 1)
                    dve.wait_ge(ln_sums, 2)
                    nc.vector.tensor_scalar(var[:, 4:8], ps[:, 7, 0:ST], 1.0 / SEQ, EPS, ALU.mult, ALU.add).then_inc(ln_var, 1)
            dve.wait_ge(ln_rstd, 1)
            nc.vector.tensor_copy(wide[:], rcol[:, 7, :].rearrange("p (a b) -> p a b", b=1).broadcast_to([P, ST, P])).then_inc(ln_wide, 1)
            dve.wait_ge(ln_spread, 2)
            for i in range(4):
                nc.vector.tensor_tensor(conv[:, i, :], conv[:, i, :], ps[:, 7, :], ALU.mult).then_inc(ln_norm, 1)
            split_lo(y_lo[:, 3, :], ps[:, 6, :], y_hi[:, 3, :], Y_MIX2 + 3)
            for i in range(4):
                split_lo(y_lo[:, 4 + i, :], conv[:, i, :], y_hi[:, 4 + i, :], Y_MIX2 + 4 + i)
            residual(WOUT2, NORM_TWO, lambda m: col("norm2_g_2", m))
            variance(NORM_TWO, D)
            spread(NORM_TWO, 7)
            ffn(FFN2, False)
            down = ffn_plan(FFN2)[-1][3]
            for m in range(DT):
                dve.wait_ge(blocks_done, down + m + 1)
                nc.vector.tensor_tensor(h[:, m, :], ps[:, m % RING, :], h[:, m, :], ALU.add).then_inc(banks_freed, 1)

        @block.tensor
        def _(pe):
            def three(out, w, x, first, last):
                pe.matmul(out, w[0], x[0], start=first, stop=False)
                pe.matmul(out, w[0], x[1], start=False, stop=False)
                return pe.matmul(out, w[1], x[0], start=False, stop=last)

            def features(b, use, s, x, kt=8, width=SEQ, ready=None):
                pe.wait_ge(w_lo_ready, b + 1)
                if not isinstance(use, int) or use >= RING:
                    pe.wait_ge(banks_freed, use + 1 - RING)
                for k in range(kt):
                    if ready is not None:
                        pe.wait_ge(*ready(k))
                    c = slice(k * P, (k + 1) * P)
                    mm = three(ps[:, s, 0:width], (w_hi[:, s, c], w_lo[:, s, c]),
                               (x[0][:, k, 0:width], x[1][:, k, 0:width]), k == 0, k == kt - 1)
                mm.then_inc(blocks_done, 1)

            def tokens(first, use, x, nt, bank0, ready=None):
                pe.wait_ge(banks_freed, use + 1 - RING + nt - 1)
                for s in range(4):
                    pe.wait_ge(w_lo_ready, first + s + 1)
                    for kk in range(2):
                        k = 2 * s + kk
                        if ready is not None:
                            pe.wait_ge(*ready(k))
                        c = slice(kk * SEQ, (kk + 1) * SEQ)
                        for t in range(nt):
                            tok = slice(t * P, (t + 1) * P)
                            out = ps[:, bank0 + t, :]
                            pe.matmul(out, x[0][:, k, tok], w_hi[:, s, c], start=k == 0, stop=False)
                            pe.matmul(out, x[1][:, k, tok], w_hi[:, s, c], start=False, stop=False)
                            mm = pe.matmul(out, x[0][:, k, tok], w_lo[:, s, c], start=False, stop=k == DT - 1)
                    mm.then_inc(blocks_done, 1)

            def square_sums(added, sizes=ST, which=(0,)):
                pe.wait_ge(sq_added, added)
                for i, w in enumerate(which):
                    for t in range(sizes):
                        mm = pe.matmul(ps[:, AUX, i * ST + t:i * ST + t + 1], ssq[:, w, t * P:(t + 1) * P], ones[:],
                                       start=True, stop=True)
                mm.then_inc(sums_ready, 1)

            def turn_wide(n, sizes=ST):
                pe.wait_ge(wide_ready, n)
                for t in range(sizes):
                    mm = pe.transpose(ps[:, AUX + 1, t * P:(t + 1) * P], wide[:, t, :], ident[:])
                mm.then_inc(spread_ready, 1)

            def tile_ready(norm):
                return lambda k: (tile_lo, TILE0[norm] + k + 1)

            def y_ready(y0):
                return lambda k: (y_lo_ready, y0 + k + 1)

            xg, yy = (xg_hi, xg_lo), (y_hi, y_lo)

            pe.wait_ge(consts, 7)
            for m in range(8):
                features(MEMK + m, m, m % RING, (memg_hi, memg_lo), width=MEM, ready=tile_ready(NORM_MEM) if m == 0 else None)
                if m == 0:
                    square_sums(SQ0[NORM_MEM] + 8, MT)
                if m == 1:
                    turn_wide(1, MT)
            tokens(MEMV, 8, (memg_hi, memg_lo), MT, 0)
            tokens(MEMV + 4, 10, (memg_hi, memg_lo), MT, 2)
            square_sums(SQ0[NORM_MIX] + 8, which=(1,))
            tokens(INV, 12, xg, ST, 0, tile_ready(NORM_MIX))
            turn_wide(2)
            for g in range(4):
                features(INP + g, INP + g - USE_LAG, g, xg)
            for t in range(4):
                features(INU + t, INU + t - USE_LAG, t, xg)
                if t == 0:
                    for g in range(4):
                        pe.wait_ge(pooled, g + 1)
                        pe.matmul(ps[:, AUX + g, :], pool_w[:, g, :], pp[:, g, PAD:], start=True, stop=True).then_inc(pool_done, 1)
            pe.wait_ge(vn_ready, ST)
            pe.wait_ge(sgu_masked, 1)
            for hd in range(4):
                pe.wait_ge(y_lo_ready, Y_MIX + hd + 1)
                for c in range(ST):
                    mm = pe.matmul(ps[:, AUX + hd, c * P:(c + 1) * P], vtok[:, c, hd * P:(hd + 1) * P], sgu_w[:, hd, :],
                                   start=True, stop=True)
                mm.then_inc(z_done, 1)
            for m in range(DT):
                features(WOUT + m, WOUT + m - USE_LAG, m % RING, yy, ready=y_ready(Y_MIX) if m == 0 else None)

            def x_scores_of(hd):
                pe.wait_ge(banks_freed, WQ + 2 * hd + 2 - USE_LAG)
                if hd >= 1:
                    pe.wait_ge(x_exp, ST * hd)
                for t in range(ST):
                    for d in range(2):
                        mm = pe.matmul(ps[:, AUX + t // 2, (t % 2) * MEM:(t % 2 + 1) * MEM],
                                       q1[:, 2 * hd + d, t * P:(t + 1) * P], k1[:, 2 * hd + d, :], start=d == 0, stop=d == 1)
                    if t % 2:
                        mm.then_inc(x_scores, 1)

            def x_values(hd):
                if hd >= 1:
                    pe.wait_ge(y_lo_ready, Y_X + 2 * hd)
                pe.wait_ge(x_probs, ST * (hd + 1))
                for m in range(MT):
                    for t in range(ST):
                        mm = pe.transpose(ps[:, AUX + 2 + m, t * P:(t + 1) * P], probs[:, hd % 2, t, m * P:(m + 1) * P], ident[:])
                    mm.then_inc(x_turned, 1)
                pe.wait_ge(x_copied, 2 * (hd + 1))
                for d in range(2):
                    for m in range(MT):
                        mm = pe.matmul(ps[:, AUX + 2 + d, :], v1[:, m, (2 * hd + d) * P:(2 * hd + d + 1) * P], probs_t[:, m, :],
                                       start=m == 0, stop=m == MT - 1)
                    mm.then_inc(x_out, 1)

            def query(m, ready=None):
                features(WQ + m, WQ + m - USE_LAG, m % RING, xg, ready=ready)

            query(0, tile_ready(NORM_XATTN))
            square_sums(SQ0[NORM_XATTN] + 8)
            query(1)
            turn_wide(3)
            query(2)
            query(3)
            x_scores_of(0)
            query(4)
            query(5)
            x_values(0)
            x_scores_of(1)
            query(6)
            query(7)
            for hd in range(1, XH):
                x_values(hd)
                if hd + 1 < XH:
                    x_scores_of(hd + 1)
            for m in range(DT):
                features(WO + m, WO + m - USE_LAG, m % RING, yy, ready=y_ready(Y_X) if m == 0 else None)

            def ffn(first, norm, wides, y0):
                for first_b, n, pair0, down in ffn_plan(first):
                    start = 0
                    if pair0 == 0:
                        start = 1
                        for s in range(RING):
                            features(first_b + s, first_b + s - USE_LAG, s, xg, ready=tile_ready(norm) if s == 0 else None)
                            if s == 0:
                                square_sums(SQ0[norm] + 8)
                            if s == 1:
                                turn_wide(wides)
                    with pe.Fori(start, n // 2) as i:
                        for s in range(RING):
                            features(i * RING + (first_b + s), i * RING + (first_b + s - USE_LAG), s, xg)
                    with pe.Fori(0, DT // RING) as i:
                        for s in range(RING):
                            features(i * RING + (down + s), i * RING + (down + s - USE_LAG), s, yy, kt=n,
                                     ready=y_ready(y0 + pair0) if s == 0 else None)

            ffn(FFN1, NORM_FFN, 4, Y_F1)

            features(GLU, GLU - USE_LAG, 0, xg, ready=tile_ready(NORM_ONE))
            square_sums(SQ0[NORM_FINAL] + 16, which=(0, 1))
            features(GLU + 1, GLU + 1 - USE_LAG, 1, xg)
            features(GLU + 2, GLU + 2 - USE_LAG, 2, xg)
            turn_wide(5)
            features(GLU + 3, GLU + 3 - USE_LAG, 3, xg)
            turn_wide(6)
            for b in range(GLU + 4, V2):
                features(b, b - USE_LAG, b % RING, xg)
            tokens(V2, V2 - USE_LAG, xg, ST, 0)

            def qk_sum(t):
                if t >= 1:
                    pe.wait_ge(qk_var, t)
                pe.wait_ge(qk_square, t + 1)
                for c in range(ST):
                    mm = pe.matmul(ps[:, AUX, 2 * c:2 * c + 2], sq[:, t % 2, c * P:(c + 1) * P], half[:], start=True, stop=True)
                mm.then_inc(qk_sums, 1)

            def qk_turn(t):
                if t >= 1:
                    pe.wait_ge(qk_ready, t)
                pe.wait_ge(qk_wide, t + 1)
                for c in range(ST):
                    mm = pe.transpose(ps[:, AUX + 1, c * P:(c + 1) * P], wide[:, c, :], ident[:])
                mm.then_inc(qk_spread, 1)

            for t in range(8 + 2):
                if t < 8:
                    features(QK + t, QK + t - USE_LAG, t % RING, xg)
                if t >= 2:
                    qk_turn(t - 2)
                if 1 <= t <= 8:
                    qk_sum(t - 1)

            TILES = ((0, 0, 512), (1, 0, 384), (2, 0, 256), (1, 384, 128))
            AT = (0, 512, 1024, 896)

            def s_scores(hd):
                if hd < 2:
                    pe.wait_ge(banks_freed, WOUT2 - USE_LAG)
                    pe.wait_ge(qk_ready, 8)
                else:
                    pe.wait_ge(s_att, 3 * (hd - 1))
                r = slice(HD * (hd % 2), HD * (hd % 2) + HD)
                for tile in (0, 1, 3, 2):
                    bank, at, n = TILES[tile]
                    mm = pe.matmul(ps[:, 3 * (hd % 2) + bank, at:at + n], k2[r, hd // 2, tile * P:(tile + 1) * P],
                                   q2[r, hd // 2, tile * P:], start=tile != 3, stop=False, skip_group_check=True)
                    if tile != 1:
                        mm.then_inc(s_z, 1)

            def s_cumulate(hd):
                t = stick[:, hd % 3, :]
                later = later_sums[:, hd % 2, :]
                pe.wait_ge(s_sp, hd + 1)

                def add(tile, col0, n, w, src):
                    bank, at, _ = TILES[tile]
                    return pe.matmul(ps[:, 3 * (hd % 2) + bank, at + col0:at + col0 + n], w[:], src, start=False, stop=True,
                                     skip_group_check=True)

                for tile in range(ST):
                    add(tile, 0, TILES[tile][2], neg_tri, t[:, AT[tile]:AT[tile] + TILES[tile][2]])
                add(2, P, P, neg_ones, t[:, AT[3]:AT[3] + P])
                add(1, P, P, neg_ones, t[:, AT[2]:AT[2] + P])
                add(1, 2 * P, P, neg_ones, later[:, 0:P])
                add(0, P, P, neg_ones, t[:, AT[1]:AT[1] + P])
                add(0, 2 * P, 2 * P, neg_ones, later[:, P:3 * P]).then_inc(s_cum, 1)

            def s_values(hd):
                t = stick[:, hd % 3, :]
                r = slice(HD * (hd % 2), HD * (hd % 2) + HD)
                if hd % 2 == 0 and hd >= 2:
                    pe.wait_ge(y_lo_ready, Y_MIX2 + hd // 2)
                pe.wait_ge(s_att, 3 * (hd + 1))
                for tile in range(ST):
                    mm = pe.matmul(ps[r, 6, tile * P:], v2[:, tile, hd * HD:(hd + 1) * HD],
                                   t[:, AT[tile]:AT[tile] + TILES[tile][2]], start=tile == 0, stop=tile == ST - 1,
                                   skip_group_check=True)
                mm.then_inc(s_out, 1)

            def ln_column_sums(n):
                if n == 0:
                    pe.wait_ge(ln_col, 1)
                else:
                    pe.wait_ge(ln_sq, 4)
                for c in range(ST):
                    mm = pe.matmul(ps[:, 7, c:c + 1], ssq[:, 0, c * P:(c + 1) * P], ones[:], start=True, stop=True)
                mm.then_inc(ln_sums, 1)

            def ln_turn(n):
                pe.wait_ge(ln_wide, n + 1)
                for c in range(ST):
                    mm = pe.transpose(ps[:, 7, c * P:(c + 1) * P], wide[:, c, :], ident[:])
                mm.then_inc(ln_spread, 1)

            s_scores(0)
            for hd in range(HEADS):
                if hd + 1 < HEADS:
                    s_scores(hd + 1)
                s_cumulate(hd)
                if hd >= 1:
                    s_values(hd - 1)
                if hd == 5:
                    ln_column_sums(0)
                    ln_turn(0)
                if hd == 6:
                    pass
            ln_column_sums(1)
            s_values(HEADS - 1)
            ln_turn(1)
            for m in range(DT):
                features(WOUT2 + m, WOUT2 + m - USE_LAG, m % RING, yy, ready=y_ready(Y_MIX2) if m == 0 else None)
            ffn(FFN2, NORM_TWO, 7, Y_F2)


def _feature_blocks(w):
    k, m = w.shape
    return w.reshape(k // P, P, m // P, P).transpose(2, 1, 0, 3).reshape(m // P, P, k)


def _token_blocks(w):
    return w.reshape(4, 2, P, SEQ).transpose(0, 2, 1, 3).reshape(4, P, BLK)


def _ffn_blocks(up, down, halves):
    ups = _feature_blocks(up)
    out, pair = [], 0
    for n in FFN_CHUNKS:
        out.append(np.stack([ups[pair:pair + n], ups[FT + pair:FT + pair + n]], 1).reshape(2 * n, P, BLK))
        part = _feature_blocks(down[pair * P:(pair + n) * P])
        out.append(np.pad(part, ((0, 0), (0, 0), (0, BLK - n * P))))
        pair += n
    return out


def kernel(**inputs):
    import concourse.bacc as _bacc
    from concourse.bass_utils import run_bass_kernel_spmd as _run

    a = {n: np.asarray(v) for n, v in inputs.items()}
    g = {n: (v if n in ("x", "mem", "final_norm_g") else v[0]) for n, v in a.items()}

    def columns(v):
        return v.reshape(-1, P).T

    parts = []
    for name in COLS:
        v = g[name]
        if name in ("q_norm_g_2", "k_norm_g_2"):
            v = np.concatenate([v, v])
        parts.append(columns(v))
    cols = np.concatenate(parts, 1)
    rows = np.concatenate([g["sgu_g"], g["sgu_b"].reshape(-1)])
    mats = np.concatenate([g["pool_w"].transpose(1, 0, 2).reshape(P, 512), g["sgu_w"].transpose(2, 0, 1).reshape(P, 512),
                           np.broadcast_to(rows, (P, 1024))], 1)
    corr = np.array([[w / min(t + 1, w) for t in range(PAD)] for w in POOL_WINDOWS], np.float32)
    corr = np.broadcast_to(corr, (P, 4, PAD))
    w_in, w_in2 = g["w_in"], g["w_in_2"]
    glu = _feature_blocks(w_in2[:, 1536:2560])
    qk = _feature_blocks(w_in2[:, 0:1024])
    stream = [
        _feature_blocks(g["wk"]), _token_blocks(g["wv"][:, 0:512]), _token_blocks(g["wv"][:, 512:1024]),
        _token_blocks(w_in[:, 1024:1536]), _feature_blocks(w_in[:, 0:512]), _feature_blocks(w_in[:, 512:1024]),
        _feature_blocks(g["w_out"]), _feature_blocks(g["wq"]), _feature_blocks(g["wo"]),
        *_ffn_blocks(g["w_up"], g["w_down"], 2),
        np.stack([glu[0:4], glu[4:8]], 1).reshape(8, P, BLK), _token_blocks(w_in2[:, 1024:1536]),
        np.stack([qk[0:4], qk[4:8]], 1).reshape(8, P, BLK), _feature_blocks(g["w_out_2"]),
        *_ffn_blocks(g["w_up_2"], g["w_down_2"], 1),
    ]
    w = np.concatenate(stream, 0)
    assert w.shape == (BLOCKS, P, BLK), w.shape
    arrays = {
        "mem_t": g["mem"][0].T.reshape(DT, P, MEM).transpose(1, 0, 2),
        "x_t": g["x"][0].T.reshape(DT, P, SEQ).transpose(1, 0, 2),
        "cols_in": cols, "mats_in": mats, "corr_in": corr, "weights": w,
    }
    arrays = {n: np.ascontiguousarray(v) for n, v in arrays.items()}
    nc = _bacc.Bacc("TRN2", target_bir_lowering=False, num_devices=1)
    args = [nc.dram_tensor(n, v.shape, F32, kind="ExternalInput").ap() for n, v in arrays.items()]
    args.append(nc.dram_tensor("out_t", (P, DT, SEQ), F32, kind="ExternalOutput").ap())
    build(nc, *args)
    r = _run(nc, [arrays], core_ids=[0])
    out = np.asarray(r.results[0]["out_t"])
    return out.transpose(1, 0, 2).reshape(D, SEQ).T.reshape(1, SEQ, D)
```

```python
from contextlib import ExitStack

import concourse.bass as bass
import numpy as np
from concourse import mybir

F32 = mybir.dt.float32
F32R = mybir.dt.float32r
ACT = mybir.ActivationFunctionType
ALU = mybir.AluOpType
AX = mybir.AxisListType

P = 128
D = 1024
DT = D // P
SEQ = 512
ST = SEQ // P
MEM = 256
MT = MEM // P
FF = 2816
FT = FF // P
EPS = 1e-6
POOL_WINDOWS = (2, 4, 8, 16)
PAD = 16
XH = 4
HEADS = 8
HD = 64
TAPS = 31
FFN_CHUNKS = (8, 8, 6)
BLK = 8 * P
RING = 4
AUX = 4
X_SCORES = (6, 4)
X_VALUES = 2
Z_MAX = 40.0
FAR_BELOW = -1e30

MEMK = 0
MEMV = MEMK + 8
INV = MEMV + 8
INP = INV + 4
INU = INP + 4
WOUT = INU + 4
WQ = WOUT + 8
WO = WQ + 8
FFN1 = WO + 8
FFN_BLOCKS = 2 * FT + DT * len(FFN_CHUNKS)
GLU = FFN1 + FFN_BLOCKS
V2 = GLU + 8
QK = V2 + 4
WOUT2 = QK + 8
FFN2 = WOUT2 + 8
BLOCKS = FFN2 + FFN_BLOCKS
USE_LAG = 4

COLS = {}
_n = 0
for _name, _k in (("norm_mix_g", DT), ("norm_xattn_g", DT), ("mem_norm_g", DT), ("norm_ffn_g", DT),
                  ("final_norm_g", DT), ("norm1_g_2", DT), ("norm2_g_2", DT), ("pool_scale", 4),
                  ("conv_w", 6 * FT), ("conv_b", 2 * FT), ("ffn_dw_w_2", 3 * FT), ("ffn_dw_b_2", FT),
                  ("conv_dw_w_2", TAPS * 4), ("conv_dw_b_2", 4), ("conv_ln_g_2", 4), ("conv_ln_b_2", 4),
                  ("q_norm_g_2", 1), ("k_norm_g_2", 1)):
    COLS[_name] = _n
    _n += _k
N_COLS = _n

NORM_MEM, NORM_MIX, NORM_XATTN, NORM_FFN, NORM_FINAL, NORM_ONE, NORM_TWO = range(7)
TILE0 = {NORM_MEM: 0, NORM_MIX: 8, NORM_XATTN: 16, NORM_FFN: 24, NORM_ONE: 32, NORM_TWO: 40}
SQ0 = {NORM_MEM: 0, NORM_MIX: 8, NORM_XATTN: 16, NORM_FFN: 24, NORM_FINAL: 32, NORM_TWO: 48}


class Count:

    def __init__(self):
        self.base, self.k = 0, 0

    def tick(self):
        self.k += 1
        return self.now()

    def now(self):
        return self.base + self.k

    def enter(self, i, per):
        self.start, self.per = self.base + self.k, per
        self.base, self.k = self.start + i * per, 0

    def leave(self, times):
        assert self.k == self.per, (self.k, self.per)
        self.base, self.k = self.start + times * self.per, 0


def ffn_plan(first):
    out, b, p = [], first, 0
    for n in FFN_CHUNKS:
        out.append((b, n, p, b + 2 * n))
        b += 2 * n + DT
        p += n
    return out


def build(nc, a_mem, a_x, a_cols, a_mats, a_corr, a_w, a_out):
    ctx = ExitStack()
    with ctx:
        def sb(name, shape, dt=F32):
            return ctx.enter_context(nc.sbuf_tensor(name, shape, dt))

        def sem(name):
            return ctx.enter_context(nc.semaphore(name))

        w_raw = sb("w_raw", [P, RING, BLK])
        w_hi = sb("w_hi", [P, RING, BLK], F32R)
        w_lo = sb("w_lo", [P, RING, BLK], F32R)
        h = sb("h", [P, DT, SEQ])
        xg_hi = sb("xg_hi", [P, DT, SEQ], F32R)
        xg_lo = sb("xg_lo", [P, DT, SEQ], F32R)
        y_hi = sb("y_hi", [P, DT, SEQ], F32R)
        y_lo = sb("y_lo", [P, DT, SEQ], F32R)
        slab = sb("slab", [P, 28 * SEQ])
        memg_hi = y_hi[:, 0:4, :].rearrange("p a (b t) -> p (a b) t", b=2)
        memg_lo = y_lo[:, 0:4, :].rearrange("p a (b t) -> p (a b) t", b=2)

        def units(first, n):
            return slab[:, first * SEQ:(first + n) * SEQ]

        k1 = units(0, 4).rearrange("p (m t) -> p m t", t=MEM)
        v1 = units(4, 4).rearrange("p (m d) -> p m d", d=D)
        mem = units(8, 4).rearrange("p (m t) -> p m t", t=MEM)
        u = units(8, 4).rearrange("p (m t) -> p m t", t=SEQ)
        vtok = units(12, 4).rearrange("p (m d) -> p m d", d=SEQ)
        WP = PAD + SEQ
        pp = slab[:, 16 * SEQ:16 * SEQ + 4 * WP].rearrange("p (m t) -> p m t", t=WP)
        win = slab[:, 16 * SEQ + 4 * WP:16 * SEQ + 6 * WP].rearrange("p (m t) -> p m t", t=WP)
        mats = units(24, 4)
        pool_w = mats[:, 0:512].rearrange("p (g d) -> p g d", g=4)
        sgu_w = mats[:, 512:1024].rearrange("p (g d) -> p g d", g=4)
        sgu_g = mats[:, 1024:1536]
        sgu_b = mats[:, 1536:2048].rearrange("p (g t) -> p g t", g=4)
        q1 = units(8, 8).rearrange("p (m t) -> p m t", t=SEQ)
        probs = units(16, 4).rearrange("p (b a m) -> p b a m", b=2, m=MEM)
        probs_t = units(20, 2).rearrange("p (m t) -> p m t", t=SEQ)
        acc = units(0, 4).rearrange("p (m t) -> p m t", t=SEQ)
        prod = units(4, 2).rearrange("p (m t) -> p m t", t=SEQ)
        q2 = units(0, 4).rearrange("p (m t) -> p m t", t=SEQ)
        k2 = units(4, 4).rearrange("p (m t) -> p m t", t=SEQ)
        v2 = units(8, 4).rearrange("p (m d) -> p m d", d=SEQ)
        conv_in = units(12, 4).rearrange("p (m t) -> p m t", t=SEQ)
        conv = units(16, 4).rearrange("p (m t) -> p m t", t=SEQ)
        STICK = SEQ * ST - P * (ST * (ST - 1) // 2)
        stick = slab[:, 20 * SEQ:20 * SEQ + 3 * STICK].rearrange("p (b t) -> p b t", t=STICK)

        cols = sb("cols", [P, N_COLS])
        corr = sb("corr", [P, 4, PAD])
        gain_12 = sb("gain_12", [P, DT])
        ident = sb("ident", [P, P])
        ones = sb("ones", [P, 1])
        half = sb("half", [P, 2])
        minus_half = sb("minus_half", [P, 8])
        mask_incl = sb("mask_incl", [P, P])
        far_below = sb("far_below", [P, P])
        ident_r = sb("ident_r", [P, P], F32R)
        far_below_r = sb("far_below_r", [P, P], F32R)
        neg_tri = sb("neg_tri", [P, P])
        neg_ones = sb("neg_ones", [P, P])
        z_max = sb("z_max", [P, 1])
        sq = sb("sq", [P, 2, SEQ])
        ssq = sb("ssq", [P, 2, SEQ])
        later_sums = sb("later_sums", [P, 2, 3 * P])
        rstd_bc = sb("rstd_bc", [P, SEQ])
        var = sb("var", [P, 8])
        rcol = sb("rcol", [P, 8, ST])
        wide = sb("wide", [P, ST, P])
        bn = sb("bn", [P, ST, 6])
        bna = sb("bna", [P, ST, 2])
        tiny = sb("tiny", [P, 4, 8])
        top = sb("top", [P, XH, ST])
        rsum = sb("rsum", [P, XH, ST])
        ps = ctx.enter_context(nc.psum_tensor("ps", [P, 8, SEQ], F32))

        def col(name, k):
            return cols[:, bass.ds(COLS[name] + k, 1)]

        loaded_mem, loaded_x0, loaded_x1 = sem("loaded_mem"), sem("loaded_x0"), sem("loaded_x1")
        loaded_cols, loaded_mats = sem("loaded_cols"), sem("loaded_mats")
        w_loaded = [sem(f"w_loaded{s}") for s in range(RING)]
        w_hi_ready, w_lo_ready = sem("w_hi_ready"), sem("w_lo_ready")
        blocks_done, banks_freed = sem("blocks_done"), sem("banks_freed")
        consts0, consts, rounded, gain_ready = sem("consts0"), sem("consts"), sem("rounded"), sem("gain_ready")
        vstep, astep = sem("vstep"), sem("astep")
        tile_hi, tile_lo = sem("tile_hi"), sem("tile_lo")
        sq_ready, sq_added = sem("sq_ready"), sem("sq_added")
        sums_ready, var_ready, rcol_ready = sem("sums_ready"), sem("var_ready"), sem("rcol_ready")
        wide_ready, spread_ready = sem("wide_ready"), sem("spread_ready")
        y_hi_ready, y_lo_ready = sem("y_hi_ready"), sem("y_lo_ready")
        v_scaled, v_gelu, v_var, v_rstd, vn_ready = (sem(n) for n in ("v_scaled", "v_gelu", "v_var", "v_rstd", "vn_ready"))
        u_gelu, pooled, pool_done, z_done, sgu_masked = (sem(n) for n in ("u_gelu", "pooled", "pool_done", "z_done", "sgu_masked"))
        sgu_prod = sem("sgu_prod")
        x_scores, x_top, x_exp, x_probs, x_turned, x_copied, x_out = (
            sem(n) for n in ("x_scores", "x_top", "x_exp", "x_probs", "x_turned", "x_copied", "x_out"))
        f_scaled, f_base, f_silu, f_prod = (sem(n) for n in ("f_scaled", "f_base", "f_silu", "f_prod"))
        glu_sig, glu_done, conv_init = sem("glu_sig"), sem("glu_done"), sem("conv_init")
        qk_sums, qk_var, qk_rstd, qk_wide, qk_spread, qk_ready = (
            sem(n) for n in ("qk_sums", "qk_var", "qk_rstd", "qk_wide", "qk_spread", "qk_ready"))
        s_z, s_min, s_exp, s_log, s_sp, s_cum, s_att, s_out = (
            sem(n) for n in ("s_z", "s_min", "s_exp", "s_log", "s_sp", "s_cum", "s_att", "s_out"))
        ln_sum, ln_sums, ln_col, ln_wide, ln_spread, ln_xc, ln_sq, ln_var, ln_rstd, ln_norm, ln_silu = (
            sem(n) for n in ("ln_sum", "ln_sums", "ln_col", "ln_wide", "ln_spread", "ln_xc", "ln_sq", "ln_var",
                             "ln_rstd", "ln_norm", "ln_silu"))
        qk_square, ln_square = sem("qk_square"), sem("ln_square")
        stored = sem("stored")

        def z_of(hd):
            return ps[:, 3 * (hd % 2):3 * (hd % 2) + 3, :].rearrange("p a t -> p (a t)")[:, 0:STICK]

        Y_MIX, Y_X, Y_F1, Y_MIX2, Y_F2 = 0, 8, 16, 16 + FT, 24 + FT

        block = ctx.enter_context(nc.Block())

        @block.sync
        def _(sp):
            sp.dma_start(mem, a_mem).then_inc(loaded_mem, 16)
            for b in range(RING):
                sp.dma_start(w_raw[:, b, :], a_w[b]).then_inc(w_loaded[b], 16)
            region = [(RING, FFN1 + FFN_BLOCKS - DT, BLK), (FFN1 + FFN_BLOCKS - DT, GLU, FFN_CHUNKS[-1] * P),
                      (GLU, BLOCKS - DT, BLK), (BLOCKS - DT, BLOCKS, FFN_CHUNKS[-1] * P)]
            for first, end, width in region:
                with sp.Fori(0, (end - first) // RING) as i:
                    for s in range(RING):
                        sp.wait_ge(w_lo_ready, i * RING + (first + s + 1 - RING))
                        sp.dma_start(w_raw[:, s, 0:width], a_w[i * RING + (first + s)][:, 0:width]).then_inc(w_loaded[s], 16)
            last_down = ffn_plan(FFN2)[-1][3]
            for m in range(DT):
                sp.wait_ge(banks_freed, last_down + m + 1 - USE_LAG)
                sp.dma_start(a_out[:, m, :], h[:, m, :]).then_inc(stored, 16)
            sp.wait_ge(stored, 16 * DT)

        @block.gpsimd
        def _(pool):
            def weights_lo(b, s):
                pool.wait_ge(w_hi_ready, b + 1)
                nc.gpsimd.tensor_tensor(w_lo[:, s, :], w_raw[:, s, :], w_hi[:, s, :].bitcast(F32),
                                        ALU.subtract).then_inc(w_lo_ready, 1)

            def weights_lo_for(first, n):
                n = min(n, BLOCKS - RING - first)
                if n > 0:
                    with pool.Fori(0, n // RING) as i:
                        for s in range(RING):
                            pool.wait_ge(blocks_done, i * RING + (first + s + 1))
                            weights_lo(i * RING + (first + s + RING), s)

            def rstd(n, sizes=ST):
                pool.wait_ge(var_ready, n + 1)
                nc.gpsimd.tensor_tensor(rcol[:, n, 0:sizes], var[:, 0:sizes], minus_half[:, 0:sizes],
                                        ALU.pow).then_inc(rcol_ready, 1)

            for t, value in ((ident, 0.0), (ones, 1.0), (half, 1.0), (minus_half, -0.5), (mask_incl, 1.0),
                             (far_below, 0.0), (neg_tri, -1.0), (neg_ones, -1.0), (z_max, Z_MAX)):
                nc.gpsimd.memset(t[:], value).then_inc(consts0, 1)
            pool.wait_ge(consts0, 9)

            def select(t, op, fill, base, step, per_partition):
                nc.gpsimd.affine_select(out=t, in_=t, compare_op=op, fill=fill, base=base, pattern=[[step, t.shape[1]]],
                                        channel_multiplier=per_partition).then_inc(consts, 1)

            select(ident[:], ALU.not_equal, 1.0, 0, -1, 1)
            select(half[:, 0:1], ALU.is_ge, 0.0, HD - 1, 0, -1)
            select(half[:, 1:2], ALU.is_ge, 0.0, -HD, 0, 1)
            select(mask_incl[:], ALU.is_ge, 0.0, 0, 1, -1)
            select(far_below[:], ALU.is_ge, FAR_BELOW, -1, 1, -1)
            select(neg_tri[:], ALU.is_ge, 0.0, 0, -1, 1)

            for b in range(RING):
                weights_lo(b, b)
            rstd(NORM_MEM, MT)
            weights_lo_for(MEMK, INV - MEMK)
            rstd(NORM_MIX)
            weights_lo_for(INV, INP - INV)
            pool.wait_ge(v_var, ST)
            nc.gpsimd.tensor_tensor(tiny[:, 0, 0:ST], tiny[:, 1, 0:ST], minus_half[:, 0:ST], ALU.pow).then_inc(v_rstd, 1)
            weights_lo_for(INP, WQ - INP)
            rstd(NORM_XATTN)
            weights_lo_for(WQ, FFN1 - WQ)
            rstd(NORM_FFN)
            weights_lo_for(FFN1, FFN_BLOCKS)
            rstd(NORM_FINAL)
            rstd(NORM_ONE)
            weights_lo_for(GLU, QK - GLU)
            for t in range(8):
                pool.wait_ge(blocks_done, QK + t + 1)
                weights_lo(QK + t + RING, t % RING)
                pool.wait_ge(qk_var, t + 1)
                nc.gpsimd.tensor_tensor(tiny[:, 2 + t % 2, :], tiny[:, t % 2, :], minus_half[:], ALU.pow).then_inc(qk_rstd, 1)
            pool.wait_ge(ln_var, 1)
            nc.gpsimd.tensor_tensor(rcol[:, 7, :], var[:, 4:8], minus_half[:, 0:ST], ALU.pow).then_inc(ln_rstd, 1)
            weights_lo_for(WOUT2, FFN2 - WOUT2)
            rstd(NORM_TWO)
            weights_lo_for(FFN2, FFN_BLOCKS)

        @block.scalar
        def _(act):
            own = Count()
            act.dma_start(cols[:], a_cols).then_inc(loaded_cols, 16)
            act.dma_start(h[:, 0:4, :], a_x[:, 0:4, :]).then_inc(loaded_x0, 16)
            act.dma_start(h[:, 4:8, :], a_x[:, 4:8, :]).then_inc(loaded_x1, 16)
            act.dma_start(mats, a_mats).then_inc(loaded_mats, 16)
            act.dma_start(corr[:], a_corr).then_inc(loaded_mats, 16)

            def weights_hi(b, s, use):
                if b >= RING:
                    act.wait_ge(blocks_done, b + 1 - RING)
                act.wait_ge(w_loaded[s], 16 * (use + 1))
                nc.scalar.activation(w_hi[:, s, :], w_raw[:, s, :], ACT.Copy).then_inc(w_hi_ready, 1)

            def weights_hi_for(b):
                b += RING
                if b < BLOCKS:
                    weights_hi(b, b % RING, b // RING)

            def weights_hi_loop(i, first, s):
                act.wait_ge(blocks_done, i * RING + (first + s + 1))
                act.wait_ge(w_loaded[s], i * 16 + 16 * (first // RING + 2))
                nc.scalar.activation(w_hi[:, s, :], w_raw[:, s, :], ACT.Copy).then_inc(w_hi_ready, 1)

            def weights_hi_run(first, n):
                n = min(n, BLOCKS - RING - first)
                if n > 0:
                    with act.Fori(0, n // RING) as i:
                        for s in range(RING):
                            weights_hi_loop(i, first, s)

            def square(src, gain, n):
                if n >= 2:
                    act.wait_ge(sq_added, n - 1)
                nc.scalar.activation(sq[:, n % 2, 0:src.shape[1]], src, ACT.Square, scale=gain).then_inc(sq_ready, 1)

            def split_gain(dst, src, gain):
                nc.scalar.activation(dst, src, ACT.Copy, scale=gain).then_inc(tile_hi, 1)

            def residual(first, norm, gain):
                for m in range(DT):
                    act.wait_ge(banks_freed, first + m + 1 - USE_LAG)
                    split_gain(xg_hi[:, m, :], h[:, m, :], gain(m))
                    if norm == NORM_FINAL:
                        square(h[:, m, :], 1.0, SQ0[norm] + 2 * m)
                        square(h[:, m, :], col("final_norm_g", m), SQ0[norm] + 2 * m + 1)
                    else:
                        square(h[:, m, :], 1.0, SQ0[norm] + m)
                    weights_hi_for(first + m)

            def ffn(first, both):
                nc.scalar.preload_act_table_set("silu_and_others")
                w, b, n_w = ("conv_w", "conv_b", 2 * FT) if both else ("ffn_dw_w_2", "ffn_dw_b_2", FT)
                f0, y0, s0 = (0, Y_F1, 0) if both else (FT, Y_F2, 2 * FT)
                p0 = 0 if both else 2 * FT
                for first_b, n, pair0, down in ffn_plan(first):
                    with act.Fori(0, n // 2) as i:
                        for j in range(2):
                            s, pair = 2 * j, i * 2 + (pair0 + j)
                            for v in range(2 if both else 1):
                                act.wait_ge(f_scaled, pair * 2 + (s0 + v + 1))
                                nc.scalar.activation(acc[:, s + v, :], ps[:, s + v, :], ACT.Identity,
                                                     scale=col(w, pair + (2 * n_w + v * FT)),
                                                     bias=col(b, pair + v * FT)).then_inc(f_base, 1)
                            weights_hi_loop(i, first_b, s)
                            act.wait_ge(banks_freed, i * RING + (first_b + s + 1 - USE_LAG))
                            nc.scalar.activation(acc[:, s, :], acc[:, s, :], ACT.Silu).then_inc(f_silu, 1)
                            act.wait_ge(f_prod, pair + (f0 + 1))
                            nc.scalar.activation(y_hi[:, bass.ds(i * 2 + j, 1), :].rearrange("p a t -> p (a t)"),
                                                 prod[:, j, :], ACT.Copy).then_inc(y_hi_ready, 1)
                            weights_hi_loop(i, first_b, s + 1)
                    if down != ffn_plan(first)[-1][3] or not both:
                        weights_hi_run(down, DT)

            weights_hi(0, 0, 0)
            act.wait_ge(loaded_cols, 16)
            act.wait_ge(loaded_mem, 16)
            for m in range(DT):
                split_gain(memg_hi[:, m, :], mem[:, m, :], col("mem_norm_g", m))
                square(mem[:, m, :], 1.0, SQ0[NORM_MEM] + m)
            for b in range(1, RING):
                weights_hi(b, b, 0)
            for m in range(DT):
                if m in (0, 4):
                    act.wait_ge((loaded_x0, loaded_x1)[m // 4], 16)
                split_gain(xg_hi[:, m, :], h[:, m, :], col("norm_mix_g", m))
                square(h[:, m, :], 1.0, SQ0[NORM_MIX] + m)
                weights_hi_for(MEMK + m)
            weights_hi_run(MEMV, INP - MEMV)

            nc.scalar.preload_act_table_set("gelu_and_others")
            for t in range(ST):
                act.wait_ge(v_scaled, t + 1)
                nc.scalar.activation(vtok[:, t, :], vtok[:, t, :], ACT.Gelu).then_inc(v_gelu, 1)
            for b in range(INP, INU):
                weights_hi_for(b)
            for t in range(4):
                act.wait_ge(banks_freed, INU + t + 1 - USE_LAG)
                nc.scalar.activation(u[:, t, :], u[:, t, :], ACT.Gelu).then_inc(u_gelu, 1)
                weights_hi_for(INU + t)
                if t == 0:
                    for g in range(4):
                        act.wait_ge(pool_done, g + 1)
                        nc.scalar.activation(y_hi[:, g, :], ps[:, AUX + g, :], ACT.Copy,
                                             scale=col("pool_scale", g)).then_inc(y_hi_ready, 1)
            for g in range(4):
                act.wait_ge(sgu_prod, 2 * g + 2)
                nc.scalar.activation(y_hi[:, 4 + g, :], u[:, g, :], ACT.Copy).then_inc(y_hi_ready, 1)
            residual(WOUT, NORM_XATTN, lambda m: col("norm_xattn_g", m))

            def x_softmax(hd):
                act.wait_ge(x_top, hd + 1)
                for t in range(ST):
                    nc.scalar.activation(probs[:, hd % 2, t, :], ps[:, X_SCORES[hd % 2] + t // 2, (t % 2) * MEM:(t % 2 + 1) * MEM],
                                         ACT.Exp, bias=top[:, hd, t:t + 1], scale=MEM ** -0.5,
                                         accum_out=rsum[:, hd, t:t + 1]).then_inc(x_exp, 1)

            def x_result(hd):
                for d in range(2):
                    act.wait_ge(x_out, 2 * hd + d + 1)
                    nc.scalar.activation(y_hi[:, 2 * hd + d, :], ps[:, X_VALUES + d, :], ACT.Copy).then_inc(y_hi_ready, 1)

            nc.scalar.preload_act_table_set("natural_log_exp_and_others")
            for b in range(4):
                weights_hi_for(WQ + b)
            x_softmax(0)
            weights_hi_for(WQ + 4)
            weights_hi_for(WQ + 5)
            x_softmax(1)
            x_result(0)
            weights_hi_for(WQ + 6)
            weights_hi_for(WQ + 7)
            for hd in range(1, XH):
                if hd + 1 < XH:
                    x_softmax(hd + 1)
                x_result(hd)
            residual(WO, NORM_FFN, lambda m: col("norm_ffn_g", m))
            ffn(FFN1, True)
            act.wait_ge(gain_ready, 1)
            residual(ffn_plan(FFN1)[-1][3], NORM_FINAL, lambda m: gain_12[:, m:m + 1])

            nc.scalar.preload_act_table_set("sigmoid_and_others")
            for i in range(4):
                act.wait_ge(banks_freed, GLU + 2 * i + 2 - USE_LAG)
                nc.scalar.activation(k2[:, i, :], k2[:, i, :], ACT.Sigmoid).then_inc(glu_sig, 1)
                weights_hi_for(GLU + 2 * i)
                weights_hi_for(GLU + 2 * i + 1)
                act.wait_ge(glu_done, i + 1)
                nc.scalar.activation(conv[:, i, :], conv_in[:, i, :], ACT.Identity,
                                     scale=col("conv_dw_w_2", (TAPS - 1) * 4 + i),
                                     bias=col("conv_dw_b_2", i)).then_inc(conv_init, 1)
            for b in range(V2, QK):
                weights_hi_for(b)
            nc.scalar.preload_act_table_set("natural_log_exp_and_others")

            def s_logs(hd):
                t = stick[:, hd % 3, :]
                act.wait_ge(s_z, hd + 1)
                if hd >= 3:
                    act.wait_ge(s_out, hd - 2)
                nc.scalar.activation(t, z_of(hd), ACT.Relu, scale=-1.0, bias=z_max[:]).then_inc(s_min, 1)
                act.wait_ge(s_min, hd + 1)
                nc.scalar.activation(t, t, ACT.Exp, scale=-1.0, bias=z_max[:]).then_inc(s_exp, 1)
                act.wait_ge(s_exp, hd + 1)
                nc.scalar.activation(t, t, ACT.Ln, bias=1.0).then_inc(s_log, 1)

            act.wait_ge(consts0, 9)
            for t in range(8):
                act.wait_ge(banks_freed, QK + t + 1 - USE_LAG)
                if t >= 2:
                    act.wait_ge(qk_sums, t - 1)
                nc.scalar.activation(sq[:, t % 2, :], (q2, k2)[t % 2][:, t // 2, :], ACT.Square).then_inc(qk_square, 1)
                weights_hi_for(QK + t)
                if t == 5:
                    s_logs(0)
            for hd in range(HEADS):
                if hd + 1 < HEADS:
                    s_logs(hd + 1)
                if hd == 4:
                    for i in range(4):
                        act.wait_ge(ln_xc, i + 1)
                        if i >= 2:
                            act.wait_ge(ln_sq, i - 1)
                        nc.scalar.activation(sq[:, i % 2, :], conv[:, i, :], ACT.Square).then_inc(ln_square, 1)
                if hd == 7:
                    nc.scalar.preload_act_table_set("silu_and_others")
                    for i in range(4):
                        act.wait_ge(ln_norm, i + 1)
                        nc.scalar.activation(conv[:, i, :], conv[:, i, :], ACT.Silu, scale=col("conv_ln_g_2", i),
                                             bias=col("conv_ln_b_2", i)).then_inc(ln_silu, 1)
                    nc.scalar.preload_act_table_set("natural_log_exp_and_others")
                act.wait_ge(s_cum, hd + 1)
                nc.scalar.activation(stick[:, hd % 3, :], z_of(hd), ACT.Exp).then_inc(s_att, 1)
                if hd % 2 == 0 and hd >= 2:
                    act.wait_ge(s_out, hd)
                    nc.scalar.activation(y_hi[:, hd // 2 - 1, :], ps[:, 6, :], ACT.Copy).then_inc(y_hi_ready, 1)
            for i in range(4):
                act.wait_ge(ln_silu, i + 1)
                nc.scalar.activation(y_hi[:, 4 + i, :], conv[:, i, :], ACT.Copy).then_inc(y_hi_ready, 1)
            act.wait_ge(s_out, HEADS)
            nc.scalar.activation(y_hi[:, 3, :], ps[:, 6, :], ACT.Copy).then_inc(y_hi_ready, 1)
            residual(WOUT2, NORM_TWO, lambda m: col("norm2_g_2", m))
            ffn(FFN2, False)

        @block.vector
        def _(dve):
            own = Count()

            def multiply_by_rstd(out, b, bank, width=SEQ):
                dve.wait_ge(blocks_done, b + 1)
                return nc.vector.tensor_tensor(out, ps[:, bank, 0:width], rstd_bc[:, 0:width], ALU.mult)

            def add_squares(n, which, first, width=SEQ):
                dve.wait_ge(sq_ready, n + 1)
                dst = ssq[:, which, 0:width]
                if first:
                    nc.vector.tensor_copy(dst, sq[:, n % 2, 0:width]).then_inc(sq_added, 1)
                else:
                    dve.wait_ge(sq_added, n)
                    nc.vector.tensor_tensor(dst, dst, sq[:, n % 2, 0:width], ALU.add).then_inc(sq_added, 1)

            def split_gain_lo(n, dst, src, gain, hi):
                dve.wait_ge(tile_hi, n + 1)
                nc.vector.scalar_tensor_tensor(out=dst, in0=src, scalar=gain, in1=hi.bitcast(F32), op0=ALU.mult,
                                               op1=ALU.subtract).then_inc(tile_lo, 1)

            def split_lo(dst, src, hi, n):
                dve.wait_ge(y_hi_ready, n + 1)
                nc.vector.tensor_tensor(dst, src, hi.bitcast(F32), ALU.subtract).then_inc(y_lo_ready, 1)

            def variance(n, count, sizes=ST, sums=None):
                dve.wait_ge(sums_ready, n + 1 if n <= NORM_FINAL else n)
                nc.vector.tensor_scalar(var[:, 0:sizes], ps[:, AUX, 0:sizes], 1.0 / count, EPS, ALU.mult,
                                        ALU.add).then_inc(var_ready, 1)

            def spread(n, wides, sizes=ST, dst=None):
                dve.wait_ge(rcol_ready, n + 1)
                nc.vector.tensor_copy(wide[:, 0:sizes, :], rcol[:, n, 0:sizes].rearrange("p (a b) -> p a b", b=1)
                                      .broadcast_to([P, sizes, P])).then_inc(wide_ready, 1)
                dve.wait_ge(spread_ready, wides)
                nc.vector.tensor_copy(rstd_bc[:, 0:sizes * P], ps[:, AUX + 1, 0:sizes * P]).then_inc(vstep, 1)
                own.tick()
                dve.wait_ge(vstep, own.now())

            def residual(first, norm, gain):
                for m in range(DT):
                    dve.wait_ge(blocks_done, first + m + 1)
                    nc.vector.tensor_tensor(h[:, m, :], ps[:, m % RING, :], h[:, m, :], ALU.add).then_inc(banks_freed, 1)
                    n = TILE0[NORM_ONE if norm == NORM_FINAL else norm] + m
                    split_gain_lo(n, xg_lo[:, m, :], h[:, m, :], gain(m), xg_hi[:, m, :])
                    if norm == NORM_FINAL:
                        add_squares(SQ0[norm] + 2 * m, 0, m == 0)
                        add_squares(SQ0[norm] + 2 * m + 1, 1, m == 0)
                    else:
                        add_squares(SQ0[norm] + m, 0, m == 0)

            def ffn(first, both):
                w, n_w = ("conv_w", 2 * FT) if both else ("ffn_dw_w_2", FT)
                f0, y0, s0, c0 = (0, Y_F1, 0, 0) if both else (FT, Y_F2, 2 * FT, 2 * FT)
                for first_b, n, pair0, down in ffn_plan(first):
                    with dve.Fori(0, n // 2) as i:
                        own.enter(i, 4 if both else 2)
                        for j in range(2):
                            s, pair = 2 * j, i * 2 + (pair0 + j)
                            b = i * RING + (first_b + s)
                            for v in range(2):
                                multiply_by_rstd(ps[:, s + v, :], b + v, s + v).then_inc(f_scaled, 1)
                            convolved = range(2 if both else 1)
                            for v in convolved:
                                dve.wait_ge(f_base, (pair * 2 if both else pair) + (c0 + v + 1))
                                nc.vector.scalar_tensor_tensor(out=acc[:, s + v, 1:], in0=ps[:, s + v, 0:SEQ - 1],
                                                               scalar=col(w, pair + (n_w + v * FT)),
                                                               in1=acc[:, s + v, 1:], op0=ALU.mult, op1=ALU.add).then_inc(vstep, 1)
                                own.tick()
                            for v in convolved:
                                dve.wait_ge(vstep, own.now() - (convolved[-1] - v))
                                nc.vector.scalar_tensor_tensor(out=acc[:, s + v, 2:], in0=ps[:, s + v, 0:SEQ - 2],
                                                               scalar=col(w, pair + v * FT),
                                                               in1=acc[:, s + v, 2:], op0=ALU.mult, op1=ALU.add).then_inc(banks_freed, 1)
                            dve.wait_ge(f_silu, pair + (f0 + 1))
                            if both:
                                dve.wait_ge(banks_freed, b + (2 - USE_LAG))
                                nc.vector.tensor_tensor(prod[:, j, :], acc[:, s, :], acc[:, s + 1, :], ALU.mult).then_inc(f_prod, 1)
                            else:
                                dve.wait_ge(f_scaled, pair * 2 + (s0 + 2))
                                nc.vector.tensor_tensor(prod[:, j, :], ps[:, s + 1, :], acc[:, s, :], ALU.mult).then_inc(f_prod, 1)
                                dve.wait_ge(f_prod, pair + (f0 + 1))
                                nc.vector.memset(tiny[:, 3, 0:1], 0.0).then_inc(banks_freed, 1)
                            y = y_lo[:, bass.ds(i * 2 + j, 1), :].rearrange("p a t -> p (a t)")
                            yh = y_hi[:, bass.ds(i * 2 + j, 1), :].rearrange("p a t -> p (a t)")
                            dve.wait_ge(f_prod, pair + (f0 + 1))
                            split_lo(y, prod[:, j, :], yh, pair + y0)
                            if not both:
                                pass
                        if both:
                            own.leave(n // 2)
                        else:
                            own.leave(n // 2)
                    if down != ffn_plan(first)[-1][3]:
                        for m in range(DT):
                            dve.wait_ge(blocks_done, down + m + 1)
                            nc.vector.tensor_tensor(h[:, m, :], ps[:, m % RING, :], h[:, m, :], ALU.add).then_inc(banks_freed, 1)

            nc.vector.memset(slab[:, 16 * SEQ:16 * SEQ + 6 * WP], 0.0).then_inc(vstep, 1)
            own.tick()
            dve.wait_ge(loaded_cols, 16)
            nc.vector.tensor_tensor(gain_12[:], cols[:, COLS["final_norm_g"]:COLS["final_norm_g"] + DT],
                                    cols[:, COLS["norm1_g_2"]:COLS["norm1_g_2"] + DT], ALU.mult).then_inc(gain_ready, 1)
            dve.wait_ge(loaded_mem, 16)
            for m in range(DT):
                split_gain_lo(TILE0[NORM_MEM] + m, memg_lo[:, m, :], mem[:, m, :], col("mem_norm_g", m), memg_hi[:, m, :])
                add_squares(SQ0[NORM_MEM] + m, 0, m == 0, MEM)
            variance(NORM_MEM, D, MT)
            spread(NORM_MEM, 1, MT)
            for m in range(DT):
                if m in (0, 4):
                    dve.wait_ge((loaded_x0, loaded_x1)[m // 4], 16)
                split_gain_lo(TILE0[NORM_MIX] + m, xg_lo[:, m, :], h[:, m, :], col("norm_mix_g", m), xg_hi[:, m, :])
                add_squares(SQ0[NORM_MIX] + m, 1, m == 0)
                multiply_by_rstd(k1[:, m, :], MEMK + m, m % RING, MEM).then_inc(banks_freed, 1)
            for half_ in range(2):
                dve.wait_ge(blocks_done, MEMV + 4 * half_ + 4)
                for t in range(MT):
                    nc.vector.tensor_scalar(v1[:, t, half_ * SEQ:(half_ + 1) * SEQ], ps[:, 2 * half_ + t, :],
                                            rcol[:, NORM_MEM, t:t + 1], None, ALU.mult).then_inc(banks_freed, 1)
                if half_ == 0:
                    dve.wait_ge(loaded_mats, 32)
                    dve.wait_ge(consts, 6)
                    nc.vector.tensor_copy(ident_r[:], ident[:]).then_inc(rounded, 1)
                    nc.vector.tensor_copy(far_below_r[:], far_below[:]).then_inc(rounded, 1)
                    nc.vector.tensor_tensor(sgu_w, sgu_w, mask_incl[:].rearrange("p (a t) -> p a t", a=1)
                                            .broadcast_to([P, 4, P]), ALU.mult).then_inc(sgu_masked, 1)
            variance(NORM_MIX, D)
            spread(NORM_MIX, 2)

            dve.wait_ge(blocks_done, INV + 4)
            for t in range(ST):
                nc.vector.tensor_scalar(vtok[:, t, :], ps[:, t, :], rcol[:, NORM_MIX, t:t + 1], None,
                                        ALU.mult).then_inc(v_scaled, 1)
            dve.wait_ge(v_scaled, ST)
            for t in range(ST):
                nc.vector.memset(tiny[:, 3, t:t + 1], 0.0).then_inc(banks_freed, 1)
            for t in range(ST):
                dve.wait_ge(v_gelu, t + 1)
                nc.vector.bn_stats(bn[:, t, :], vtok[:, t, :]).then_inc(vstep, 1)
                own.tick()
            for t in range(ST):
                dve.wait_ge(vstep, own.now() - (ST - 1 - t) if t == 0 else own.now() - (ST - 1))
                nc.vector.bn_aggr(bna[:, t, :], bn[:, t, :]).then_inc(vstep, 1)
                own.tick()
            dve.wait_ge(vstep, own.now())
            for t in range(ST):
                nc.vector.tensor_scalar(tiny[:, 1, t:t + 1], bna[:, t, 1:2], EPS, None, ALU.add).then_inc(v_var, 1)

            def pool_windows(g):
                multiply_by_rstd(pp[:, g, PAD:], INP + g, g).then_inc(banks_freed, 1)
                dve.wait_ge(banks_freed, INP + g + 1 - USE_LAG)
                src, step, at = pp[:, g, :], 1, 0
                while step < POOL_WINDOWS[g]:
                    dst = win[:, at, :]
                    nc.vector.tensor_tensor(dst[:, step:], src[:, step:], src[:, 0:WP - step], ALU.add).then_inc(vstep, 1)
                    own.tick()
                    dve.wait_ge(vstep, own.now())
                    src, step, at = dst, 2 * step, 1 - at
                nc.vector.tensor_tensor(src[:, PAD:2 * PAD], src[:, PAD:2 * PAD], corr[:, g, :], ALU.mult).then_inc(vstep, 1)
                own.tick()
                dve.wait_ge(vstep, own.now())
                nc.vector.scalar_tensor_tensor(out=pp[:, g, PAD:], in0=src[:, PAD:], scalar=1.0 / POOL_WINDOWS[g],
                                               in1=pp[:, g, PAD:], op0=ALU.mult, op1=ALU.subtract).then_inc(pooled, 1)
                dve.wait_ge(pooled, g + 1)

            pool_windows(0)
            dve.wait_ge(v_rstd, 1)
            for t in range(ST):
                nc.vector.tensor_scalar(vtok[:, t, :], vtok[:, t, :], bna[:, t, 0:1], tiny[:, 0, t:t + 1], ALU.subtract,
                                        ALU.mult).then_inc(vstep, 1)
                own.tick()
            for t in range(ST):
                dve.wait_ge(vstep, own.now() - (ST - 1 - t))
                nc.vector.tensor_tensor(vtok[:, t, :], vtok[:, t, :], sgu_g, ALU.mult).then_inc(vn_ready, 1)
            for g in range(1, 4):
                pool_windows(g)
            for t in range(4):
                multiply_by_rstd(u[:, t, :], INU + t, t).then_inc(banks_freed, 1)
                if t == 0:
                    for g in range(4):
                        dve.wait_ge(y_hi_ready, Y_MIX + g + 1)
                        nc.vector.scalar_tensor_tensor(out=y_lo[:, g, :], in0=ps[:, AUX + g, :], scalar=col("pool_scale", g),
                                                       in1=y_hi[:, g, :].bitcast(F32), op0=ALU.mult,
                                                       op1=ALU.subtract).then_inc(y_lo_ready, 1)
            for g in range(4):
                dve.wait_ge(z_done, g + 1)
                z = ps[:, AUX + g, :].rearrange("p (c t) -> p c t", t=P)
                nc.vector.tensor_tensor(z, z, sgu_b[:, g:g + 1, :].broadcast_to([P, ST, P]), ALU.add).then_inc(sgu_prod, 1)
                dve.wait_ge(sgu_prod, 2 * g + 1)
                dve.wait_ge(u_gelu, g + 1)
                nc.vector.tensor_tensor(u[:, g, :], ps[:, AUX + g, :], u[:, g, :], ALU.mult).then_inc(sgu_prod, 1)
                dve.wait_ge(sgu_prod, 2 * g + 2)
                split_lo(y_lo[:, 4 + g, :], u[:, g, :], y_hi[:, 4 + g, :], Y_MIX + 4 + g)
            residual(WOUT, NORM_XATTN, lambda m: col("norm_xattn_g", m))

            def x_max(hd):
                for b in range(2):
                    dve.wait_ge(x_scores, 2 * hd + b + 1)
                    nc.vector.tensor_reduce(top[:, hd, 2 * b:2 * b + 2], ps[:, X_SCORES[hd % 2] + b, :].rearrange("p (a m) -> p a m", m=MEM),
                                            AX.X, ALU.max).then_inc(vstep, 1)
                    own.tick()
                dve.wait_ge(vstep, own.now())
                nc.vector.tensor_scalar(top[:, hd, :], top[:, hd, :], -(MEM ** -0.5), None, ALU.mult).then_inc(x_top, 1)

            def x_normalise(hd):
                dve.wait_ge(x_exp, ST * (hd + 1))
                nc.vector.reciprocal(rsum[:, hd, :], rsum[:, hd, :]).then_inc(vstep, 1)
                own.tick()
                dve.wait_ge(vstep, own.now())
                for t in range(ST):
                    nc.vector.tensor_scalar(probs[:, hd % 2, t, :], probs[:, hd % 2, t, :], rsum[:, hd, t:t + 1], None,
                                            ALU.mult).then_inc(x_probs, 1)

            def x_turn(hd):
                for m in range(MT):
                    dve.wait_ge(x_turned, 2 * hd + m + 1)
                    nc.vector.tensor_copy(probs_t[:, m, :], ps[:, X_VALUES + m, :]).then_inc(x_copied, 1)

            def x_lo(hd):
                for d in range(2):
                    t = 2 * hd + d
                    split_lo(y_lo[:, t, :], ps[:, X_VALUES + d, :], y_hi[:, t, :], Y_X + t)

            variance(NORM_XATTN, D)
            spread(NORM_XATTN, 3)

            def x_query(m):
                multiply_by_rstd(q1[:, m, :], WQ + m, m if m < 4 else m % 2).then_inc(banks_freed, 1)

            for m in range(4):
                x_query(m)
            x_max(0)
            x_query(4)
            x_query(5)
            x_max(1)
            for hd in range(XH):
                x_normalise(hd)
                x_turn(hd)
                x_lo(hd)
                if hd == 0:
                    x_query(6)
                    x_query(7)
                if hd + 2 < XH:
                    x_max(hd + 2)
            residual(WO, NORM_FFN, lambda m: col("norm_ffn_g", m))
            variance(NORM_FFN, D)
            spread(NORM_FFN, 4)
            ffn(FFN1, True)
            residual(ffn_plan(FFN1)[-1][3], NORM_FINAL, lambda m: gain_12[:, m:m + 1])

            variance(NORM_FINAL, D)
            dve.wait_ge(rcol_ready, NORM_FINAL + 1)
            nc.vector.tensor_tensor(tiny[:, 0, 0:ST], rcol[:, NORM_FINAL, :], rcol[:, NORM_FINAL, :], ALU.mult).then_inc(vstep, 1)
            own.tick()
            dve.wait_ge(vstep, own.now())
            nc.vector.tensor_tensor(tiny[:, 0, 0:ST], ps[:, AUX, ST:2 * ST], tiny[:, 0, 0:ST], ALU.mult).then_inc(vstep, 1)
            own.tick()
            dve.wait_ge(vstep, own.now())
            nc.vector.tensor_scalar(var[:, 0:ST], tiny[:, 0, 0:ST], 1.0 / D, EPS, ALU.mult, ALU.add).then_inc(var_ready, 1)
            dve.wait_ge(rcol_ready, NORM_ONE + 1)
            nc.vector.tensor_tensor(rcol[:, NORM_ONE, :], rcol[:, NORM_ONE, :], rcol[:, NORM_FINAL, :], ALU.mult).then_inc(vstep, 1)
            own.tick()
            dve.wait_ge(vstep, own.now())
            spread(NORM_ONE, 5)

            def final_norm():
                nc.vector.tensor_copy(wide[:], rcol[:, NORM_FINAL, :].rearrange("p (a b) -> p a b", b=1)
                                      .broadcast_to([P, ST, P])).then_inc(wide_ready, 1)
                dve.wait_ge(spread_ready, 6)
                nc.vector.tensor_copy(ssq[:, 0, :], ps[:, AUX + 1, :]).then_inc(vstep, 1)
                own.tick()
                dve.wait_ge(vstep, own.now())
                for m in range(DT):
                    nc.vector.scalar_tensor_tensor(out=h[:, m, :], in0=h[:, m, :], scalar=col("final_norm_g", m),
                                                   in1=ssq[:, 0, :], op0=ALU.mult, op1=ALU.mult).then_inc(vstep, 1)
                    own.tick()

            tap_order = [(i0 + i, j) for i0 in (0, 2) for j in range(1, TAPS) for i in range(2)]
            taps_done = Count()

            def conv_taps(n):
                for _ in range(n):
                    if not tap_order:
                        return
                    i, j = tap_order.pop(0)
                    if j == 1:
                        dve.wait_ge(conv_init, i + 1)
                    else:
                        dve.wait_ge(ln_sum, taps_done.now() - 1)
                    nc.vector.scalar_tensor_tensor(out=conv[:, i, j:], in0=conv_in[:, i, 0:SEQ - j],
                                                   scalar=col("conv_dw_w_2", (TAPS - 1 - j) * 4 + i),
                                                   in1=conv[:, i, j:], op0=ALU.mult, op1=ALU.add).then_inc(ln_sum, 1)
                    taps_done.tick()

            for i in range(4):
                multiply_by_rstd(q2[:, i, :], GLU + 2 * i, (2 * i) % RING).then_inc(banks_freed, 1)
                multiply_by_rstd(k2[:, i, :], GLU + 2 * i + 1, (2 * i + 1) % RING).then_inc(banks_freed, 1)
                dve.wait_ge(banks_freed, GLU + 2 * i + 2 - USE_LAG)
                dve.wait_ge(glu_sig, i + 1)
                nc.vector.tensor_tensor(conv_in[:, i, :], q2[:, i, :], k2[:, i, :], ALU.mult).then_inc(glu_done, 1)
                if i == 0:
                    final_norm()
                else:
                    conv_taps((0, 10, 12, 12)[i])
            conv_taps(22)
            dve.wait_ge(blocks_done, V2 + 4)
            for t in range(ST):
                nc.vector.tensor_scalar(v2[:, t, :], ps[:, t, :], rcol[:, NORM_ONE, t:t + 1], None, ALU.mult).then_inc(banks_freed, 1)

            def qk_square_sums(t):
                dve.wait_ge(qk_sums, t + 1)
                if t >= 2:
                    dve.wait_ge(qk_rstd, t - 1)
                nc.vector.tensor_scalar(tiny[:, t % 2, :], ps[:, AUX, 0:8], 1.0 / HD, EPS, ALU.mult, ALU.add).then_inc(qk_var, 1)

            def qk_scale(t):
                dve.wait_ge(qk_rstd, t + 1)
                nc.vector.tensor_scalar(wide[:].rearrange("p a (b c) -> p (a b) c", b=2),
                                        tiny[:, 2 + t % 2, :].rearrange("p (a b) -> p a b", b=1).broadcast_to([P, 8, HD]),
                                        HD ** -0.5 if t % 2 == 0 else 1.0, None, ALU.mult).then_inc(qk_wide, 1)

            def qk_apply(t):
                dst = (q2, k2)[t % 2][:, t // 2, :]
                dve.wait_ge(qk_spread, t + 1)
                nc.vector.scalar_tensor_tensor(out=dst, in0=dst, scalar=col(("q_norm_g_2", "k_norm_g_2")[t % 2], 0),
                                               in1=ps[:, AUX + 1, :], op0=ALU.mult, op1=ALU.mult).then_inc(qk_ready, 1)

            AT = (0, 512, 1024, 896)

            def s_softplus(hd):
                t = stick[:, hd % 3, :]
                dve.wait_ge(s_log, hd + 1)
                nc.vector.tensor_tensor(t, z_of(hd), t, ALU.max).then_inc(vstep, 1)
                own.tick()
                dve.wait_ge(vstep, own.now())
                later = later_sums[:, hd % 2, :]
                if hd >= 2:
                    dve.wait_ge(s_cum, hd - 1)
                for dst, a, b in ((later[:, 0:P], t[:, AT[2] + P:AT[2] + 2 * P], t[:, AT[3]:AT[3] + P]),
                                  (later[:, P:2 * P], t[:, AT[1] + P:AT[1] + 2 * P], t[:, AT[2]:AT[2] + P])):
                    nc.vector.tensor_tensor(dst, a, b, ALU.add).then_inc(vstep, 1)
                    own.tick()
                dve.wait_ge(vstep, own.now())
                nc.vector.tensor_tensor(later[:, 2 * P:3 * P], t[:, AT[1] + 2 * P:AT[1] + 3 * P], later[:, 0:P],
                                        ALU.add).then_inc(s_sp, 1)

            for t in range(8 + 2):
                if t < 8:
                    multiply_by_rstd((q2, k2)[t % 2][:, t // 2, :], QK + t, 6 + t % 2).then_inc(banks_freed, 1)
                if t >= 2:
                    qk_apply(t - 2)
                if 1 <= t <= 8:
                    qk_square_sums(t - 1)
                    conv_taps(4)
                    qk_scale(t - 1)
                if t == 7:
                    s_softplus(0)

            def ln_mean_sum():
                assert not tap_order
                dve.wait_ge(ln_sum, taps_done.now())
                nc.vector.tensor_tensor(ssq[:, 0, :], conv[:, 0, :], conv[:, 1, :], ALU.add).then_inc(vstep, 1)
                nc.vector.tensor_tensor(ssq[:, 1, :], conv[:, 2, :], conv[:, 3, :], ALU.add).then_inc(vstep, 1)
                own.tick()
                own.tick()
                dve.wait_ge(vstep, own.now())
                nc.vector.tensor_tensor(ssq[:, 0, :], ssq[:, 0, :], ssq[:, 1, :], ALU.add).then_inc(ln_col, 1)

            def ln_mean():
                dve.wait_ge(ln_sums, 1)
                nc.vector.tensor_scalar(wide[:], ps[:, 7, 0:ST].rearrange("p (a b) -> p a b", b=1).broadcast_to([P, ST, P]),
                                        1.0 / SEQ, None, ALU.mult).then_inc(ln_wide, 1)

            def ln_centre():
                dve.wait_ge(ln_spread, 1)
                for i in range(4):
                    nc.vector.tensor_tensor(conv[:, i, :], ps[:, 7, :], conv[:, i, :], ALU.subtract).then_inc(ln_xc, 1)

            def ln_square_sum():
                for i in range(4):
                    dve.wait_ge(ln_square, i + 1)
                    if i == 0:
                        nc.vector.tensor_copy(ssq[:, 0, :], sq[:, i % 2, :]).then_inc(ln_sq, 1)
                    else:
                        dve.wait_ge(ln_sq, i)
                        nc.vector.tensor_tensor(ssq[:, 0, :], ssq[:, 0, :], sq[:, i % 2, :], ALU.add).then_inc(ln_sq, 1)

            def ln_variance():
                dve.wait_ge(ln_sums, 2)
                nc.vector.tensor_scalar(var[:, 4:8], ps[:, 7, 0:ST], 1.0 / SEQ, EPS, ALU.mult, ALU.add).then_inc(ln_var, 1)

            def ln_rstd_wide():
                dve.wait_ge(ln_rstd, 1)
                nc.vector.tensor_scalar(wide[:], rcol[:, 7, :].rearrange("p (a b) -> p a b", b=1).broadcast_to([P, ST, P]),
                                        -1.0, None, ALU.mult).then_inc(ln_wide, 1)

            def ln_apply():
                dve.wait_ge(ln_spread, 2)
                for i in range(4):
                    nc.vector.tensor_tensor(conv[:, i, :], ps[:, 7, :], conv[:, i, :], ALU.mult).then_inc(ln_norm, 1)

            for hd in range(HEADS):
                if hd == 3:
                    ln_mean()
                if hd == 5:
                    ln_variance()
                if hd + 1 < HEADS:
                    s_softplus(hd + 1)
                conv_taps((10, 10, 12, 0, 0, 0, 0, 0)[hd])
                if hd == 4:
                    ln_square_sum()
                if hd % 2 == 0 and hd >= 2:
                    split_lo(y_lo[:, hd // 2 - 1, :], ps[:, 6, :], y_hi[:, hd // 2 - 1, :], Y_MIX2 + hd // 2 - 1)
                if hd == 2:
                    ln_mean_sum()
                if hd == 3:
                    ln_centre()
                if hd == 5:
                    ln_rstd_wide()
                    ln_apply()
            for i in range(4):
                split_lo(y_lo[:, 4 + i, :], conv[:, i, :], y_hi[:, 4 + i, :], Y_MIX2 + 3 + i)
            split_lo(y_lo[:, 3, :], ps[:, 6, :], y_hi[:, 3, :], Y_MIX2 + 7)
            residual(WOUT2, NORM_TWO, lambda m: col("norm2_g_2", m))
            variance(NORM_TWO, D)
            spread(NORM_TWO, 7)
            ffn(FFN2, False)
            down = ffn_plan(FFN2)[-1][3]
            for m in range(DT):
                dve.wait_ge(blocks_done, down + m + 1)
                nc.vector.tensor_tensor(h[:, m, :], ps[:, m % RING, :], h[:, m, :], ALU.add).then_inc(banks_freed, 1)

        @block.tensor
        def _(pe):
            def three(out, w, x, first, last):
                pe.matmul(out, w[0], x[0], start=first, stop=False)
                pe.matmul(out, w[0], x[1], start=False, stop=False)
                return pe.matmul(out, w[1], x[0], start=False, stop=last)

            def features(b, use, s, x, kt=8, width=SEQ, ready=None, bank=None, behind=RING, order=None):
                bank = s if bank is None else bank
                order = order or range(kt)
                pe.wait_ge(w_lo_ready, b + 1)
                if behind and (not isinstance(use, int) or use >= RING):
                    pe.wait_ge(banks_freed, use + 1 - behind)
                for n, k in enumerate(order):
                    if ready is not None:
                        pe.wait_ge(*ready(n))
                    c = slice(k * P, (k + 1) * P)
                    mm = three(ps[:, bank, 0:width], (w_hi[:, s, c], w_lo[:, s, c]),
                               (x[0][:, k, 0:width], x[1][:, k, 0:width]), n == 0, n == kt - 1)
                mm.then_inc(blocks_done, 1)

            def tokens(first, use, x, nt, bank0, ready=None):
                pe.wait_ge(banks_freed, use + 1 - RING + nt - 1)
                for s in range(4):
                    pe.wait_ge(w_lo_ready, first + s + 1)
                    for kk in range(2):
                        k = 2 * s + kk
                        if ready is not None:
                            pe.wait_ge(*ready(k))
                        c = slice(kk * SEQ, (kk + 1) * SEQ)
                        for t in range(nt):
                            tok = slice(t * P, (t + 1) * P)
                            out = ps[:, bank0 + t, :]
                            pe.matmul(out, x[0][:, k, tok], w_hi[:, s, c], start=k == 0, stop=False)
                            pe.matmul(out, x[1][:, k, tok], w_hi[:, s, c], start=False, stop=False)
                            mm = pe.matmul(out, x[0][:, k, tok], w_lo[:, s, c], start=False, stop=k == DT - 1)
                    mm.then_inc(blocks_done, 1)

            def square_sums(added, sizes=ST, which=(0,)):
                pe.wait_ge(sq_added, added)
                for i, w in enumerate(which):
                    for t in range(sizes):
                        mm = pe.matmul(ps[:, AUX, i * ST + t:i * ST + t + 1], ssq[:, w, t * P:(t + 1) * P], ones[:],
                                       start=True, stop=True)
                mm.then_inc(sums_ready, 1)

            def turn_wide(n, sizes=ST):
                pe.wait_ge(wide_ready, n)
                for t in range(sizes):
                    mm = pe.transpose(ps[:, AUX + 1, t * P:(t + 1) * P], wide[:, t, :], ident[:])
                mm.then_inc(spread_ready, 1)

            def tile_ready(norm):
                return lambda k: (tile_lo, TILE0[norm] + k + 1)

            def y_ready(y0):
                return lambda k: (y_lo_ready, y0 + k + 1)

            xg, yy = (xg_hi, xg_lo), (y_hi, y_lo)

            pe.wait_ge(consts, 6)
            for m in range(8):
                features(MEMK + m, m, m % RING, (memg_hi, memg_lo), width=MEM, ready=tile_ready(NORM_MEM) if m == 0 else None)
                if m == 0:
                    square_sums(SQ0[NORM_MEM] + 8, MT)
                if m == 1:
                    turn_wide(1, MT)
            tokens(MEMV, 8, (memg_hi, memg_lo), MT, 0)
            tokens(MEMV + 4, 10, (memg_hi, memg_lo), MT, 2)
            square_sums(SQ0[NORM_MIX] + 8, which=(1,))
            tokens(INV, 12, xg, ST, 0, tile_ready(NORM_MIX))
            turn_wide(2)
            for g in range(4):
                features(INP + g, INP + g - USE_LAG, g, xg)
            for t in range(4):
                features(INU + t, INU + t - USE_LAG, t, xg)
                if t == 0:
                    for g in range(4):
                        pe.wait_ge(pooled, g + 1)
                        pe.matmul(ps[:, AUX + g, :], pool_w[:, g, :], pp[:, g, PAD:], start=True, stop=True).then_inc(pool_done, 1)
            pe.wait_ge(vn_ready, ST)
            pe.wait_ge(sgu_masked, 1)
            for hd in range(4):
                pe.wait_ge(y_lo_ready, Y_MIX + hd + 1)
                for c in range(ST):
                    mm = pe.matmul(ps[:, AUX + hd, c * P:(c + 1) * P], vtok[:, c, hd * P:(hd + 1) * P], sgu_w[:, hd, :],
                                   start=True, stop=True)
                mm.then_inc(z_done, 1)
            for m in range(DT):
                features(WOUT + m, WOUT + m - USE_LAG, m % RING, yy, ready=y_ready(Y_MIX) if m == 0 else None)

            def x_scores_of(hd):
                pe.wait_ge(banks_freed, WQ + 2 * hd + 2 - USE_LAG)
                if hd >= 2:
                    pe.wait_ge(x_exp, ST * (hd - 1))
                for t in range(ST):
                    for d in range(2):
                        mm = pe.matmul(ps[:, X_SCORES[hd % 2] + t // 2, (t % 2) * MEM:(t % 2 + 1) * MEM],
                                       q1[:, 2 * hd + d, t * P:(t + 1) * P], k1[:, 2 * hd + d, :], start=d == 0, stop=d == 1)
                    if t % 2:
                        mm.then_inc(x_scores, 1)

            def x_values(hd):
                if hd == 0:
                    pe.wait_ge(banks_freed, WQ + 4 - USE_LAG)
                else:
                    pe.wait_ge(y_lo_ready, Y_X + 2 * hd)
                pe.wait_ge(x_probs, ST * (hd + 1))
                for m in range(MT):
                    for t in range(ST):
                        mm = pe.transpose(ps[:, X_VALUES + m, t * P:(t + 1) * P], probs[:, hd % 2, t, m * P:(m + 1) * P], ident[:])
                    mm.then_inc(x_turned, 1)
                pe.wait_ge(x_copied, 2 * (hd + 1))
                for d in range(2):
                    for m in range(MT):
                        mm = pe.matmul(ps[:, X_VALUES + d, :], v1[:, m, (2 * hd + d) * P:(2 * hd + d + 1) * P], probs_t[:, m, :],
                                       start=m == 0, stop=m == MT - 1)
                    mm.then_inc(x_out, 1)

            def query(m, ready=None):
                features(WQ + m, WQ + m - USE_LAG, m % RING, xg, ready=ready, bank=m if m < 4 else m % 2,
                         behind=4 if m < 6 else 2)

            query(0, tile_ready(NORM_XATTN))
            square_sums(SQ0[NORM_XATTN] + 8)
            query(1)
            turn_wide(3)
            query(2)
            query(3)
            x_scores_of(0)
            query(4)
            query(5)
            x_scores_of(1)
            x_values(0)
            query(6)
            query(7)
            for hd in range(1, XH):
                if hd + 1 < XH:
                    x_scores_of(hd + 1)
                x_values(hd)
            for m in range(DT):
                features(WO + m, WO + m - USE_LAG, m % RING, yy, ready=y_ready(Y_X) if m == 0 else None)

            def ffn(first, norm, wides, y0):
                for first_b, n, pair0, down in ffn_plan(first):
                    start = 0
                    if pair0 == 0:
                        start = 1
                        for s in range(RING):
                            features(first_b + s, first_b + s - USE_LAG, s, xg, ready=tile_ready(norm) if s == 0 else None)
                            if s == 0:
                                square_sums(SQ0[norm] + 8)
                            if s == 1:
                                turn_wide(wides)
                    with pe.Fori(start, n // 2) as i:
                        for s in range(RING):
                            features(i * RING + (first_b + s), i * RING + (first_b + s - USE_LAG), s, xg)
                    with pe.Fori(0, DT // RING) as i:
                        for s in range(RING):
                            features(i * RING + (down + s), i * RING + (down + s - USE_LAG), s, yy, kt=n,
                                     ready=y_ready(y0 + pair0) if s == 0 else None)

            ffn(FFN1, NORM_FFN, 4, Y_F1)

            features(GLU, GLU - USE_LAG, 0, xg, ready=tile_ready(NORM_ONE))
            square_sums(SQ0[NORM_FINAL] + 16, which=(0, 1))
            features(GLU + 1, GLU + 1 - USE_LAG, 1, xg)
            turn_wide(5)
            for b in range(GLU + 2, V2):
                features(b, b - USE_LAG, b % RING, xg)
                if b == GLU + 4:
                    turn_wide(6)
            tokens(V2, V2 - USE_LAG, xg, ST, 0)

            def qk_sum(t):
                if t >= 1:
                    pe.wait_ge(qk_var, t)
                pe.wait_ge(qk_square, t + 1)
                for c in range(ST):
                    mm = pe.matmul(ps[:, AUX, 2 * c:2 * c + 2], sq[:, t % 2, c * P:(c + 1) * P], half[:], start=True, stop=True)
                mm.then_inc(qk_sums, 1)

            def qk_turn(t):
                if t >= 1:
                    pe.wait_ge(qk_ready, t)
                pe.wait_ge(qk_wide, t + 1)
                for c in range(ST):
                    mm = pe.transpose(ps[:, AUX + 1, c * P:(c + 1) * P], wide[:, c, :], ident[:])
                mm.then_inc(qk_spread, 1)

            TILES = ((0, 0, 512), (1, 0, 384), (2, 0, 256), (1, 384, 128))
            AT = (0, 512, 1024, 896)

            def s_scores(hd):
                if hd == 0:
                    pe.wait_ge(banks_freed, QK - USE_LAG)
                    pe.wait_ge(qk_ready, 2)
                    pe.wait_ge(rounded, 2)
                elif hd == 1:
                    pe.wait_ge(qk_ready, 8)
                else:
                    pe.wait_ge(s_att, hd - 1)
                r = slice(HD * (hd % 2), HD * (hd % 2) + HD)
                for tile in (0, 1, 3, 2):
                    bank, at, n = TILES[tile]
                    pe.matmul(ps[:, 3 * (hd % 2) + bank, at:at + n], k2[r, hd // 2, tile * P:(tile + 1) * P],
                                   q2[r, hd // 2, tile * P:], start=tile != 3, stop=False, skip_group_check=True)
                    mm = pe.matmul(ps[:, 3 * (hd % 2) + bank, at:at + P], ident_r[:], far_below_r[:], start=False, stop=False,
                                   skip_group_check=True)
                mm.then_inc(s_z, 1)

            def s_cumulate(hd):
                t = stick[:, hd % 3, :]
                later = later_sums[:, hd % 2, :]
                pe.wait_ge(s_sp, hd + 1)

                def add(tile, col0, n, w, src):
                    bank, at, _ = TILES[tile]
                    return pe.matmul(ps[:, 3 * (hd % 2) + bank, at + col0:at + col0 + n], w[:], src, start=False, stop=True,
                                     skip_group_check=True)

                for tile in range(ST):
                    add(tile, 0, TILES[tile][2], neg_tri, t[:, AT[tile]:AT[tile] + TILES[tile][2]])
                add(2, P, P, neg_ones, t[:, AT[3]:AT[3] + P])
                add(1, P, P, neg_ones, t[:, AT[2]:AT[2] + P])
                add(1, 2 * P, P, neg_ones, later[:, 0:P])
                add(0, P, P, neg_ones, t[:, AT[1]:AT[1] + P])
                add(0, 2 * P, 2 * P, neg_ones, later[:, P:3 * P]).then_inc(s_cum, 1)

            def s_values(hd):
                t = stick[:, hd % 3, :]
                r = slice(HD * (hd % 2), HD * (hd % 2) + HD)
                if hd % 2 == 0 and hd >= 2:
                    pe.wait_ge(y_lo_ready, Y_MIX2 + hd // 2)
                pe.wait_ge(s_att, hd + 1)
                for tile in range(ST):
                    mm = pe.matmul(ps[r, 6, tile * P:], v2[:, tile, hd * HD:(hd + 1) * HD],
                                   t[:, AT[tile]:AT[tile] + TILES[tile][2]], start=tile == 0, stop=tile == ST - 1,
                                   skip_group_check=True)
                mm.then_inc(s_out, 1)

            def ln_column_sums(n):
                if n == 0:
                    pe.wait_ge(ln_col, 1)
                else:
                    pe.wait_ge(ln_sq, 4)
                for c in range(ST):
                    mm = pe.matmul(ps[:, 7, c:c + 1], ssq[:, 0, c * P:(c + 1) * P], ones[:], start=True, stop=True)
                mm.then_inc(ln_sums, 1)

            def ln_turn(n):
                pe.wait_ge(ln_wide, n + 1)
                for c in range(ST):
                    mm = pe.transpose(ps[:, 7, c * P:(c + 1) * P], wide[:, c, :], ident[:])
                mm.then_inc(ln_spread, 1)

            for t in range(8 + 2):
                if t < 8:
                    features(QK + t, QK + t - USE_LAG, t % RING, xg, bank=6 + t % 2, behind=2 if t >= 2 else 0)
                if t >= 2:
                    qk_turn(t - 2)
                if 1 <= t <= 8:
                    qk_sum(t - 1)
                if t == 5:
                    s_scores(0)
            for hd in range(HEADS):
                if hd == 3:
                    ln_column_sums(0)
                if hd == 5:
                    ln_column_sums(1)
                if hd + 1 < HEADS:
                    s_scores(hd + 1)
                s_cumulate(hd)
                if hd >= 1:
                    s_values(hd - 1)
                if hd == 3:
                    ln_turn(0)
                if hd == 5:
                    ln_turn(1)
            s_values(HEADS - 1)
            for m in range(DT):
                features(WOUT2 + m, WOUT2 + m - USE_LAG, m % RING, yy, ready=y_ready(Y_MIX2) if m == 0 else None,
                         order=(0, 1, 2, 4, 5, 6, 7, 3))
            ffn(FFN2, NORM_TWO, 7, Y_F2)


def _feature_blocks(w):
    k, m = w.shape
    return w.reshape(k // P, P, m // P, P).transpose(2, 1, 0, 3).reshape(m // P, P, k)


def _token_blocks(w):
    return w.reshape(4, 2, P, SEQ).transpose(0, 2, 1, 3).reshape(4, P, BLK)


def _ffn_blocks(up, down, halves):
    ups = _feature_blocks(up)
    out, pair = [], 0
    for n in FFN_CHUNKS:
        out.append(np.stack([ups[pair:pair + n], ups[FT + pair:FT + pair + n]], 1).reshape(2 * n, P, BLK))
        part = _feature_blocks(down[pair * P:(pair + n) * P])
        out.append(np.pad(part, ((0, 0), (0, 0), (0, BLK - n * P))))
        pair += n
    return out


def kernel(**inputs):
    import concourse.bacc as _bacc
    from concourse.bass_utils import run_bass_kernel_spmd as _run

    a = {n: np.asarray(v) for n, v in inputs.items()}
    g = {n: (v if n in ("x", "mem", "final_norm_g") else v[0]) for n, v in a.items()}

    def columns(v):
        return v.reshape(-1, P).T

    parts = []
    for name in COLS:
        v = g[name]
        if name in ("q_norm_g_2", "k_norm_g_2"):
            v = np.concatenate([v, v])
        parts.append(columns(v))
    cols = np.concatenate(parts, 1)
    rows = np.concatenate([g["sgu_g"], g["sgu_b"].reshape(-1)])
    mats = np.concatenate([g["pool_w"].transpose(1, 0, 2).reshape(P, 512), g["sgu_w"].transpose(2, 0, 1).reshape(P, 512),
                           np.broadcast_to(rows, (P, 1024))], 1)
    corr = np.array([[w / min(t + 1, w) for t in range(PAD)] for w in POOL_WINDOWS], np.float32)
    corr = np.broadcast_to(corr, (P, 4, PAD))
    w_in, w_in2 = g["w_in"], g["w_in_2"]
    glu = _feature_blocks(w_in2[:, 1536:2560])
    qk = _feature_blocks(w_in2[:, 0:1024])
    stream = [
        _feature_blocks(g["wk"]), _token_blocks(g["wv"][:, 0:512]), _token_blocks(g["wv"][:, 512:1024]),
        _token_blocks(w_in[:, 1024:1536]), _feature_blocks(w_in[:, 0:512]), _feature_blocks(w_in[:, 512:1024]),
        _feature_blocks(g["w_out"]), _feature_blocks(g["wq"]), _feature_blocks(g["wo"]),
        *_ffn_blocks(g["w_up"], g["w_down"], 2),
        np.stack([glu[0:4], glu[4:8]], 1).reshape(8, P, BLK), _token_blocks(w_in2[:, 1024:1536]),
        np.stack([qk[0:4], qk[4:8]], 1).reshape(8, P, BLK), _feature_blocks(g["w_out_2"]),
        *_ffn_blocks(g["w_up_2"], g["w_down_2"], 1),
    ]
    w = np.concatenate(stream, 0)
    assert w.shape == (BLOCKS, P, BLK), w.shape
    arrays = {
        "mem_t": g["mem"][0].T.reshape(DT, P, MEM).transpose(1, 0, 2),
        "x_t": g["x"][0].T.reshape(DT, P, SEQ).transpose(1, 0, 2),
        "cols_in": cols, "mats_in": mats, "corr_in": corr, "weights": w,
    }
    arrays = {n: np.ascontiguousarray(v) for n, v in arrays.items()}
    nc = _bacc.Bacc("TRN2", target_bir_lowering=False, num_devices=1)
    args = [nc.dram_tensor(n, v.shape, F32, kind="ExternalInput").ap() for n, v in arrays.items()]
    args.append(nc.dram_tensor("out_t", (P, DT, SEQ), F32, kind="ExternalOutput").ap())
    build(nc, *args)
    r = _run(nc, [arrays], core_ids=[0])
    out = np.asarray(r.results[0]["out_t"])
    return out.transpose(1, 0, 2).reshape(D, SEQ).T.reshape(1, SEQ, D)
```

```python
from contextlib import ExitStack

import concourse.bass as bass
import numpy as np
from concourse import mybir

F32 = mybir.dt.float32
F32R = mybir.dt.float32r
ACT = mybir.ActivationFunctionType
ALU = mybir.AluOpType
AX = mybir.AxisListType

P = 128
D = 1024
DT = D // P
SEQ = 512
ST = SEQ // P
MEM = 256
MT = MEM // P
FF = 2816
FT = FF // P
EPS = 1e-6
POOL_WINDOWS = (2, 4, 8, 16)
PAD = 16
XH = 4
HEADS = 8
HD = 64
TAPS = 31
FFN_CHUNKS = (8, 8, 6)
BLK = 8 * P
RING = 4
AUX = 4
INP_BANKS = (6, 7, 2, 3)
X_SCORES = (6, 4)
X_VALUES = 2
Z_MAX = 40.0
FAR_BELOW = -1e30

MEMK = 0
MEMV = MEMK + 8
INV = MEMV + 8
INP = INV + 4
INU = INP + 4
WOUT = INU + 4
WQ = WOUT + 8
WO = WQ + 8
FFN1 = WO + 8
FFN_BLOCKS = 2 * FT + DT * len(FFN_CHUNKS)
GLU = FFN1 + FFN_BLOCKS
V2 = GLU + 8
QK = V2 + 4
WOUT2 = QK + 8
FFN2 = WOUT2 + 8
BLOCKS = FFN2 + FFN_BLOCKS
USE_LAG = 4

COLS = {}
_n = 0
for _name, _k in (("norm_mix_g", DT), ("norm_xattn_g", DT), ("mem_norm_g", DT), ("norm_ffn_g", DT),
                  ("final_norm_g", DT), ("norm1_g_2", DT), ("norm2_g_2", DT), ("pool_scale", 4),
                  ("conv_w", 6 * FT), ("conv_b", 2 * FT), ("ffn_dw_w_2", 3 * FT), ("ffn_dw_b_2", FT),
                  ("conv_dw_w_2", TAPS * 4), ("conv_dw_b_2", 4), ("conv_ln_g_2", 4), ("conv_ln_b_2", 4),
                  ("q_norm_g_2", 1), ("k_norm_g_2", 1)):
    COLS[_name] = _n
    _n += _k
N_COLS = _n

NORM_MEM, NORM_MIX, NORM_XATTN, NORM_FFN, NORM_FINAL, NORM_ONE, NORM_TWO = range(7)
TILE0 = {NORM_MEM: 0, NORM_MIX: 8, NORM_XATTN: 16, NORM_FFN: 24, NORM_ONE: 32, NORM_TWO: 40}
SQ0 = {NORM_MEM: 0, NORM_MIX: 8, NORM_XATTN: 16, NORM_FFN: 24, NORM_FINAL: 32, NORM_TWO: 48}


class Count:

    def __init__(self):
        self.base, self.k = 0, 0

    def tick(self):
        self.k += 1
        return self.now()

    def now(self):
        return self.base + self.k

    def enter(self, i, per):
        self.start, self.per = self.base + self.k, per
        self.base, self.k = self.start + i * per, 0

    def leave(self, times):
        assert self.k == self.per, (self.k, self.per)
        self.base, self.k = self.start + times * self.per, 0


def ffn_plan(first):
    out, b, p = [], first, 0
    for n in FFN_CHUNKS:
        out.append((b, n, p, b + 2 * n))
        b += 2 * n + DT
        p += n
    return out


def build(nc, a_mem, a_x, a_cols, a_mats, a_corr, a_w, a_out):
    ctx = ExitStack()
    with ctx:
        def sb(name, shape, dt=F32):
            return ctx.enter_context(nc.sbuf_tensor(name, shape, dt))

        def sem(name):
            return ctx.enter_context(nc.semaphore(name))

        w_raw = sb("w_raw", [P, RING, BLK])
        w_hi = sb("w_hi", [P, RING, BLK], F32R)
        w_lo = sb("w_lo", [P, RING, BLK], F32R)
        h = sb("h", [P, DT, SEQ])
        xg_hi = sb("xg_hi", [P, DT, SEQ], F32R)
        xg_lo = sb("xg_lo", [P, DT, SEQ], F32R)
        y_hi = sb("y_hi", [P, DT, SEQ], F32R)
        y_lo = sb("y_lo", [P, DT, SEQ], F32R)
        slab = sb("slab", [P, 28 * SEQ])
        memg_hi = y_hi[:, 0:4, :].rearrange("p a (b t) -> p (a b) t", b=2)
        memg_lo = y_lo[:, 0:4, :].rearrange("p a (b t) -> p (a b) t", b=2)

        def units(first, n):
            return slab[:, first * SEQ:(first + n) * SEQ]

        k1 = units(0, 4).rearrange("p (m t) -> p m t", t=MEM)
        v1 = units(4, 4).rearrange("p (m d) -> p m d", d=D)
        mem = units(8, 4).rearrange("p (m t) -> p m t", t=MEM)
        u = units(8, 4).rearrange("p (m t) -> p m t", t=SEQ)
        vtok = units(12, 4).rearrange("p (m d) -> p m d", d=SEQ)
        WP = PAD + SEQ
        pp = slab[:, 16 * SEQ:16 * SEQ + 4 * WP].rearrange("p (m t) -> p m t", t=WP)
        win = slab[:, 16 * SEQ + 4 * WP:16 * SEQ + 6 * WP].rearrange("p (m t) -> p m t", t=WP)
        mats = units(24, 4)
        pool_w = mats[:, 0:512].rearrange("p (g d) -> p g d", g=4)
        sgu_w = mats[:, 512:1024].rearrange("p (g d) -> p g d", g=4)
        sgu_g = mats[:, 1024:1536]
        sgu_b = mats[:, 1536:2048].rearrange("p (g t) -> p g t", g=4)
        q1 = units(8, 8).rearrange("p (m t) -> p m t", t=SEQ)
        probs = units(16, 4).rearrange("p (b a m) -> p b a m", b=2, m=MEM)
        probs_t = units(20, 2).rearrange("p (m t) -> p m t", t=SEQ)
        acc = units(0, 4).rearrange("p (m t) -> p m t", t=SEQ)
        prod = units(4, 2).rearrange("p (m t) -> p m t", t=SEQ)
        q2 = units(0, 4).rearrange("p (m t) -> p m t", t=SEQ)
        k2 = units(4, 4).rearrange("p (m t) -> p m t", t=SEQ)
        v2 = units(8, 4).rearrange("p (m d) -> p m d", d=SEQ)
        conv_in = units(12, 4).rearrange("p (m t) -> p m t", t=SEQ)
        conv = units(16, 4).rearrange("p (m t) -> p m t", t=SEQ)
        STICK = SEQ * ST - P * (ST * (ST - 1) // 2)
        stick = slab[:, 20 * SEQ:20 * SEQ + 3 * STICK].rearrange("p (b t) -> p b t", t=STICK)

        cols = sb("cols", [P, N_COLS])
        corr = sb("corr", [P, 4, PAD])
        gain_12 = sb("gain_12", [P, DT])
        ident = sb("ident", [P, P])
        ones = sb("ones", [P, 1])
        half = sb("half", [P, 2])
        minus_half = sb("minus_half", [P, 8])
        mask_incl = sb("mask_incl", [P, P])
        far_below = sb("far_below", [P, P])
        ident_r = sb("ident_r", [P, P], F32R)
        far_below_r = sb("far_below_r", [P, P], F32R)
        neg_tri = sb("neg_tri", [P, P])
        neg_ones = sb("neg_ones", [P, P])
        z_max = sb("z_max", [P, 1])
        sq = sb("sq", [P, 2, SEQ])
        ssq = sb("ssq", [P, 2, SEQ])
        later_sums = sb("later_sums", [P, 2, 3 * P])
        rstd_bc = sb("rstd_bc", [P, SEQ])
        final_bc = sb("final_bc", [P, SEQ])
        var = sb("var", [P, 8])
        rcol = sb("rcol", [P, 8, ST])
        wide = sb("wide", [P, ST, P])
        bn = sb("bn", [P, ST, 6])
        bna = sb("bna", [P, ST, 2])
        tiny = sb("tiny", [P, 4, 8])
        top = sb("top", [P, XH, ST])
        rsum = sb("rsum", [P, XH, ST])
        ps = ctx.enter_context(nc.psum_tensor("ps", [P, 8, SEQ], F32))

        def col(name, k):
            return cols[:, bass.ds(COLS[name] + k, 1)]

        loaded_mem0, loaded_mem1, loaded_x0, loaded_x1 = sem("loaded_mem0"), sem("loaded_mem1"), sem("loaded_x0"), sem("loaded_x1")
        loaded_cols, loaded_mats = sem("loaded_cols"), sem("loaded_mats")
        w_loaded = [sem(f"w_loaded{s}") for s in range(RING)]
        w_hi_ready, w_lo_ready = sem("w_hi_ready"), sem("w_lo_ready")
        blocks_done, banks_freed = sem("blocks_done"), sem("banks_freed")
        consts0, consts, rounded, gain_ready = sem("consts0"), sem("consts"), sem("rounded"), sem("gain_ready")
        vstep = sem("vstep")
        tile_hi, tile_lo = sem("tile_hi"), sem("tile_lo")
        sq_ready, sq_added = sem("sq_ready"), sem("sq_added")
        sums_ready, var_ready, rcol_ready = sem("sums_ready"), sem("var_ready"), sem("rcol_ready")
        wide_ready, spread_ready = sem("wide_ready"), sem("spread_ready")
        y_hi_ready, y_lo_ready = sem("y_hi_ready"), sem("y_lo_ready")
        v_scaled, v_gelu, v_var, v_rstd, vn_ready = (sem(n) for n in ("v_scaled", "v_gelu", "v_var", "v_rstd", "vn_ready"))
        u_gelu, pooled, pool_done, z_done, sgu_masked = (sem(n) for n in ("u_gelu", "pooled", "pool_done", "z_done", "sgu_masked"))
        sgu_bias_in, sgu_prod = sem("sgu_bias_in"), sem("sgu_prod")
        x_scores, x_top, x_exp, x_probs, x_turned, x_copied, x_out = (
            sem(n) for n in ("x_scores", "x_top", "x_exp", "x_probs", "x_turned", "x_copied", "x_out"))
        f_scaled, f_base, f_silu, f_prod = (sem(n) for n in ("f_scaled", "f_base", "f_silu", "f_prod"))
        glu_sig, glu_done, conv_init = sem("glu_sig"), sem("glu_done"), sem("conv_init")
        qk_sums, qk_var, qk_rstd, qk_wide, qk_spread, qk_ready = (
            sem(n) for n in ("qk_sums", "qk_var", "qk_rstd", "qk_wide", "qk_spread", "qk_ready"))
        s_z, s_min, s_exp, s_log, s_sp, s_cum, s_att, s_out = (
            sem(n) for n in ("s_z", "s_min", "s_exp", "s_log", "s_sp", "s_cum", "s_att", "s_out"))
        ln_sum, ln_sums, ln_col, ln_wide, ln_spread, ln_xc, ln_sq, ln_var, ln_rstd, ln_norm, ln_silu = (
            sem(n) for n in ("ln_sum", "ln_sums", "ln_col", "ln_wide", "ln_spread", "ln_xc", "ln_sq", "ln_var",
                             "ln_rstd", "ln_norm", "ln_silu"))
        qk_square, ln_square = sem("qk_square"), sem("ln_square")
        final_ready, final_done = sem("final_ready"), sem("final_done")
        stored = sem("stored")

        TILES = ((0, 0, 512), (1, 0, 384), (2, 0, 256), (1, 384, 128))
        AT = (0, 512, 1024, 896)

        def z_of(hd):
            return ps[:, 3 * (hd % 2):3 * (hd % 2) + 3, :].rearrange("p a t -> p (a t)")[:, 0:STICK]

        def qk_banks(t):
            return (AUX, AUX + 1) if t < 6 else (6, 7)

        Y_MIX, Y_X, Y_F1, Y_MIX2, Y_F2 = 0, 8, 16, 16 + FT, 24 + FT

        block = ctx.enter_context(nc.Block())

        @block.sync
        def _(sp):
            for b in range(RING):
                sp.dma_start(w_raw[:, b, :], a_w[b]).then_inc(w_loaded[b], 16)
                if b == 0:
                    sp.dma_start(mem[:, 0:4, :], a_mem[:, 0:4, :]).then_inc(loaded_mem0, 16)
                    sp.dma_start(mem[:, 4:8, :], a_mem[:, 4:8, :]).then_inc(loaded_mem1, 16)
            sp.dma_start(h[:, 0:4, :], a_x[:, 0:4, :]).then_inc(loaded_x0, 16)
            sp.dma_start(h[:, 4:8, :], a_x[:, 4:8, :]).then_inc(loaded_x1, 16)
            sp.dma_start(mats, a_mats).then_inc(loaded_mats, 16)
            sp.dma_start(corr[:], a_corr).then_inc(loaded_mats, 16)
            region = [(RING, FFN1 + FFN_BLOCKS - DT, BLK), (FFN1 + FFN_BLOCKS - DT, GLU, FFN_CHUNKS[-1] * P),
                      (GLU, BLOCKS - DT, BLK), (BLOCKS - DT, BLOCKS, FFN_CHUNKS[-1] * P)]
            for first, end, width in region:
                with sp.Fori(0, (end - first) // RING) as i:
                    for s in range(RING):
                        sp.wait_ge(w_lo_ready, i * RING + (first + s + 1 - RING))
                        sp.dma_start(w_raw[:, s, 0:width], a_w[i * RING + (first + s)][:, 0:width]).then_inc(w_loaded[s], 16)
            last_down = ffn_plan(FFN2)[-1][3]
            for m in range(DT):
                sp.wait_ge(banks_freed, last_down + m + 1 - USE_LAG)
                sp.dma_start(a_out[:, m, :], h[:, m, :]).then_inc(stored, 16)
            sp.wait_ge(stored, 16 * DT)

        @block.gpsimd
        def _(pool):
            def weights_lo(b, s):
                pool.wait_ge(w_hi_ready, b + 1)
                nc.gpsimd.tensor_tensor(w_lo[:, s, :], w_raw[:, s, :], w_hi[:, s, :].bitcast(F32),
                                        ALU.subtract).then_inc(w_lo_ready, 1)

            def weights_lo_for(first, n):
                n = min(n, BLOCKS - RING - first)
                if n > 0:
                    with pool.Fori(0, n // RING) as i:
                        for s in range(RING):
                            pool.wait_ge(blocks_done, i * RING + (first + s + 1))
                            weights_lo(i * RING + (first + s + RING), s)

            def rstd(n, sizes=ST):
                pool.wait_ge(var_ready, n + 1)
                nc.gpsimd.tensor_tensor(rcol[:, n, 0:sizes], var[:, 0:sizes], minus_half[:, 0:sizes],
                                        ALU.pow).then_inc(rcol_ready, 1)

            for t, value in ((ident, 0.0), (ones, 1.0), (half, 1.0), (minus_half, -0.5), (mask_incl, 1.0),
                             (far_below, 0.0), (neg_tri, -1.0), (neg_ones, -1.0), (z_max, Z_MAX)):
                nc.gpsimd.memset(t[:], value).then_inc(consts0, 1)
            pool.wait_ge(consts0, 9)

            def select(t, op, fill, base, step, per_partition):
                nc.gpsimd.affine_select(out=t, in_=t, compare_op=op, fill=fill, base=base, pattern=[[step, t.shape[1]]],
                                        channel_multiplier=per_partition).then_inc(consts, 1)

            select(ident[:], ALU.not_equal, 1.0, 0, -1, 1)
            select(half[:, 0:1], ALU.is_ge, 0.0, HD - 1, 0, -1)
            select(half[:, 1:2], ALU.is_ge, 0.0, -HD, 0, 1)
            select(mask_incl[:], ALU.is_ge, 0.0, 0, 1, -1)
            select(far_below[:], ALU.is_ge, FAR_BELOW, -1, 1, -1)
            select(neg_tri[:], ALU.is_ge, 0.0, 0, -1, 1)

            pool.wait_ge(w_lo_ready, 1)
            for b in range(1, RING):
                weights_lo(b, b)
                if b == 2:
                    rstd(NORM_MEM, MT)
            weights_lo_for(MEMK, INV - MEMK)
            rstd(NORM_MIX)
            weights_lo_for(INV, INP - INV)
            pool.wait_ge(v_var, ST)
            nc.gpsimd.tensor_tensor(tiny[:, 0, 0:ST], tiny[:, 1, 0:ST], minus_half[:, 0:ST], ALU.pow).then_inc(v_rstd, 1)
            weights_lo_for(INP, WQ - INP)
            rstd(NORM_XATTN)
            weights_lo_for(WQ, FFN1 - WQ)
            rstd(NORM_FFN)
            weights_lo_for(FFN1, FFN_BLOCKS)
            rstd(NORM_FINAL)
            rstd(NORM_ONE)
            weights_lo_for(GLU, QK - GLU)
            for t in range(8):
                pool.wait_ge(blocks_done, QK + t + 1)
                weights_lo(QK + t + RING, t % RING)
                pool.wait_ge(qk_var, t + 1)
                nc.gpsimd.tensor_tensor(tiny[:, 2 + t % 2, :], tiny[:, t % 2, :], minus_half[:], ALU.pow).then_inc(qk_rstd, 1)
            pool.wait_ge(ln_var, 1)
            nc.gpsimd.tensor_tensor(rcol[:, 7, :], var[:, 4:8], minus_half[:, 0:ST], ALU.pow).then_inc(ln_rstd, 1)
            weights_lo_for(WOUT2, FFN2 - WOUT2)
            rstd(NORM_TWO)
            weights_lo_for(FFN2, FFN_BLOCKS)

        @block.scalar
        def _(act):
            act.dma_start(cols[:], a_cols).then_inc(loaded_cols, 16)

            def weights_hi(b, s, use):
                if b >= RING:
                    act.wait_ge(blocks_done, b + 1 - RING)
                act.wait_ge(w_loaded[s], 16 * (use + 1))
                nc.scalar.activation(w_hi[:, s, :], w_raw[:, s, :], ACT.Copy).then_inc(w_hi_ready, 1)

            def weights_hi_for(b):
                b += RING
                if b < BLOCKS:
                    weights_hi(b, b % RING, b // RING)

            def weights_hi_loop(i, first, s):
                act.wait_ge(blocks_done, i * RING + (first + s + 1))
                act.wait_ge(w_loaded[s], i * 16 + 16 * (first // RING + 2))
                nc.scalar.activation(w_hi[:, s, :], w_raw[:, s, :], ACT.Copy).then_inc(w_hi_ready, 1)

            def weights_hi_run(first, n):
                n = min(n, BLOCKS - RING - first)
                if n > 0:
                    with act.Fori(0, n // RING) as i:
                        for s in range(RING):
                            weights_hi_loop(i, first, s)

            def square(src, gain, n):
                if n >= 2:
                    act.wait_ge(sq_added, n - 1)
                nc.scalar.activation(sq[:, n % 2, 0:src.shape[1]], src, ACT.Square, scale=gain).then_inc(sq_ready, 1)

            def split_gain(dst, src, gain):
                nc.scalar.activation(dst, src, ACT.Copy, scale=gain).then_inc(tile_hi, 1)

            def residual(first, norm, gain):
                for m in range(DT):
                    act.wait_ge(banks_freed, first + m + 1 - USE_LAG)
                    split_gain(xg_hi[:, m, :], h[:, m, :], gain(m))
                    if norm == NORM_FINAL:
                        square(h[:, m, :], 1.0, SQ0[norm] + 2 * m)
                        square(h[:, m, :], col("final_norm_g", m), SQ0[norm] + 2 * m + 1)
                    else:
                        square(h[:, m, :], 1.0, SQ0[norm] + m)
                    weights_hi_for(first + m)

            def ffn(first, both):
                nc.scalar.preload_act_table_set("silu_and_others")
                w, b, n_w = ("conv_w", "conv_b", 2 * FT) if both else ("ffn_dw_w_2", "ffn_dw_b_2", FT)
                f0, y0, s0 = (0, Y_F1, 0) if both else (FT, Y_F2, 2 * FT)
                p0 = 0 if both else 2 * FT
                for first_b, n, pair0, down in ffn_plan(first):
                    with act.Fori(0, n // 2) as i:
                        for j in range(2):
                            s, pair = 2 * j, i * 2 + (pair0 + j)
                            for v in range(2 if both else 1):
                                act.wait_ge(f_scaled, pair * 2 + (s0 + v + 1))
                                nc.scalar.activation(acc[:, s + v, :], ps[:, s + v, :], ACT.Identity,
                                                     scale=col(w, pair + (2 * n_w + v * FT)),
                                                     bias=col(b, pair + v * FT)).then_inc(f_base, 1)
                            weights_hi_loop(i, first_b, s)
                            act.wait_ge(banks_freed, i * RING + (first_b + s + 1 - USE_LAG))
                            nc.scalar.activation(acc[:, s, :], acc[:, s, :], ACT.Silu).then_inc(f_silu, 1)
                            act.wait_ge(f_prod, pair + (f0 + 1))
                            nc.scalar.activation(y_hi[:, bass.ds(i * 2 + j, 1), :].rearrange("p a t -> p (a t)"),
                                                 prod[:, j, :], ACT.Copy).then_inc(y_hi_ready, 1)
                            weights_hi_loop(i, first_b, s + 1)
                    if down != ffn_plan(first)[-1][3] or not both:
                        weights_hi_run(down, DT)

            weights_hi(0, 0, 0)
            act.wait_ge(loaded_cols, 16)
            for m in range(DT):
                if m in (0, 4):
                    act.wait_ge((loaded_mem0, loaded_mem1)[m // 4], 16)
                split_gain(memg_hi[:, m, :], mem[:, m, :], col("mem_norm_g", m))
                square(mem[:, m, :], 1.0, SQ0[NORM_MEM] + m)
                if m == 4:
                    weights_hi(1, 1, 0)
            for b in range(2, RING):
                weights_hi(b, b, 0)
            for m in range(DT):
                if m in (0, 4):
                    act.wait_ge((loaded_x0, loaded_x1)[m // 4], 16)
                split_gain(xg_hi[:, m, :], h[:, m, :], col("norm_mix_g", m))
                square(h[:, m, :], 1.0, SQ0[NORM_MIX] + m)
                weights_hi_for(MEMK + m)
            weights_hi_run(MEMV, INP - MEMV)

            nc.scalar.preload_act_table_set("gelu_and_others")
            for t in range(ST):
                act.wait_ge(v_scaled, t + 1)
                nc.scalar.activation(vtok[:, t, :], vtok[:, t, :], ACT.Gelu).then_inc(v_gelu, 1)
            for b in range(INP, INU):
                weights_hi_for(b)
            for t in range(4):
                act.wait_ge(banks_freed, INU + t + 1 - USE_LAG)
                nc.scalar.activation(u[:, t, :], u[:, t, :], ACT.Gelu).then_inc(u_gelu, 1)
                weights_hi_for(INU + t)
                if t == 0:
                    for g in range(4):
                        act.wait_ge(pool_done, g + 1)
                        nc.scalar.activation(y_hi[:, g, :], ps[:, AUX + g, :], ACT.Copy,
                                             scale=col("pool_scale", g)).then_inc(y_hi_ready, 1)
            for g in range(4):
                act.wait_ge(sgu_prod, g + 1)
                nc.scalar.activation(y_hi[:, 4 + g, :], u[:, g, :], ACT.Copy).then_inc(y_hi_ready, 1)
            residual(WOUT, NORM_XATTN, lambda m: col("norm_xattn_g", m))

            def x_softmax(hd):
                act.wait_ge(x_top, hd + 1)
                for t in range(ST):
                    nc.scalar.activation(probs[:, hd % 2, t, :], ps[:, X_SCORES[hd % 2] + t // 2, (t % 2) * MEM:(t % 2 + 1) * MEM],
                                         ACT.Exp, bias=top[:, hd, t:t + 1], scale=MEM ** -0.5,
                                         accum_out=rsum[:, hd, t:t + 1]).then_inc(x_exp, 1)

            def x_result(hd):
                for d in range(2):
                    act.wait_ge(x_out, 2 * hd + d + 1)
                    nc.scalar.activation(y_hi[:, 2 * hd + d, :], ps[:, X_VALUES + d, :], ACT.Copy).then_inc(y_hi_ready, 1)

            nc.scalar.preload_act_table_set("natural_log_exp_and_others")
            for b in range(4):
                weights_hi_for(WQ + b)
            x_softmax(0)
            for hd in range(XH):
                for b in ((4,), (5,), (6, 7), ())[hd]:
                    weights_hi_for(WQ + b)
                if hd + 1 < XH:
                    x_softmax(hd + 1)
                x_result(hd)
            residual(WO, NORM_FFN, lambda m: col("norm_ffn_g", m))
            ffn(FFN1, True)
            act.wait_ge(gain_ready, 1)
            residual(ffn_plan(FFN1)[-1][3], NORM_FINAL, lambda m: gain_12[:, m:m + 1])

            nc.scalar.preload_act_table_set("sigmoid_and_others")
            for i in range(4):
                weights_hi_for(GLU + 2 * i)
                weights_hi_for(GLU + 2 * i + 1)
                act.wait_ge(banks_freed, GLU + 2 * i + 2 - USE_LAG)
                nc.scalar.activation(k2[:, i, :], k2[:, i, :], ACT.Sigmoid).then_inc(glu_sig, 1)
                act.wait_ge(glu_done, i + 1)
                nc.scalar.activation(conv[:, i, :], conv_in[:, i, :], ACT.Identity,
                                     scale=col("conv_dw_w_2", (TAPS - 1) * 4 + i),
                                     bias=col("conv_dw_b_2", i)).then_inc(conv_init, 1)
            for b in range(V2, QK):
                weights_hi_for(b)
            nc.scalar.preload_act_table_set("natural_log_exp_and_others")

            def s_logs(hd):
                t = stick[:, hd % 3, :]
                act.wait_ge(s_z, hd + 1)
                if hd >= 3:
                    act.wait_ge(s_out, hd - 2)
                nc.scalar.activation(t, z_of(hd), ACT.Relu, scale=-1.0, bias=z_max[:]).then_inc(s_min, 1)
                act.wait_ge(s_min, hd + 1)
                nc.scalar.activation(t, t, ACT.Exp, scale=-1.0, bias=z_max[:]).then_inc(s_exp, 1)
                act.wait_ge(s_exp, hd + 1)
                nc.scalar.activation(t, t, ACT.Ln, bias=1.0).then_inc(s_log, 1)

            act.wait_ge(consts0, 9)
            for t in range(8):
                act.wait_ge(banks_freed, QK + t + 1 - USE_LAG)
                if t >= 2:
                    act.wait_ge(qk_sums, t - 1)
                nc.scalar.activation(sq[:, t % 2, :], (q2, k2)[t % 2][:, t // 2, :], ACT.Square).then_inc(qk_square, 1)
                weights_hi_for(QK + t)
                if t == 4:
                    s_logs(0)

            def s_weights(hd):
                for part, c in enumerate((slice(0, SEQ), slice(SEQ, STICK))):
                    act.wait_ge(s_cum, 2 * hd + part + 1)
                    nc.scalar.activation(stick[:, hd % 3, c], z_of(hd)[:, c], ACT.Exp).then_inc(s_att, 1)

            s_weights(0)
            for hd in range(HEADS):
                if hd + 1 < HEADS:
                    s_logs(hd + 1)
                if hd >= 1:
                    s_weights(hd)
                if hd == 5:
                    for i in range(4):
                        act.wait_ge(ln_xc, i + 1)
                        nc.scalar.activation(conv_in[:, i, :], conv[:, i, :], ACT.Square).then_inc(ln_square, 1)
                if hd % 2 == 0 and hd >= 2:
                    act.wait_ge(s_out, hd)
                    nc.scalar.activation(y_hi[:, hd // 2 - 1, :], ps[:, 6, :], ACT.Copy).then_inc(y_hi_ready, 1)
            nc.scalar.preload_act_table_set("silu_and_others")
            for i in range(4):
                act.wait_ge(ln_norm, i + 1)
                nc.scalar.activation(conv[:, i, :], conv[:, i, :], ACT.Silu, scale=col("conv_ln_g_2", i),
                                     bias=col("conv_ln_b_2", i)).then_inc(ln_silu, 1)
            act.wait_ge(s_out, HEADS)
            nc.scalar.activation(y_hi[:, 3, :], ps[:, 6, :], ACT.Copy).then_inc(y_hi_ready, 1)
            for i in range(4):
                act.wait_ge(ln_silu, i + 1)
                nc.scalar.activation(y_hi[:, 4 + i, :], conv[:, i, :], ACT.Copy).then_inc(y_hi_ready, 1)
            residual(WOUT2, NORM_TWO, lambda m: col("norm2_g_2", m))
            ffn(FFN2, False)

        @block.vector
        def _(dve):
            own = Count()

            def multiply_by_rstd(out, b, bank, width=SEQ):
                dve.wait_ge(blocks_done, b + 1)
                return nc.vector.tensor_tensor(out, ps[:, bank, 0:width], rstd_bc[:, 0:width], ALU.mult)

            def add_squares(n, which, first, width=SEQ):
                dve.wait_ge(sq_ready, n + 1)
                dst = ssq[:, which, 0:width]
                if first:
                    nc.vector.tensor_copy(dst, sq[:, n % 2, 0:width]).then_inc(sq_added, 1)
                else:
                    dve.wait_ge(sq_added, n)
                    nc.vector.tensor_tensor(dst, dst, sq[:, n % 2, 0:width], ALU.add).then_inc(sq_added, 1)

            def split_gain_lo(n, dst, src, gain, hi):
                dve.wait_ge(tile_hi, n + 1)
                nc.vector.scalar_tensor_tensor(out=dst, in0=src, scalar=gain, in1=hi.bitcast(F32), op0=ALU.mult,
                                               op1=ALU.subtract).then_inc(tile_lo, 1)

            def split_lo(dst, src, hi, n):
                dve.wait_ge(y_hi_ready, n + 1)
                nc.vector.tensor_tensor(dst, src, hi.bitcast(F32), ALU.subtract).then_inc(y_lo_ready, 1)

            def variance(n, count, sizes=ST):
                dve.wait_ge(sums_ready, n + 1 if n <= NORM_FINAL else n)
                nc.vector.tensor_scalar(var[:, 0:sizes], ps[:, AUX, 0:sizes], 1.0 / count, EPS, ALU.mult,
                                        ALU.add).then_inc(var_ready, 1)

            def spread(n, wides, sizes=ST):
                dve.wait_ge(rcol_ready, n + 1)
                nc.vector.tensor_copy(wide[:, 0:sizes, :], rcol[:, n, 0:sizes].rearrange("p (a b) -> p a b", b=1)
                                      .broadcast_to([P, sizes, P])).then_inc(wide_ready, 1)
                dve.wait_ge(spread_ready, wides)
                nc.vector.tensor_copy(rstd_bc[:, 0:sizes * P], ps[:, AUX + 1, 0:sizes * P]).then_inc(vstep, 1)
                own.tick()
                dve.wait_ge(vstep, own.now())

            def residual(first, norm, gain):
                for m in range(DT):
                    dve.wait_ge(blocks_done, first + m + 1)
                    nc.vector.tensor_tensor(h[:, m, :], ps[:, m % RING, :], h[:, m, :], ALU.add).then_inc(banks_freed, 1)
                    n = TILE0[NORM_ONE if norm == NORM_FINAL else norm] + m
                    split_gain_lo(n, xg_lo[:, m, :], h[:, m, :], gain(m), xg_hi[:, m, :])
                    if norm == NORM_FINAL:
                        add_squares(SQ0[norm] + 2 * m, 0, m == 0)
                        add_squares(SQ0[norm] + 2 * m + 1, 1, m == 0)
                    else:
                        add_squares(SQ0[norm] + m, 0, m == 0)

            def ffn(first, both):
                w, n_w = ("conv_w", 2 * FT) if both else ("ffn_dw_w_2", FT)
                f0, y0, s0, c0 = (0, Y_F1, 0, 0) if both else (FT, Y_F2, 2 * FT, 2 * FT)
                for first_b, n, pair0, down in ffn_plan(first):
                    with dve.Fori(0, n // 2) as i:
                        own.enter(i, 4 if both else 2)
                        for j in range(2):
                            s, pair = 2 * j, i * 2 + (pair0 + j)
                            b = i * RING + (first_b + s)
                            for v in range(2):
                                multiply_by_rstd(ps[:, s + v, :], b + v, s + v).then_inc(f_scaled, 1)
                            convolved = range(2 if both else 1)
                            for v in convolved:
                                dve.wait_ge(f_base, (pair * 2 if both else pair) + (c0 + v + 1))
                                nc.vector.scalar_tensor_tensor(out=acc[:, s + v, 1:], in0=ps[:, s + v, 0:SEQ - 1],
                                                               scalar=col(w, pair + (n_w + v * FT)),
                                                               in1=acc[:, s + v, 1:], op0=ALU.mult, op1=ALU.add).then_inc(vstep, 1)
                                own.tick()
                            for v in convolved:
                                dve.wait_ge(vstep, own.now() - (convolved[-1] - v))
                                nc.vector.scalar_tensor_tensor(out=acc[:, s + v, 2:], in0=ps[:, s + v, 0:SEQ - 2],
                                                               scalar=col(w, pair + v * FT),
                                                               in1=acc[:, s + v, 2:], op0=ALU.mult, op1=ALU.add).then_inc(banks_freed, 1)
                            dve.wait_ge(f_silu, pair + (f0 + 1))
                            if both:
                                dve.wait_ge(banks_freed, b + (2 - USE_LAG))
                                nc.vector.tensor_tensor(prod[:, j, :], acc[:, s, :], acc[:, s + 1, :], ALU.mult).then_inc(f_prod, 1)
                            else:
                                dve.wait_ge(f_scaled, pair * 2 + (s0 + 2))
                                nc.vector.tensor_tensor(prod[:, j, :], ps[:, s + 1, :], acc[:, s, :], ALU.mult).then_inc(f_prod, 1)
                                dve.wait_ge(f_prod, pair + (f0 + 1))
                                nc.vector.memset(tiny[:, 3, 0:1], 0.0).then_inc(banks_freed, 1)
                            y = y_lo[:, bass.ds(i * 2 + j, 1), :].rearrange("p a t -> p (a t)")
                            yh = y_hi[:, bass.ds(i * 2 + j, 1), :].rearrange("p a t -> p (a t)")
                            dve.wait_ge(f_prod, pair + (f0 + 1))
                            split_lo(y, prod[:, j, :], yh, pair + y0)
                        own.leave(n // 2)
                    if down != ffn_plan(first)[-1][3]:
                        for m in range(DT):
                            dve.wait_ge(blocks_done, down + m + 1)
                            nc.vector.tensor_tensor(h[:, m, :], ps[:, m % RING, :], h[:, m, :], ALU.add).then_inc(banks_freed, 1)

            nc.vector.memset(slab[:, 16 * SEQ:16 * SEQ + 6 * WP], 0.0).then_inc(vstep, 1)
            own.tick()
            dve.wait_ge(loaded_cols, 16)
            nc.vector.tensor_tensor(gain_12[:], cols[:, COLS["final_norm_g"]:COLS["final_norm_g"] + DT],
                                    cols[:, COLS["norm1_g_2"]:COLS["norm1_g_2"] + DT], ALU.mult).then_inc(gain_ready, 1)
            dve.wait_ge(w_hi_ready, 1)
            nc.vector.tensor_tensor(w_lo[:, 0, :], w_raw[:, 0, :], w_hi[:, 0, :].bitcast(F32), ALU.subtract).then_inc(w_lo_ready, 1)
            for m in range(DT):
                if m in (0, 4):
                    dve.wait_ge((loaded_mem0, loaded_mem1)[m // 4], 16)
                split_gain_lo(TILE0[NORM_MEM] + m, memg_lo[:, m, :], mem[:, m, :], col("mem_norm_g", m), memg_hi[:, m, :])
                add_squares(SQ0[NORM_MEM] + m, 0, m == 0, MEM)
            variance(NORM_MEM, D, MT)
            spread(NORM_MEM, 1, MT)
            for m in range(DT):
                if m in (0, 4):
                    dve.wait_ge((loaded_x0, loaded_x1)[m // 4], 16)
                split_gain_lo(TILE0[NORM_MIX] + m, xg_lo[:, m, :], h[:, m, :], col("norm_mix_g", m), xg_hi[:, m, :])
                add_squares(SQ0[NORM_MIX] + m, 1, m == 0)
                multiply_by_rstd(k1[:, m, :], MEMK + m, m % RING, MEM).then_inc(banks_freed, 1)
            for side in range(2):
                dve.wait_ge(blocks_done, MEMV + 4 * side + 4)
                for t in range(MT):
                    nc.vector.tensor_scalar(v1[:, t, side * SEQ:(side + 1) * SEQ], ps[:, 2 * side + t, :],
                                            rcol[:, NORM_MEM, t:t + 1], None, ALU.mult).then_inc(banks_freed, 1)
                if side == 0:
                    dve.wait_ge(loaded_mats, 32)
                    dve.wait_ge(consts, 6)
                    nc.vector.tensor_copy(ident_r[:], ident[:]).then_inc(rounded, 1)
                    nc.vector.tensor_copy(far_below_r[:], far_below[:]).then_inc(rounded, 1)
                    nc.vector.tensor_tensor(sgu_w, sgu_w, mask_incl[:].rearrange("p (a t) -> p a t", a=1)
                                            .broadcast_to([P, 4, P]), ALU.mult).then_inc(sgu_masked, 1)
            variance(NORM_MIX, D)
            spread(NORM_MIX, 2)

            dve.wait_ge(blocks_done, INV + 4)
            for t in range(ST):
                nc.vector.tensor_scalar(vtok[:, t, :], ps[:, t, :], rcol[:, NORM_MIX, t:t + 1], None,
                                        ALU.mult).then_inc(v_scaled, 1)
            dve.wait_ge(v_scaled, ST)
            for t in range(ST):
                nc.vector.memset(tiny[:, 3, t:t + 1], 0.0).then_inc(banks_freed, 1)
            for t in range(ST):
                dve.wait_ge(v_gelu, t + 1)
                nc.vector.bn_stats(bn[:, t, :], vtok[:, t, :]).then_inc(vstep, 1)
                own.tick()
            for t in range(ST):
                dve.wait_ge(vstep, own.now() - (ST - 1 - t) if t == 0 else own.now() - (ST - 1))
                nc.vector.bn_aggr(bna[:, t, :], bn[:, t, :]).then_inc(vstep, 1)
                own.tick()
            dve.wait_ge(vstep, own.now())
            for t in range(ST):
                nc.vector.tensor_scalar(tiny[:, 1, t:t + 1], bna[:, t, 1:2], EPS, None, ALU.add).then_inc(v_var, 1)

            def pool_windows(g):
                multiply_by_rstd(pp[:, g, PAD:], INP + g, INP_BANKS[g]).then_inc(banks_freed, 1)
                dve.wait_ge(banks_freed, INP + g + 1 - USE_LAG)
                src, step, at = pp[:, g, :], 1, 0
                while step < POOL_WINDOWS[g]:
                    dst = win[:, at, :]
                    nc.vector.tensor_tensor(dst[:, step:], src[:, step:], src[:, 0:WP - step], ALU.add).then_inc(vstep, 1)
                    own.tick()
                    dve.wait_ge(vstep, own.now())
                    src, step, at = dst, 2 * step, 1 - at
                nc.vector.tensor_tensor(src[:, PAD:2 * PAD], src[:, PAD:2 * PAD], corr[:, g, :], ALU.mult).then_inc(vstep, 1)
                own.tick()
                dve.wait_ge(vstep, own.now())
                nc.vector.scalar_tensor_tensor(out=pp[:, g, PAD:], in0=src[:, PAD:], scalar=1.0 / POOL_WINDOWS[g],
                                               in1=pp[:, g, PAD:], op0=ALU.mult, op1=ALU.subtract).then_inc(pooled, 1)
                dve.wait_ge(pooled, g + 1)

            pool_windows(0)
            dve.wait_ge(v_rstd, 1)
            for t in range(ST):
                nc.vector.tensor_scalar(vtok[:, t, :], vtok[:, t, :], bna[:, t, 0:1], tiny[:, 0, t:t + 1], ALU.subtract,
                                        ALU.mult).then_inc(vstep, 1)
                own.tick()
            for t in range(ST):
                dve.wait_ge(vstep, own.now() - (ST - 1 - t))
                nc.vector.tensor_tensor(vtok[:, t, :], vtok[:, t, :], sgu_g, ALU.mult).then_inc(vn_ready, 1)
            for g in range(1, 4):
                pool_windows(g)
            for t in range(4):
                multiply_by_rstd(u[:, t, :], INU + t, t).then_inc(banks_freed, 1)
                if t == 0:
                    for g in range(4):
                        dve.wait_ge(y_hi_ready, Y_MIX + g + 1)
                        nc.vector.scalar_tensor_tensor(out=y_lo[:, g, :], in0=ps[:, AUX + g, :], scalar=col("pool_scale", g),
                                                       in1=y_hi[:, g, :].bitcast(F32), op0=ALU.mult,
                                                       op1=ALU.subtract).then_inc(y_lo_ready, 1)
            def sgu_bias(g):
                dve.wait_ge(z_done, g + 1)
                z = ps[:, AUX + g, :].rearrange("p (c t) -> p c t", t=P)
                nc.vector.tensor_tensor(z, z, sgu_b[:, g:g + 1, :].broadcast_to([P, ST, P]), ALU.add).then_inc(sgu_bias_in, 1)

            def sgu_gate(g):
                dve.wait_ge(sgu_bias_in, g + 1)
                dve.wait_ge(u_gelu, g + 1)
                nc.vector.tensor_tensor(u[:, g, :], ps[:, AUX + g, :], u[:, g, :], ALU.mult).then_inc(sgu_prod, 1)

            def sgu_lo(g):
                dve.wait_ge(sgu_prod, g + 1)
                split_lo(y_lo[:, 4 + g, :], u[:, g, :], y_hi[:, 4 + g, :], Y_MIX + 4 + g)

            sgu_bias(0)
            for g in range(4 + 1):
                if g + 1 < 4:
                    sgu_bias(g + 1)
                if g < 4:
                    sgu_gate(g)
                if g >= 1:
                    sgu_lo(g - 1)
            residual(WOUT, NORM_XATTN, lambda m: col("norm_xattn_g", m))

            def x_max(hd):
                for b in range(2):
                    dve.wait_ge(x_scores, 2 * hd + b + 1)
                    nc.vector.tensor_reduce(top[:, hd, 2 * b:2 * b + 2], ps[:, X_SCORES[hd % 2] + b, :].rearrange("p (a m) -> p a m", m=MEM),
                                            AX.X, ALU.max).then_inc(vstep, 1)
                    own.tick()
                dve.wait_ge(vstep, own.now())
                nc.vector.tensor_scalar(top[:, hd, :], top[:, hd, :], -(MEM ** -0.5), None, ALU.mult).then_inc(x_top, 1)

            def x_normalise(hd):
                dve.wait_ge(x_exp, ST * (hd + 1))
                nc.vector.reciprocal(rsum[:, hd, :], rsum[:, hd, :]).then_inc(vstep, 1)
                own.tick()
                dve.wait_ge(vstep, own.now())
                for t in range(ST):
                    nc.vector.tensor_scalar(probs[:, hd % 2, t, :], probs[:, hd % 2, t, :], rsum[:, hd, t:t + 1], None,
                                            ALU.mult).then_inc(x_probs, 1)

            def x_turn(hd):
                for m in range(MT):
                    dve.wait_ge(x_turned, 2 * hd + m + 1)
                    nc.vector.tensor_copy(probs_t[:, m, :], ps[:, X_VALUES + m, :]).then_inc(x_copied, 1)

            def x_lo(hd):
                for d in range(2):
                    t = 2 * hd + d
                    split_lo(y_lo[:, t, :], ps[:, X_VALUES + d, :], y_hi[:, t, :], Y_X + t)

            variance(NORM_XATTN, D)
            spread(NORM_XATTN, 3)

            def x_query(m):
                multiply_by_rstd(q1[:, m, :], WQ + m, m if m < 4 else m % 2).then_inc(banks_freed, 1)

            for m in range(4):
                x_query(m)
            x_max(0)
            x_normalise(0)
            for hd in range(XH):
                for m in ((4,), (5,), (6, 7), ())[hd]:
                    x_query(m)
                x_turn(hd)
                if hd + 1 < XH:
                    x_max(hd + 1)
                    x_normalise(hd + 1)
                x_lo(hd)
            residual(WO, NORM_FFN, lambda m: col("norm_ffn_g", m))
            variance(NORM_FFN, D)
            spread(NORM_FFN, 4)
            ffn(FFN1, True)
            residual(ffn_plan(FFN1)[-1][3], NORM_FINAL, lambda m: gain_12[:, m:m + 1])

            variance(NORM_FINAL, D)
            dve.wait_ge(rcol_ready, NORM_FINAL + 1)
            nc.vector.tensor_tensor(tiny[:, 0, 0:ST], rcol[:, NORM_FINAL, :], rcol[:, NORM_FINAL, :], ALU.mult).then_inc(vstep, 1)
            own.tick()
            dve.wait_ge(vstep, own.now())
            nc.vector.tensor_tensor(tiny[:, 0, 0:ST], ps[:, AUX, ST:2 * ST], tiny[:, 0, 0:ST], ALU.mult).then_inc(vstep, 1)
            own.tick()
            dve.wait_ge(vstep, own.now())
            nc.vector.tensor_scalar(var[:, 0:ST], tiny[:, 0, 0:ST], 1.0 / D, EPS, ALU.mult, ALU.add).then_inc(var_ready, 1)
            dve.wait_ge(rcol_ready, NORM_ONE + 1)
            nc.vector.tensor_tensor(rcol[:, NORM_ONE, :], rcol[:, NORM_ONE, :], rcol[:, NORM_FINAL, :], ALU.mult).then_inc(vstep, 1)
            own.tick()
            dve.wait_ge(vstep, own.now())
            spread(NORM_ONE, 5)

            def final_rstd():
                nc.vector.tensor_copy(wide[:], rcol[:, NORM_FINAL, :].rearrange("p (a b) -> p a b", b=1)
                                      .broadcast_to([P, ST, P])).then_inc(wide_ready, 1)
                dve.wait_ge(spread_ready, 6)
                nc.vector.tensor_copy(final_bc[:], ps[:, AUX + 1, :]).then_inc(final_ready, 1)

            def final_norm(tiles):
                dve.wait_ge(final_ready, 1)
                for m in tiles:
                    nc.vector.scalar_tensor_tensor(out=h[:, m, :], in0=h[:, m, :], scalar=col("final_norm_g", m),
                                                   in1=final_bc[:], op0=ALU.mult, op1=ALU.mult).then_inc(final_done, 1)

            tap_order = [(i0 + i, j) for i0 in (0, 2) for j in range(1, TAPS) for i in range(2)]
            taps_done = Count()

            def conv_taps(n):
                for _ in range(n):
                    if not tap_order:
                        return
                    i, j = tap_order.pop(0)
                    if j == 1:
                        dve.wait_ge(conv_init, i + 1)
                    else:
                        dve.wait_ge(ln_sum, taps_done.now() - 1)
                    nc.vector.scalar_tensor_tensor(out=conv[:, i, j:], in0=conv_in[:, i, 0:SEQ - j],
                                                   scalar=col("conv_dw_w_2", (TAPS - 1 - j) * 4 + i),
                                                   in1=conv[:, i, j:], op0=ALU.mult, op1=ALU.add).then_inc(ln_sum, 1)
                    taps_done.tick()

            for i in range(4):
                multiply_by_rstd(q2[:, i, :], GLU + 2 * i, (2 * i) % RING).then_inc(banks_freed, 1)
                multiply_by_rstd(k2[:, i, :], GLU + 2 * i + 1, (2 * i + 1) % RING).then_inc(banks_freed, 1)
                dve.wait_ge(banks_freed, GLU + 2 * i + 2 - USE_LAG)
                dve.wait_ge(glu_sig, i + 1)
                nc.vector.tensor_tensor(conv_in[:, i, :], q2[:, i, :], k2[:, i, :], ALU.mult).then_inc(glu_done, 1)
                if i == 0:
                    final_rstd()
                else:
                    conv_taps((0, 10, 11, 14)[i])
            conv_taps(26)
            dve.wait_ge(blocks_done, V2 + 4)
            for t in range(ST):
                nc.vector.tensor_scalar(v2[:, t, :], ps[:, t, :], rcol[:, NORM_ONE, t:t + 1], None, ALU.mult).then_inc(banks_freed, 1)

            def qk_square_sums(t):
                dve.wait_ge(qk_sums, t + 1)
                if t >= 2:
                    dve.wait_ge(qk_rstd, t - 1)
                nc.vector.tensor_scalar(tiny[:, t % 2, :], ps[:, qk_banks(t)[0], 0:8], 1.0 / HD, EPS, ALU.mult, ALU.add).then_inc(qk_var, 1)

            def qk_scale(t):
                dve.wait_ge(qk_rstd, t + 1)
                nc.vector.tensor_scalar(wide[:].rearrange("p a (b c) -> p (a b) c", b=2),
                                        tiny[:, 2 + t % 2, :].rearrange("p (a b) -> p a b", b=1).broadcast_to([P, 8, HD]),
                                        HD ** -0.5 if t % 2 == 0 else 1.0, None, ALU.mult).then_inc(qk_wide, 1)

            def qk_apply(t):
                dst = (q2, k2)[t % 2][:, t // 2, :]
                dve.wait_ge(qk_spread, t + 1)
                nc.vector.scalar_tensor_tensor(out=dst, in0=dst, scalar=col(("q_norm_g_2", "k_norm_g_2")[t % 2], 0),
                                               in1=ps[:, qk_banks(t)[1], :], op0=ALU.mult, op1=ALU.mult).then_inc(qk_ready, 1)

            def s_softplus(hd):
                t = stick[:, hd % 3, :]
                dve.wait_ge(s_log, hd + 1)
                nc.vector.tensor_tensor(t, z_of(hd), t, ALU.max).then_inc(vstep, 1)
                own.tick()
                dve.wait_ge(vstep, own.now())
                later = later_sums[:, hd % 2, :]
                if hd >= 2:
                    dve.wait_ge(s_cum, 2 * (hd - 1))
                for dst, a, b in ((later[:, 0:P], t[:, AT[2] + P:AT[2] + 2 * P], t[:, AT[3]:AT[3] + P]),
                                  (later[:, P:2 * P], t[:, AT[1] + P:AT[1] + 2 * P], t[:, AT[2]:AT[2] + P])):
                    nc.vector.tensor_tensor(dst, a, b, ALU.add).then_inc(vstep, 1)
                    own.tick()
                dve.wait_ge(vstep, own.now())
                nc.vector.tensor_tensor(later[:, 2 * P:3 * P], t[:, AT[1] + 2 * P:AT[1] + 3 * P], later[:, 0:P],
                                        ALU.add).then_inc(s_sp, 1)

            for t in range(8 + 1):
                if t < 8:
                    multiply_by_rstd((q2, k2)[t % 2][:, t // 2, :], QK + t, 6 + t % 2).then_inc(banks_freed, 1)
                if 2 <= t < 8:
                    qk_apply(t - 2)
                if 1 <= t <= 8:
                    qk_square_sums(t - 1)
                    conv_taps((0, 7, 7, 7, 7, 7, 5, 2, 1)[t])
                if 1 <= t < 8:
                    qk_scale(t - 1)
                if t == 6:
                    s_softplus(0)
                if t == 8:
                    qk_apply(6)
                    qk_scale(7)
                    qk_apply(7)

            def ln_mean_sum():
                assert not tap_order
                dve.wait_ge(ln_sum, taps_done.now())
                nc.vector.tensor_tensor(ssq[:, 0, :], conv[:, 0, :], conv[:, 1, :], ALU.add).then_inc(vstep, 1)
                nc.vector.tensor_tensor(ssq[:, 1, :], conv[:, 2, :], conv[:, 3, :], ALU.add).then_inc(vstep, 1)
                own.tick()
                own.tick()
                dve.wait_ge(vstep, own.now())
                nc.vector.tensor_tensor(ssq[:, 0, :], ssq[:, 0, :], ssq[:, 1, :], ALU.add).then_inc(ln_col, 1)

            def ln_mean():
                dve.wait_ge(ln_sums, 1)
                nc.vector.tensor_scalar(wide[:], ps[:, 7, 0:ST].rearrange("p (a b) -> p a b", b=1).broadcast_to([P, ST, P]),
                                        1.0 / SEQ, None, ALU.mult).then_inc(ln_wide, 1)

            def ln_centre():
                dve.wait_ge(ln_spread, 1)
                for i in range(4):
                    nc.vector.tensor_tensor(conv[:, i, :], ps[:, 7, :], conv[:, i, :], ALU.subtract).then_inc(ln_xc, 1)

            def ln_square_sum():
                for i in range(4):
                    dve.wait_ge(ln_square, i + 1)
                    if i == 0:
                        continue
                    if i >= 2:
                        dve.wait_ge(ln_sq, i - 1)
                    nc.vector.tensor_tensor(ssq[:, 0, :], ssq[:, 0, :] if i >= 2 else conv_in[:, 0, :], conv_in[:, i, :],
                                            ALU.add).then_inc(ln_sq, 1)

            def ln_variance():
                dve.wait_ge(ln_sums, 2)
                nc.vector.tensor_scalar(var[:, 4:8], ps[:, 7, 0:ST], 1.0 / SEQ, EPS, ALU.mult, ALU.add).then_inc(ln_var, 1)

            def ln_rstd_wide():
                dve.wait_ge(ln_rstd, 1)
                nc.vector.tensor_scalar(wide[:], rcol[:, 7, :].rearrange("p (a b) -> p a b", b=1).broadcast_to([P, ST, P]),
                                        -1.0, None, ALU.mult).then_inc(ln_wide, 1)

            def ln_apply():
                dve.wait_ge(ln_spread, 2)
                for i in range(4):
                    nc.vector.tensor_tensor(conv[:, i, :], ps[:, 7, :], conv[:, i, :], ALU.mult).then_inc(ln_norm, 1)

            for hd in range(HEADS):
                if hd == 4:
                    ln_mean()
                if hd == 6:
                    ln_square_sum()
                if hd == 7:
                    ln_rstd_wide()
                if hd + 1 < HEADS:
                    s_softplus(hd + 1)
                conv_taps((8, 4, 4, 0, 0, 0, 0, 0)[hd])
                if hd % 2 == 0 and hd >= 2:
                    split_lo(y_lo[:, hd // 2 - 1, :], ps[:, 6, :], y_hi[:, hd // 2 - 1, :], Y_MIX2 + hd // 2 - 1)
                if hd in (3, 5):
                    final_norm(range(4 * (hd // 5), 4 * (hd // 5) + 4))
                if hd == 2:
                    ln_mean_sum()
                if hd == 4:
                    ln_centre()
                if hd == 6:
                    ln_variance()
                if hd == 7:
                    ln_apply()
            split_lo(y_lo[:, 3, :], ps[:, 6, :], y_hi[:, 3, :], Y_MIX2 + 3)
            for i in range(4):
                split_lo(y_lo[:, 4 + i, :], conv[:, i, :], y_hi[:, 4 + i, :], Y_MIX2 + 4 + i)
            dve.wait_ge(final_done, DT)
            residual(WOUT2, NORM_TWO, lambda m: col("norm2_g_2", m))
            variance(NORM_TWO, D)
            spread(NORM_TWO, 7)
            ffn(FFN2, False)
            down = ffn_plan(FFN2)[-1][3]
            for m in range(DT):
                dve.wait_ge(blocks_done, down + m + 1)
                nc.vector.tensor_tensor(h[:, m, :], ps[:, m % RING, :], h[:, m, :], ALU.add).then_inc(banks_freed, 1)

        @block.tensor
        def _(pe):
            def three(out, w, x, first, last):
                pe.matmul(out, w[0], x[0], start=first, stop=False)
                pe.matmul(out, w[0], x[1], start=False, stop=False)
                return pe.matmul(out, w[1], x[0], start=False, stop=last)

            def features(b, use, s, x, kt=8, width=SEQ, ready=None, bank=None, behind=RING, order=None,
                         begin=True, end=True):
                bank = s if bank is None else bank
                order = order or range(kt)
                if begin:
                    pe.wait_ge(w_lo_ready, b + 1)
                if begin and behind and (not isinstance(use, int) or use >= RING):
                    pe.wait_ge(banks_freed, use + 1 - behind)
                for n, k in enumerate(order):
                    if ready is not None:
                        pe.wait_ge(*ready(k))
                    c = slice(k * P, (k + 1) * P)
                    mm = three(ps[:, bank, 0:width], (w_hi[:, s, c], w_lo[:, s, c]),
                               (x[0][:, k, 0:width], x[1][:, k, 0:width]), begin and n == 0, end and n == len(order) - 1)
                if end:
                    mm.then_inc(blocks_done, 1)

            def tokens(first, use, x, nt, bank0, ready=None):
                pe.wait_ge(banks_freed, use + 1 - RING + nt - 1)
                for s in range(4):
                    pe.wait_ge(w_lo_ready, first + s + 1)
                    for kk in range(2):
                        k = 2 * s + kk
                        if ready is not None:
                            pe.wait_ge(*ready(k))
                        c = slice(kk * SEQ, (kk + 1) * SEQ)
                        for t in range(nt):
                            tok = slice(t * P, (t + 1) * P)
                            out = ps[:, bank0 + t, :]
                            pe.matmul(out, x[0][:, k, tok], w_hi[:, s, c], start=k == 0, stop=False)
                            pe.matmul(out, x[1][:, k, tok], w_hi[:, s, c], start=False, stop=False)
                            mm = pe.matmul(out, x[0][:, k, tok], w_lo[:, s, c], start=False, stop=k == DT - 1)
                    mm.then_inc(blocks_done, 1)

            def square_sums(added, sizes=ST, which=(0,)):
                pe.wait_ge(sq_added, added)
                for i, w in enumerate(which):
                    for t in range(sizes):
                        mm = pe.matmul(ps[:, AUX, i * ST + t:i * ST + t + 1], ssq[:, w, t * P:(t + 1) * P], ones[:],
                                       start=True, stop=True)
                mm.then_inc(sums_ready, 1)

            def turn_wide(n, sizes=ST):
                pe.wait_ge(wide_ready, n)
                for t in range(sizes):
                    mm = pe.transpose(ps[:, AUX + 1, t * P:(t + 1) * P], wide[:, t, :], ident[:])
                mm.then_inc(spread_ready, 1)

            def tile_ready(norm):
                return lambda k: (tile_lo, TILE0[norm] + k + 1)

            def y_ready(y0):
                return lambda k: (y_lo_ready, y0 + k + 1)

            xg, yy = (xg_hi, xg_lo), (y_hi, y_lo)

            pe.wait_ge(consts, 6)
            for m in range(8):
                features(MEMK + m, m, m % RING, (memg_hi, memg_lo), width=MEM, ready=tile_ready(NORM_MEM) if m == 0 else None)
                if m == 0:
                    square_sums(SQ0[NORM_MEM] + 8, MT)
                if m == 2:
                    turn_wide(1, MT)
            tokens(MEMV, 8, (memg_hi, memg_lo), MT, 0)
            tokens(MEMV + 4, 10, (memg_hi, memg_lo), MT, 2)
            square_sums(SQ0[NORM_MIX] + 8, which=(1,))
            tokens(INV, 12, xg, ST, 0, tile_ready(NORM_MIX))
            turn_wide(2)
            for g in range(4):
                features(INP + g, INP + g - USE_LAG, g, xg, bank=INP_BANKS[g], behind=0 if g < 2 else RING)
            for t in range(4):
                features(INU + t, INU + t - USE_LAG, t, xg)
                if t == 0:
                    for g in range(4):
                        pe.wait_ge(pooled, g + 1)
                        pe.matmul(ps[:, AUX + g, :], pool_w[:, g, :], pp[:, g, PAD:], start=True, stop=True).then_inc(pool_done, 1)
            pe.wait_ge(vn_ready, ST)
            pe.wait_ge(sgu_masked, 1)
            for hd in range(4):
                pe.wait_ge(y_lo_ready, Y_MIX + hd + 1)
                for c in range(ST):
                    mm = pe.matmul(ps[:, AUX + hd, c * P:(c + 1) * P], vtok[:, c, hd * P:(hd + 1) * P], sgu_w[:, hd, :],
                                   start=True, stop=True)
                mm.then_inc(z_done, 1)
            for ks in (range(4), range(4, 8)):
                for m in range(3):
                    features(WOUT + m, WOUT + m - USE_LAG, m % RING, yy, ready=y_ready(Y_MIX), order=ks,
                             begin=ks[0] == 0, end=ks[0] == 4)
            for m in range(3, DT):
                features(WOUT + m, WOUT + m - USE_LAG, m % RING, yy)

            def x_scores_of(hd):
                pe.wait_ge(banks_freed, WQ + 2 * hd + 2 - USE_LAG)
                if hd >= 2:
                    pe.wait_ge(x_exp, ST * (hd - 1))
                for t in range(ST):
                    for d in range(2):
                        mm = pe.matmul(ps[:, X_SCORES[hd % 2] + t // 2, (t % 2) * MEM:(t % 2 + 1) * MEM],
                                       q1[:, 2 * hd + d, t * P:(t + 1) * P], k1[:, 2 * hd + d, :], start=d == 0, stop=d == 1)
                    if t % 2:
                        mm.then_inc(x_scores, 1)

            def x_turn(hd):
                if hd == 0:
                    pe.wait_ge(banks_freed, WQ + 4 - USE_LAG)
                else:
                    pe.wait_ge(y_lo_ready, Y_X + 2 * hd)
                pe.wait_ge(x_probs, ST * (hd + 1))
                for m in range(MT):
                    for t in range(ST):
                        mm = pe.transpose(ps[:, X_VALUES + m, t * P:(t + 1) * P], probs[:, hd % 2, t, m * P:(m + 1) * P], ident[:])
                    mm.then_inc(x_turned, 1)

            def x_values(hd):
                pe.wait_ge(x_copied, 2 * (hd + 1))
                for d in range(2):
                    for m in range(MT):
                        mm = pe.matmul(ps[:, X_VALUES + d, :], v1[:, m, (2 * hd + d) * P:(2 * hd + d + 1) * P], probs_t[:, m, :],
                                       start=m == 0, stop=m == MT - 1)
                    mm.then_inc(x_out, 1)

            def output(m, ks, begin=False, end=False):
                features(WO + m, WO + m - USE_LAG, m % RING, yy, ready=y_ready(Y_X), order=ks, begin=begin, end=end,
                         behind=2 if m < 2 else RING)

            def query(m, ready=None):
                features(WQ + m, WQ + m - USE_LAG, m % RING, xg, ready=ready, bank=m if m < 4 else m % 2,
                         behind=4 if m < 6 else 2)

            query(0, tile_ready(NORM_XATTN))
            square_sums(SQ0[NORM_XATTN] + 8)
            query(1)
            turn_wide(3)
            query(2)
            query(3)
            x_scores_of(0)
            query(4)
            x_turn(0)
            x_scores_of(1)
            x_values(0)
            query(5)
            x_turn(1)
            x_scores_of(2)
            x_values(1)
            query(6)
            query(7)
            x_turn(2)
            x_scores_of(3)
            x_values(2)
            output(0, (0, 1, 2, 3), begin=True)
            x_turn(3)
            output(1, (0, 1, 2, 3), begin=True)
            x_values(3)
            output(0, (4, 5))
            output(1, (4, 5))
            output(0, (6, 7), end=True)
            output(1, (6, 7), end=True)
            for m in range(2, DT):
                features(WO + m, WO + m - USE_LAG, m % RING, yy)

            def ffn(first, norm, wides, y0):
                for first_b, n, pair0, down in ffn_plan(first):
                    start = 0
                    if pair0 == 0:
                        start = 1
                        for s in range(RING):
                            features(first_b + s, first_b + s - USE_LAG, s, xg, ready=tile_ready(norm) if s == 0 else None)
                            if s == 0:
                                square_sums(SQ0[norm] + 8)
                            if s == 1:
                                turn_wide(wides)
                    with pe.Fori(start, n // 2) as i:
                        for s in range(RING):
                            features(i * RING + (first_b + s), i * RING + (first_b + s - USE_LAG), s, xg)
                    for ks in (range(n - 2), range(n - 2, n)):
                        for s in range(3):
                            features(down + s, down + s - USE_LAG, s, yy, ready=y_ready(y0 + pair0), order=ks,
                                     begin=ks[0] == 0, end=ks[0] != 0)
                    for s in range(3, RING):
                        features(down + s, down + s - USE_LAG, s, yy, kt=n)
                    with pe.Fori(1, DT // RING) as i:
                        for s in range(RING):
                            features(i * RING + (down + s), i * RING + (down + s - USE_LAG), s, yy, kt=n)

            ffn(FFN1, NORM_FFN, 4, Y_F1)

            features(GLU, GLU - USE_LAG, 0, xg, ready=tile_ready(NORM_ONE))
            square_sums(SQ0[NORM_FINAL] + 16, which=(0, 1))
            features(GLU + 1, GLU + 1 - USE_LAG, 1, xg)
            turn_wide(5)
            for b in range(GLU + 2, V2):
                features(b, b - USE_LAG, b % RING, xg)
                if b == GLU + 3:
                    turn_wide(6)
            tokens(V2, V2 - USE_LAG, xg, ST, 0)

            def qk_sum(t):
                if t >= 1:
                    pe.wait_ge(qk_var, t)
                pe.wait_ge(qk_square, t + 1)
                for c in range(ST):
                    mm = pe.matmul(ps[:, qk_banks(t)[0], 2 * c:2 * c + 2], sq[:, t % 2, c * P:(c + 1) * P], half[:], start=True, stop=True)
                mm.then_inc(qk_sums, 1)

            def qk_turn(t):
                if t >= 1:
                    pe.wait_ge(qk_ready, t)
                if t == 6:
                    pe.wait_ge(banks_freed, QK + 8 - USE_LAG)
                pe.wait_ge(qk_wide, t + 1)
                for c in range(ST):
                    mm = pe.transpose(ps[:, qk_banks(t)[1], c * P:(c + 1) * P], wide[:, c, :], ident[:])
                mm.then_inc(qk_spread, 1)

            def s_scores(hd):
                if hd == 0:
                    pe.wait_ge(banks_freed, QK - USE_LAG)
                    pe.wait_ge(qk_ready, 2)
                    pe.wait_ge(rounded, 2)
                elif hd == 1:
                    pe.wait_ge(qk_ready, 6)
                elif hd == 6:
                    pe.wait_ge(qk_ready, 8)
                r = slice(HD * (hd % 2), HD * (hd % 2) + HD)
                for tile in (0, 1, 3, 2):
                    if hd >= 2 and tile in (0, 1):
                        pe.wait_ge(s_att, 2 * (hd - 2) + tile + 1)
                    bank, at, n = TILES[tile]
                    pe.matmul(ps[:, 3 * (hd % 2) + bank, at:at + n], k2[r, hd // 2, tile * P:(tile + 1) * P],
                                   q2[r, hd // 2, tile * P:], start=tile != 3, stop=False, skip_group_check=True)
                    mm = pe.matmul(ps[:, 3 * (hd % 2) + bank, at:at + P], ident_r[:], far_below_r[:], start=False, stop=False,
                                   skip_group_check=True)
                mm.then_inc(s_z, 1)

            def s_cumulate(hd):
                t = stick[:, hd % 3, :]
                later = later_sums[:, hd % 2, :]
                pe.wait_ge(s_sp, hd + 1)

                def add(tile, col0, n, w, src):
                    bank, at, _ = TILES[tile]
                    return pe.matmul(ps[:, 3 * (hd % 2) + bank, at + col0:at + col0 + n], w[:], src, start=False, stop=True,
                                     skip_group_check=True)

                def diagonal(tile):
                    return add(tile, 0, TILES[tile][2], neg_tri, t[:, AT[tile]:AT[tile] + TILES[tile][2]])

                diagonal(0)
                add(0, P, P, neg_ones, t[:, AT[1]:AT[1] + P])
                add(0, 2 * P, 2 * P, neg_ones, later[:, P:3 * P]).then_inc(s_cum, 1)
                for tile in range(1, ST):
                    diagonal(tile)
                add(2, P, P, neg_ones, t[:, AT[3]:AT[3] + P])
                add(1, P, P, neg_ones, t[:, AT[2]:AT[2] + P])
                add(1, 2 * P, P, neg_ones, later[:, 0:P]).then_inc(s_cum, 1)

            def s_values(hd):
                t = stick[:, hd % 3, :]
                r = slice(HD * (hd % 2), HD * (hd % 2) + HD)
                if hd == 0:
                    pe.wait_ge(qk_var, 8)
                elif hd % 2 == 0:
                    pe.wait_ge(y_lo_ready, Y_MIX2 + hd // 2)
                for tile in range(ST):
                    if tile < 2:
                        pe.wait_ge(s_att, 2 * hd + tile + 1)
                    mm = pe.matmul(ps[r, 6, tile * P:], v2[:, tile, hd * HD:(hd + 1) * HD],
                                   t[:, AT[tile]:AT[tile] + TILES[tile][2]], start=tile == 0, stop=tile == ST - 1,
                                   skip_group_check=True)
                mm.then_inc(s_out, 1)

            def ln_column_sums(n):
                if n == 0:
                    pe.wait_ge(ln_col, 1)
                else:
                    pe.wait_ge(ln_sq, 3)
                for c in range(ST):
                    mm = pe.matmul(ps[:, 7, c:c + 1], ssq[:, 0, c * P:(c + 1) * P], ones[:], start=True, stop=True)
                mm.then_inc(ln_sums, 1)

            def ln_turn(n):
                pe.wait_ge(ln_wide, n + 1)
                for c in range(ST):
                    mm = pe.transpose(ps[:, 7, c * P:(c + 1) * P], wide[:, c, :], ident[:])
                mm.then_inc(ln_spread, 1)

            for t in range(8):
                features(QK + t, QK + t - USE_LAG, t % RING, xg, bank=6 + t % 2, behind=2 if t >= 2 else 0)
                if t >= 2:
                    qk_turn(t - 2)
                if t >= 1:
                    qk_sum(t - 1)
                if t == 4:
                    s_scores(0)
            s_cumulate(0)
            s_scores(1)
            qk_sum(7)
            qk_turn(6)
            s_values(0)
            qk_turn(7)
            def output2(m, ks, begin=False, end=False):
                features(WOUT2 + m, WOUT2 + m - USE_LAG, m % RING, yy, ready=y_ready(Y_MIX2), order=ks, begin=begin, end=end)

            for hd in range(1, HEADS):
                if hd + 1 < HEADS:
                    s_scores(hd + 1)
                else:
                    pe.wait_ge(s_att, 2 * 6 + 1)
                    output2(0, (0, 1), begin=True)
                s_cumulate(hd)
                if hd >= 2:
                    s_values(hd - 1)
                if hd in (3, 6):
                    ln_column_sums(hd // 3 - 1)
                if hd in (4, 7):
                    ln_turn(hd // 3 - 1)

            output2(0, (2,))
            s_values(HEADS - 1)
            output2(1, (0, 1, 2), begin=True)
            output2(2, (0, 1, 2), begin=True)
            for m in range(3):
                output2(m, (3,))
            for m in range(3):
                output2(m, (4, 5, 6, 7), end=True)
            for m in range(3, DT):
                features(WOUT2 + m, WOUT2 + m - USE_LAG, m % RING, yy)
            ffn(FFN2, NORM_TWO, 7, Y_F2)


def _feature_blocks(w):
    k, m = w.shape
    return w.reshape(k // P, P, m // P, P).transpose(2, 1, 0, 3).reshape(m // P, P, k)


def _token_blocks(w):
    return w.reshape(4, 2, P, SEQ).transpose(0, 2, 1, 3).reshape(4, P, BLK)


def _ffn_blocks(up, down):
    ups = _feature_blocks(up)
    out, pair = [], 0
    for n in FFN_CHUNKS:
        out.append(np.stack([ups[pair:pair + n], ups[FT + pair:FT + pair + n]], 1).reshape(2 * n, P, BLK))
        part = _feature_blocks(down[pair * P:(pair + n) * P])
        out.append(np.pad(part, ((0, 0), (0, 0), (0, BLK - n * P))))
        pair += n
    return out


def kernel(**inputs):
    import concourse.bacc as _bacc
    from concourse.bass_utils import run_bass_kernel_spmd as _run

    a = {n: np.asarray(v) for n, v in inputs.items()}
    g = {n: (v if n in ("x", "mem", "final_norm_g") else v[0]) for n, v in a.items()}

    def columns(v):
        return v.reshape(-1, P).T

    parts = []
    for name in COLS:
        v = g[name]
        if name in ("q_norm_g_2", "k_norm_g_2"):
            v = np.concatenate([v, v])
        parts.append(columns(v))
    cols = np.concatenate(parts, 1)
    rows = np.concatenate([g["sgu_g"], g["sgu_b"].reshape(-1)])
    mats = np.concatenate([g["pool_w"].transpose(1, 0, 2).reshape(P, 512), g["sgu_w"].transpose(2, 0, 1).reshape(P, 512),
                           np.broadcast_to(rows, (P, 1024))], 1)
    corr = np.array([[w / min(t + 1, w) for t in range(PAD)] for w in POOL_WINDOWS], np.float32)
    corr = np.broadcast_to(corr, (P, 4, PAD))
    w_in, w_in2 = g["w_in"], g["w_in_2"]
    glu = _feature_blocks(w_in2[:, 1536:2560])
    qk = _feature_blocks(w_in2[:, 0:1024])
    stream = [
        _feature_blocks(g["wk"]), _token_blocks(g["wv"][:, 0:512]), _token_blocks(g["wv"][:, 512:1024]),
        _token_blocks(w_in[:, 1024:1536]), _feature_blocks(w_in[:, 0:512]), _feature_blocks(w_in[:, 512:1024]),
        _feature_blocks(g["w_out"]), _feature_blocks(g["wq"]), _feature_blocks(g["wo"]),
        *_ffn_blocks(g["w_up"], g["w_down"]),
        np.stack([glu[0:4], glu[4:8]], 1).reshape(8, P, BLK), _token_blocks(w_in2[:, 1024:1536]),
        np.stack([qk[0:4], qk[4:8]], 1).reshape(8, P, BLK), _feature_blocks(g["w_out_2"]),
        *_ffn_blocks(g["w_up_2"], g["w_down_2"]),
    ]
    w = np.concatenate(stream, 0)
    assert w.shape == (BLOCKS, P, BLK), w.shape
    arrays = {
        "mem_t": g["mem"][0].T.reshape(DT, P, MEM).transpose(1, 0, 2),
        "x_t": g["x"][0].T.reshape(DT, P, SEQ).transpose(1, 0, 2),
        "cols_in": cols, "mats_in": mats, "corr_in": corr, "weights": w,
    }
    arrays = {n: np.ascontiguousarray(v) for n, v in arrays.items()}
    nc = _bacc.Bacc("TRN2", target_bir_lowering=False, num_devices=1)
    args = [nc.dram_tensor(n, v.shape, F32, kind="ExternalInput").ap() for n, v in arrays.items()]
    args.append(nc.dram_tensor("out_t", (P, DT, SEQ), F32, kind="ExternalOutput").ap())
    build(nc, *args)
    r = _run(nc, [arrays], core_ids=[0])
    out = np.asarray(r.results[0]["out_t"])
    return out.transpose(1, 0, 2).reshape(D, SEQ).T.reshape(1, SEQ, D)
```
